# Optimizing a Trainium2 kernel written in Bass

```python
import math
import jax, jax.numpy as jnp
from jax import lax
import numpy as np

D_MODEL = 1024
BATCH = 1
SEQ = 256
DEPTH = 2

HEAD_DIM = 64
D_MIX = D_MODEL
GROUP_W = D_MIX // 4
N_HEADS_A = GROUP_W // HEAD_DIM
N_HEADS_B = GROUP_W // HEAD_DIM
N_GROUPS_C = 4
N_GROUPS_D = 4
MOBA_BLOCK = 256
MOBA_TOPK = 3
QBLOCK = 128
ROPE_THETA = 500000.0
ROPE_DIM = HEAD_DIM // 4
SGU_CHUNK = 128
POOL_WINDOWS = (2, 4, 8, 16)
D_FF = 2816
CONV_WIDTH = 3
DN_ALPHA = (2 * DEPTH) ** 0.25
DN_BETA = (8 * DEPTH) ** -0.25
LN_EPS = 1e-5
IN_SIZES = (GROUP_W, GROUP_W, GROUP_W, GROUP_W, GROUP_W, GROUP_W, N_HEADS_B, GROUP_W, GROUP_W, GROUP_W)
IN_SPLITS = tuple(int(s) for s in np.cumsum(IN_SIZES)[:-1])
N_IN = int(sum(IN_SIZES))


def layer_norm(x, g, b):
    xf = x.astype(jnp.float32)
    mu = jnp.mean(xf, axis=-1, keepdims=True)
    var = jnp.mean(jnp.square(xf - mu), axis=-1, keepdims=True)
    return ((xf - mu) * lax.rsqrt(var + LN_EPS) * g.astype(jnp.float32) + b.astype(jnp.float32)).astype(x.dtype)

def to_heads(t, n_heads):
    b, s, _ = t.shape
    return t.reshape(b, s, n_heads, -1).transpose(0, 2, 1, 3)

def from_heads(t):
    b, h, s, d = t.shape
    return t.transpose(0, 2, 1, 3).reshape(b, s, h * d)

def rotary_tables(seq_len):
    pos = jnp.arange(seq_len, dtype=jnp.float32)
    inv_freq = ROPE_THETA ** (-jnp.arange(0, ROPE_DIM, 2, dtype=jnp.float32) / ROPE_DIM)
    ang = pos[:, None] * inv_freq[None, :]
    return jnp.cos(ang), jnp.sin(ang)

def partial_rotary(x, cos, sin):
    half = ROPE_DIM // 2
    cos = cos.astype(x.dtype)
    sin = sin.astype(x.dtype)
    x1 = x[..., :half]
    x2 = x[..., half:ROPE_DIM]
    return jnp.concatenate([x1 * cos - x2 * sin, x1 * sin + x2 * cos, x[..., ROPE_DIM:]], axis=-1)

def moba_attention(q, k, v):
    bsz, h, s, hd = q.shape
    s_pad = -(-s // MOBA_BLOCK) * MOBA_BLOCK
    pad = ((0, 0), (0, 0), (0, s_pad - s), (0, 0))
    q, k, v = jnp.pad(q, pad), jnp.pad(k, pad), jnp.pad(v, pad)
    nb = s_pad // MOBA_BLOCK
    n_sel = min(MOBA_TOPK, nb)
    scale = hd ** -0.5
    kb = k.reshape(bsz, h, nb, MOBA_BLOCK, hd)
    vb = v.reshape(bsz, h, nb, MOBA_BLOCK, hd)
    kbar = jnp.mean(kb.astype(jnp.float32), axis=3)
    gate = jnp.einsum('bhsd,bhnd->bhsn', q.astype(jnp.float32), kbar)
    q_blk = jnp.arange(s_pad) // MOBA_BLOCK
    fully_past = jnp.arange(nb)[None, :] < q_blk[:, None]
    gate = jnp.where(fully_past, gate, -jnp.inf)
    _, sel = lax.top_k(gate, n_sel)
    bi = jnp.arange(bsz)[:, None, None, None]
    hi = jnp.arange(h)[None, :, None, None]

    def one_chunk(n):
        start = n * QBLOCK
        blk = start // MOBA_BLOCK
        qc = lax.dynamic_slice_in_dim(q, start, QBLOCK, axis=2)
        selc = lax.dynamic_slice_in_dim(sel, start, QBLOCK, axis=2)
        valid = selc < blk
        ks = kb[bi, hi, selc]
        vs = vb[bi, hi, selc]
        s_sel = jnp.einsum('bhqd,bhqnjd->bhqnj', qc, ks).astype(jnp.float32) * scale
        s_sel = jnp.where(valid[..., None], s_sel, -jnp.inf).reshape(bsz, h, QBLOCK, n_sel * MOBA_BLOCK)
        k_own = lax.dynamic_slice_in_dim(k, blk * MOBA_BLOCK, MOBA_BLOCK, axis=2)
        v_own = lax.dynamic_slice_in_dim(v, blk * MOBA_BLOCK, MOBA_BLOCK, axis=2)
        s_own = jnp.einsum('bhqd,bhjd->bhqj', qc, k_own).astype(jnp.float32) * scale
        qpos = start + jnp.arange(QBLOCK)
        kpos = blk * MOBA_BLOCK + jnp.arange(MOBA_BLOCK)
        s_own = jnp.where(kpos[None, :] <= qpos[:, None], s_own, -jnp.inf)
        p = jax.nn.softmax(jnp.concatenate([s_sel, s_own], axis=-1), axis=-1)
        p_sel = p[..., :n_sel * MOBA_BLOCK].reshape(bsz, h, QBLOCK, n_sel, MOBA_BLOCK).astype(v.dtype)
        p_own = p[..., n_sel * MOBA_BLOCK:].astype(v.dtype)
        return (jnp.einsum('bhqnj,bhqnjd->bhqd', p_sel, vs)
                + jnp.einsum('bhqj,bhjd->bhqd', p_own, v_own))

    outs = lax.map(one_chunk, jnp.arange(s_pad // QBLOCK))
    out = outs.transpose(1, 2, 0, 3, 4).reshape(bsz, h, s_pad, hd)
    return out[:, :, :s]

def forgetting_attention(q, k, v, log_f):
    bsz, h, s, hd = q.shape
    scale = hd ** -0.5
    c = jnp.cumsum(log_f, axis=-1)
    kpos = jnp.arange(s)

    def one_block(n):
        start = n * QBLOCK
        qc = lax.dynamic_slice_in_dim(q, start, QBLOCK, axis=2)
        cq = lax.dynamic_slice_in_dim(c, start, QBLOCK, axis=2)
        logits = (jnp.einsum('bhqd,bhkd->bhqk', qc, k).astype(jnp.float32) * scale
                  + cq[..., :, None] - c[..., None, :])
        qpos = start + jnp.arange(QBLOCK)
        logits = jnp.where(kpos[None, :] <= qpos[:, None], logits, -jnp.inf)
        p = jax.nn.softmax(logits, axis=-1).astype(v.dtype)
        return jnp.einsum('bhqk,bhkd->bhqd', p, v)

    outs = lax.map(one_block, jnp.arange(s // QBLOCK))
    return outs.transpose(1, 2, 0, 3, 4).reshape(bsz, h, s, hd)

def causal_spatial_gating(u, v, ln_g, ln_b, w_s, b_s):
    bsz, s, width = v.shape
    g = N_GROUPS_C
    c = width // g
    vn = layer_norm(v.reshape(bsz, s, g, c), ln_g.reshape(g, c), ln_b.reshape(g, c))
    vc = vn.reshape(bsz, s // SGU_CHUNK, SGU_CHUNK, g, c)
    causal = jnp.tril(jnp.ones((SGU_CHUNK, SGU_CHUNK), dtype=bool))
    w = jnp.where(causal[None], w_s, jnp.zeros_like(w_s))
    mixed = jnp.einsum('gts,bnsgc->bntgc', w, vc) + b_s.T[None, None, :, :, None]
    return u * mixed.reshape(bsz, s, width)

def multiscale_pool(p, w_g, scale):
    bsz, s, width = p.shape
    g = len(POOL_WINDOWS)
    c = width // g
    pg = p.reshape(bsz, s, g, c).astype(jnp.float32)
    cs = jnp.concatenate([jnp.zeros((bsz, 1, g, c), jnp.float32), jnp.cumsum(pg, axis=1)], axis=1)
    t = jnp.arange(s)
    outs = []
    for gi, win in enumerate(POOL_WINDOWS):
        cs_g = cs[:, :, gi]
        lo = jnp.maximum(t + 1 - win, 0)
        window_sum = cs_g[:, 1:] - cs_g[:, lo]
        count = jnp.minimum(t + 1, win).astype(jnp.float32)
        outs.append(window_sum / count[None, :, None] - pg[:, :, gi])
    pooled = jnp.stack(outs, axis=2).astype(p.dtype)
    mixed = jnp.einsum('bsgc,gcd->bsgd', pooled, w_g)
    return mixed.reshape(bsz, s, width) * scale

def hybrid_mixer(x, w_in, b_forget, sgu_ln_g, sgu_ln_b, sgu_w, sgu_b, pool_w, pool_scale, w_o, cos, sin):
    z = x @ w_in
    aq, ak, av, bq, bk, bv, bf, cu, cv, dp = jnp.split(z, IN_SPLITS, axis=-1)
    ya = moba_attention(partial_rotary(to_heads(aq, N_HEADS_A), cos, sin),
                        partial_rotary(to_heads(ak, N_HEADS_A), cos, sin),
                        to_heads(av, N_HEADS_A))
    log_f = jax.nn.log_sigmoid((bf + b_forget).astype(jnp.float32)).transpose(0, 2, 1)
    yb = forgetting_attention(to_heads(bq, N_HEADS_B), to_heads(bk, N_HEADS_B),
                              to_heads(bv, N_HEADS_B), log_f)
    yc = causal_spatial_gating(jax.nn.gelu(cu, approximate=False), jax.nn.gelu(cv, approximate=False),
                               sgu_ln_g, sgu_ln_b, sgu_w, sgu_b)
    yd = multiscale_pool(dp, pool_w, pool_scale)
    y = jnp.concatenate([from_heads(ya), from_heads(yb), yc, yd], axis=-1)
    return y @ w_o

def conv_gated_ffn(x, w_up, conv_w, conv_b, w_down):
    h = x @ w_up
    h = lax.conv_general_dilated(h, conv_w[:, None, :], window_strides=(1,),
                                 padding=[(CONV_WIDTH - 1, 0)],
                                 dimension_numbers=('NWC', 'WIO', 'NWC'),
                                 feature_group_count=h.shape[-1]) + conv_b
    gate, val = jnp.split(h, 2, axis=-1)
    return (jax.nn.silu(gate) * val) @ w_down

def first_inputs(seed: int = 0) -> dict:
    key = jax.random.key(seed)
    ks = jax.random.split(key, 20)
    L = DEPTH
    nrm = jax.random.normal
    f32 = jnp.float32
    ch = GROUP_W // N_GROUPS_D
    return {
        'x': nrm(ks[0], (BATCH, SEQ, D_MODEL), f32),
        'w_in': nrm(ks[1], (L, D_MODEL, N_IN), f32) * D_MODEL ** -0.5,
        'b_forget': 3.0 + 0.1 * nrm(ks[2], (L, N_HEADS_B), f32),
        'sgu_ln_g': 1.0 + 0.05 * nrm(ks[3], (L, GROUP_W), f32),
        'sgu_ln_b': 0.02 * nrm(ks[4], (L, GROUP_W), f32),
        'sgu_w': nrm(ks[5], (L, N_GROUPS_C, SGU_CHUNK, SGU_CHUNK), f32) * SGU_CHUNK ** -0.5,
        'sgu_b': 1.0 + 0.1 * nrm(ks[6], (L, N_GROUPS_C, SGU_CHUNK), f32),
        'pool_w': nrm(ks[7], (L, N_GROUPS_D, ch, ch), f32) * ch ** -0.5,
        'pool_scale': 1.0 + 0.1 * nrm(ks[8], (L, GROUP_W), f32),
        'w_o': nrm(ks[9], (L, D_MIX, D_MODEL), f32) * D_MIX ** -0.5 * DN_BETA,
        'ln1_g': 1.0 + 0.05 * nrm(ks[10], (L, D_MODEL), f32),
        'ln1_b': 0.02 * nrm(ks[11], (L, D_MODEL), f32),
        'w_up': nrm(ks[12], (L, D_MODEL, 2 * D_FF), f32) * D_MODEL ** -0.5,
        'conv_w': nrm(ks[13], (L, CONV_WIDTH, 2 * D_FF), f32) * CONV_WIDTH ** -0.5,
        'conv_b': 0.02 * nrm(ks[14], (L, 2 * D_FF), f32),
        'w_down': nrm(ks[15], (L, D_FF, D_MODEL), f32) * D_FF ** -0.5 * DN_BETA,
        'ln2_g': 1.0 + 0.05 * nrm(ks[16], (L, D_MODEL), f32),
        'ln2_b': 0.02 * nrm(ks[17], (L, D_MODEL), f32),
    }

def first_block(x, w_in, b_forget, sgu_ln_g, sgu_ln_b, sgu_w, sgu_b, pool_w, pool_scale, w_o,
              ln1_g, ln1_b, w_up, conv_w, conv_b, w_down, ln2_g, ln2_b):
    cos, sin = rotary_tables(x.shape[1])
    for l in range(DEPTH):
        y = hybrid_mixer(x, w_in[l], b_forget[l], sgu_ln_g[l], sgu_ln_b[l], sgu_w[l], sgu_b[l],
                         pool_w[l], pool_scale[l], w_o[l], cos, sin)
        x = layer_norm(DN_ALPHA * x + y, ln1_g[l], ln1_b[l])
        y = conv_gated_ffn(x, w_up[l], conv_w[l], conv_b[l], w_down[l])
        x = layer_norm(DN_ALPHA * x + y, ln2_g[l], ln2_b[l])
    return x


CHUNK = 64
DN_HEADS = 8
DN_DK = 128
DN_DV = 128
DN_WIDTH = DN_HEADS * DN_DK
CONV_K = 4
SA_HEADS = 8
SA_HD = 128
SA_WIDTH = SA_HEADS * SA_HD
IDX_HEADS = 8
IDX_HD = 64
TOPK_MAX = 256
Q_BLOCK = 128
XA_HEADS = 4
XA_HD = 256
XA_WIDTH = XA_HEADS * XA_HD
N_MEM = 256
ROPE_DIV = 4
D_FF_2 = ((8 * D_MODEL // 3 + 255) // 256) * 256
N_BRANCH = 3
NORM_EPS = 1e-6

IN_SIZES_2 = (DN_WIDTH, DN_WIDTH, DN_HEADS * DN_DV, DN_HEADS * DN_DV, DN_HEADS, DN_HEADS,
            SA_WIDTH, SA_WIDTH, SA_WIDTH, IDX_HEADS * IDX_HD, IDX_HD, IDX_HEADS,
            XA_WIDTH, N_BRANCH * D_MODEL)
N_IN_2 = sum(IN_SIZES_2)


def rmsnorm(x, g):
    xf = x.astype(jnp.float32)
    y = xf * lax.rsqrt(jnp.mean(xf * xf, axis=-1, keepdims=True) + NORM_EPS)
    return (y * g.astype(jnp.float32)).astype(x.dtype)

def l2norm(x):
    return x * lax.rsqrt(jnp.sum(x * x, axis=-1, keepdims=True) + NORM_EPS)

def rope_partial(x, positions):
    rd = x.shape[-1] // ROPE_DIV
    half = rd // 2
    inv_freq = ROPE_THETA ** (-(jnp.arange(half, dtype=jnp.float32) * 2.0 / rd))
    ang = positions.astype(jnp.float32)[..., None] * inv_freq
    cos = jnp.cos(ang)[:, :, None, :]
    sin = jnp.sin(ang)[:, :, None, :]
    xr = x[..., :rd].astype(jnp.float32)
    x1, x2 = xr[..., :half], xr[..., half:]
    rot = jnp.concatenate([x1 * cos - x2 * sin, x2 * cos + x1 * sin], axis=-1)
    return jnp.concatenate([rot.astype(x.dtype), x[..., rd:]], axis=-1)

def causal_conv(x, w):
    c = x.shape[-1]
    return lax.conv_general_dilated(x, w[:, None, :], window_strides=(1,),
                                    padding=[(CONV_K - 1, 0)],
                                    dimension_numbers=('NWC', 'WIO', 'NWC'),
                                    feature_group_count=c)

def gated_delta_rule(q, k, v, beta, g):
    b, s, h, dk = q.shape
    dv = v.shape[-1]
    n = s // CHUNK

    def chunks(t):
        return jnp.moveaxis(t.reshape((b, n, CHUNK) + t.shape[2:]), 2, 3)

    qc, kc, vc, bc, gc = (chunks(t) for t in (q, k, v, beta, g))
    gc = jnp.cumsum(gc, axis=-1)
    pos = jnp.arange(CHUNK)
    incl = pos[:, None] >= pos[None, :]
    strict = pos[:, None] > pos[None, :]
    diff = gc[..., :, None] - gc[..., None, :]
    decay = jnp.where(incl, jnp.exp(jnp.where(incl, diff, 0.0)), 0.0)
    kb = kc * bc[..., None]
    m = jnp.where(strict, jnp.einsum('bnhid,bnhjd->bnhij', kb, kc) * decay, 0.0)
    rhs = jnp.concatenate([vc * bc[..., None], kb * jnp.exp(gc)[..., None]], axis=-1)
    sol = lax.linalg.triangular_solve(m, rhs, left_side=True, lower=True, unit_diagonal=True)
    u, w = sol[..., :dv], sol[..., dv:]
    a_qk = jnp.einsum('bnhid,bnhjd->bnhij', qc, kc) * decay
    q_dec = qc * jnp.exp(gc)[..., None]
    g_last = gc[..., -1]
    k_dec = kc * jnp.exp(g_last[..., None] - gc)[..., None]
    c_dec = jnp.exp(g_last)

    def step(state, xs):
        qd, kd, a, uu, ww, cd = xs
        v_new = uu - jnp.einsum('bhck,bhkv->bhcv', ww, state)
        o = jnp.einsum('bhck,bhkv->bhcv', qd, state) + jnp.einsum('bhij,bhjv->bhiv', a, v_new)
        state = state * cd[..., None, None] + jnp.einsum('bhck,bhcv->bhkv', kd, v_new)
        return state, o

    xs = tuple(jnp.moveaxis(t, 1, 0) for t in (q_dec, k_dec, a_qk, u, w, c_dec))
    s0 = jnp.zeros((b, h, dk, dv), jnp.float32)
    _, o = lax.scan(step, s0, xs)
    return jnp.swapaxes(jnp.moveaxis(o, 0, 1), 2, 3).reshape(b, s, h, dv)

def deltanet_branch(q_in, k_in, v_in, z_in, b_in, a_in, conv_w, a_log, dt_bias, dn_norm):
    b, s, _ = q_in.shape
    f32 = jnp.float32
    qkv = jax.nn.silu(causal_conv(jnp.concatenate([q_in, k_in, v_in], axis=-1), conv_w))
    q, k, v = jnp.split(qkv, [DN_WIDTH, 2 * DN_WIDTH], axis=-1)
    q = l2norm(q.reshape(b, s, DN_HEADS, DN_DK).astype(f32)) * DN_DK ** -0.5
    k = l2norm(k.reshape(b, s, DN_HEADS, DN_DK).astype(f32))
    v = v.reshape(b, s, DN_HEADS, DN_DV).astype(f32)
    beta = jax.nn.sigmoid(b_in.astype(f32))
    g = -jnp.exp(a_log.astype(f32)) * jax.nn.softplus(a_in.astype(f32) + dt_bias.astype(f32))
    o = gated_delta_rule(q, k, v, beta, g)
    z = z_in.reshape(b, s, DN_HEADS, DN_DV).astype(f32)
    o = rmsnorm(o, dn_norm) * jax.nn.silu(z)
    return o.reshape(b, s, DN_WIDTH).astype(q_in.dtype)

def dsa_branch(q_in, k_in, v_in, iq_in, ik_in, iw_in, positions):
    b, s, _ = q_in.shape
    f32 = jnp.float32
    q = rope_partial(q_in.reshape(b, s, SA_HEADS, SA_HD), positions)
    k = rope_partial(k_in.reshape(b, s, SA_HEADS, SA_HD), positions)
    v = v_in.reshape(b, s, SA_HEADS, SA_HD)
    iq = rope_partial(iq_in.reshape(b, s, IDX_HEADS, IDX_HD), positions).astype(f32)
    ik = rope_partial(ik_in.reshape(b, s, 1, IDX_HD), positions)[:, :, 0].astype(f32)
    iw = iw_in.astype(f32) * (IDX_HEADS ** -0.5 * IDX_HD ** -0.5)
    k_sel = min(TOPK_MAX, s // 4)
    nb = s // Q_BLOCK
    key_chunk = jnp.arange(s) // CHUNK

    def blocks(t):
        return jnp.moveaxis(t.reshape((b, nb, Q_BLOCK) + t.shape[2:]), 1, 0)

    def attend(xs):
        qb, iqb, iwb, blk = xs
        q_chunk = (blk * Q_BLOCK + jnp.arange(Q_BLOCK)) // CHUNK
        score = jax.nn.relu(jnp.einsum('bthd,bsd->bths', iqb, ik))
        score = jnp.einsum('bths,bth->bts', score, iwb)
        admissible = key_chunk[None, :] <= q_chunk[:, None]
        score = jnp.where(admissible[None], score, -jnp.inf)
        _, sel = lax.top_k(score, k_sel)
        valid = (sel // CHUNK) <= q_chunk[None, :, None]
        kg = jax.vmap(lambda a, i: a[i])(k, sel)
        vg = jax.vmap(lambda a, i: a[i])(v, sel)
        logits = jnp.einsum('bthd,btkhd->bthk', qb, kg).astype(f32) * SA_HD ** -0.5
        logits = jnp.where(valid[:, :, None, :], logits, -jnp.inf)
        p = jax.nn.softmax(logits, axis=-1).astype(vg.dtype)
        return jnp.einsum('bthk,btkhd->bthd', p, vg)

    o = lax.map(attend, (blocks(q), blocks(iq), blocks(iw), jnp.arange(nb, dtype=jnp.int32)))
    return jnp.moveaxis(o, 0, 1).reshape(b, s, SA_WIDTH)

def memory_branch(q_in, mem_n, w_mem_kv):
    b, s, _ = q_in.shape
    m = mem_n.shape[1]
    mk, mv = jnp.split(mem_n @ w_mem_kv, 2, axis=-1)
    q = q_in.reshape(b, s, XA_HEADS, XA_HD)
    mk = mk.reshape(b, m, XA_HEADS, XA_HD)
    mv = mv.reshape(b, m, XA_HEADS, XA_HD)
    logits = jnp.einsum('bshd,bmhd->bhsm', q, mk).astype(jnp.float32) * XA_HD ** -0.5
    p = jax.nn.softmax(logits, axis=-1).astype(mv.dtype)
    return jnp.einsum('bhsm,bmhd->bshd', p, mv).reshape(b, s, XA_WIDTH)

def second_inputs(seed: int = 0) -> dict:
    key = jax.random.key(seed)
    ks = jax.random.split(key, 20)
    f32 = jnp.float32

    def nrm(k, shape, fan_in):
        return jax.random.normal(k, shape, f32) * fan_in ** -0.5

    def gain(k, shape):
        return 1.0 + 0.02 * jax.random.normal(k, shape, f32)

    x = jax.random.normal(ks[0], (BATCH, SEQ, D_MODEL), f32)
    mem = jax.random.normal(ks[1], (BATCH, N_MEM, D_MODEL), f32)
    offset = jax.random.randint(ks[2], (BATCH, 1), 0, 64, dtype=jnp.int32) * CHUNK
    positions = (offset + jnp.arange(SEQ, dtype=jnp.int32)[None, :]).astype(jnp.int32)
    dt = jnp.exp(jax.random.uniform(ks[3], (DEPTH, DN_HEADS), f32, math.log(1e-3), math.log(1e-1)))
    return {
        'x': x,
        'mem': mem,
        'positions': positions,
        'norm_mix': gain(ks[4], (DEPTH, D_MODEL)),
        'norm_mem': gain(ks[5], (DEPTH, D_MODEL)),
        'w_in': nrm(ks[6], (DEPTH, D_MODEL, N_IN_2), D_MODEL),
        'b_gate': 0.1 * jax.random.normal(ks[7], (DEPTH, N_BRANCH, D_MODEL), f32),
        'conv_w': nrm(ks[8], (DEPTH, CONV_K, 3 * DN_WIDTH), CONV_K),
        'a_log': jnp.log(jax.random.uniform(ks[9], (DEPTH, DN_HEADS), f32, 1.0, 16.0)),
        'dt_bias': jnp.log(jnp.expm1(dt)),
        'dn_norm': gain(ks[10], (DEPTH, DN_DV)),
        'w_mem_kv': nrm(ks[11], (DEPTH, D_MODEL, 2 * XA_WIDTH), D_MODEL),
        'w_branch': nrm(ks[12], (DEPTH, N_BRANCH, DN_WIDTH, D_MODEL), DN_WIDTH),
        'w_out': nrm(ks[13], (DEPTH, D_MODEL, D_MODEL), D_MODEL),
        'norm_ffn': gain(ks[14], (DEPTH, D_MODEL)),
        'w_ffn_in': nrm(ks[15], (DEPTH, D_MODEL, 2 * D_FF_2), D_MODEL),
        'w_ffn_out': nrm(ks[16], (DEPTH, D_FF_2, D_MODEL), D_FF_2),
        'norm_final': gain(ks[17], (D_MODEL,)),
    }

def second_block(x, mem, positions, norm_mix, norm_mem, w_in, b_gate, conv_w, a_log, dt_bias,
              dn_norm, w_mem_kv, w_branch, w_out, norm_ffn, w_ffn_in, w_ffn_out, norm_final):
    b, s, d = x.shape
    split_pts = []
    acc = 0
    for size in IN_SIZES_2[:-1]:
        acc += size
        split_pts.append(acc)
    for l in range(DEPTH):
        h = rmsnorm(x, norm_mix[l])
        (dq, dk, dv, dz, db, da, sq, sk, sv, iq, ik, iw, xq, gl) = jnp.split(h @ w_in[l], split_pts, axis=-1)
        o_dn = deltanet_branch(dq, dk, dv, dz, db, da, conv_w[l], a_log[l], dt_bias[l], dn_norm[l])
        o_sa = dsa_branch(sq, sk, sv, iq, ik, iw, positions)
        o_xa = memory_branch(xq, rmsnorm(mem, norm_mem[l]), w_mem_kv[l])
        gates = jax.nn.sigmoid((gl.reshape(b, s, N_BRANCH, d) + b_gate[l]).astype(jnp.float32)).astype(x.dtype)
        merged = (gates[:, :, 0] * (o_dn @ w_branch[l, 0])
                  + gates[:, :, 1] * (o_sa @ w_branch[l, 1])
                  + gates[:, :, 2] * (o_xa @ w_branch[l, 2]))
        x = x + merged @ w_out[l]
        h = rmsnorm(x, norm_ffn[l])
        gt, up = jnp.split(h @ w_ffn_in[l], 2, axis=-1)
        x = x + (jax.nn.silu(gt) * up) @ w_ffn_out[l]
    return rmsnorm(x, norm_final)


def setup_inputs(seed=0):
    out = dict(first_inputs(seed))
    for name, value in second_inputs(seed + 1).items():
        if name != "x":
            out[name + "_2"] = value
    return out


def reference(
    x, w_in, b_forget, sgu_ln_g, sgu_ln_b, sgu_w, sgu_b, pool_w, pool_scale, w_o, ln1_g, ln1_b,
    w_up, conv_w, conv_b, w_down, ln2_g, ln2_b, mem_2, positions_2, norm_mix_2, norm_mem_2,
    w_in_2, b_gate_2, conv_w_2, a_log_2, dt_bias_2, dn_norm_2, w_mem_kv_2, w_branch_2, w_out_2,
    norm_ffn_2, w_ffn_in_2, w_ffn_out_2, norm_final_2,
):
    x = first_block(
        x, w_in, b_forget, sgu_ln_g, sgu_ln_b, sgu_w, sgu_b, pool_w, pool_scale, w_o, ln1_g,
        ln1_b, w_up, conv_w, conv_b, w_down, ln2_g, ln2_b,
    )
    return second_block(
        x, mem_2, positions_2, norm_mix_2, norm_mem_2, w_in_2, b_gate_2, conv_w_2, a_log_2,
        dt_bias_2, dn_norm_2, w_mem_kv_2, w_branch_2, w_out_2, norm_ffn_2, w_ffn_in_2,
        w_ffn_out_2, norm_final_2,
    )


_drawn_inputs = setup_inputs


def setup_inputs(seed=0):
    import zlib

    import numpy as np

    out = dict(_drawn_inputs(seed))
    spreads = {}
    factors = {'b_forget': 33.104,
     'sgu_ln_g': 3.576,
     'sgu_ln_b': 5.495,
     'norm_mem_2': 8.0,
     'dn_norm_2': 14.483,
     'norm_final_2': 8.074,
     'norm_ffn_2': 5.857}
    for name, (base, spread) in spreads.items():
        noise = np.random.default_rng([zlib.crc32(name.encode()), seed]).standard_normal(out[name].shape)
        drawn = base * np.exp(spread * noise) if base else spread * noise
        out[name] = __import__('jax').numpy.asarray(drawn.astype(out[name].dtype))
    for name, factor in factors.items():
        out[name] = (out[name] * factor).astype(out[name].dtype)
    return out
```

```python
from contextlib import ExitStack, contextmanager

import numpy as np

import concourse.bass as bass
from concourse import mybir

F32 = mybir.dt.float32
I32 = mybir.dt.int32
ALU = mybir.AluOpType
ACT = mybir.ActivationFunctionType
AX_X = mybir.AxisListType.X

P = 128
T = 256
TT = T // P
D = 1024
KD = D // P
DEPTH = 2
FF = 2816
KF = FF // P
HALF = 512
NEG = -1.0e30
TAKEN = -3.0e38
ALPHA = (2 * DEPTH) ** 0.25
LN_EPS = 1e-5
NORM_EPS = 1e-6
CH = 64
NCH = T // CH
TOPK = T // 4
WINDOWS = (2, 4, 8, 16)
THETA = 500000.0
IDX_SCALE = 8 ** -0.5 * 64 ** -0.5
SLOTS = 3
SLOT_W = 8 * 516


def _cols(name, total, width, k=KD):
    return [(f"{name}{i}", k, min(width, total - i * width)) for i in range(-(-total // width))]


def _rows(name, tiles, per):
    return [(f"{name}{i}", min(per, tiles - i * per), D) for i in range(-(-tiles // per))]


CHUNKS_1 = ([("in0", KD, 512), ("in1", KD, 512), ("in2", KD, 512), ("in3", KD, 516), ("in4", KD, 256)]
            + _cols("o", D, 512) + _cols("up", 2 * FF, 512) + _rows("down", KF, 4))
CHUNKS_2 = (_cols("dn", 4 * D, 512) + _cols("sa", 3 * D, 512) + [("iq", KD, 512)] + _cols("kv", 2 * D, 512)
            + _cols("xq", D, 512)
            + [(f"{b}{i}{c}", KD, 512) for c in range(2) for i in range(3) for b in ("gl", "wb")]
            + _cols("out", D, 512) + _cols("fin", 2 * FF, 512) + _rows("fout", KF, 4))


def offsets(chunks):
    at, out = 0, {}
    for n, (name, k, c) in enumerate(chunks):
        out[name] = (n, at, k, c)
        at += k * c
    return out, at


def columns(spec):
    at, out = 0, {}
    for name, n in spec:
        out[name] = slice(at, at + n)
        at += n
    return out, at


PC1, NPC1 = columns([("ln1_g", 8), ("ln1_b", 8), ("ln2_g", 8), ("ln2_b", 8), ("conv_w", 3 * 44), ("conv_b", 44),
                     ("pool_scale", 2), ("b_forget", 1), ("sgu_wT", 4 * 128), ("sgu_b", 4 * 128), ("pool_w", 2 * 64)])
PC2, NPC2 = columns([("norm_mix", 8), ("norm_mem", 8), ("norm_ffn", 8), ("b_gate", 24), ("conv_w", 4 * 24),
                     ("dn_norm", 1), ("a_log", 1), ("dt_bias", 1), ("w_small", 8 * 152)])
CC, NCC = columns([("ident", 128), ("ones", 128), ("causal", 2 * 256), ("chunk_causal", 2 * 256), ("band", 2 * 4 * 256),
                   ("cos", 256), ("sin", 256), ("perm64", 128), ("perm128", 128), ("freq", 2), ("levels", 6 * 128),
                   ("upper", 128), ("strict", 128), ("select", 8 * 128)])


def constants():
    c = np.zeros((P, NCC), np.float32)
    p = np.arange(P)
    t = np.arange(T)

    def put(name, a):
        c[:a.shape[0], CC[name]] = a.reshape(a.shape[0], -1)

    put("ident", np.eye(P))
    put("ones", np.ones((P, P)))
    q = p[:, None] + P * np.arange(TT)[None, :]
    put("causal", np.where(t[None, None, :] <= q[:, :, None], 0.0, NEG))
    put("chunk_causal", np.where(t[None, None, :] // CH <= q[:, :, None] // CH, 0.0, NEG))
    s = q[:, :, None, None]
    win = np.array(WINDOWS)[None, None, :, None]
    at = t[None, None, None, :]
    inside = (s <= at) & (s > at - win)
    put("band", inside / np.minimum(at + 1, win) - (s == at))
    half = 8
    inv = (np.float64(THETA) ** (-np.arange(0, 16, 2) / 16)).astype(np.float32)
    ang = t[None, :].astype(np.float32) * inv[p % half][:, None]
    roped = ((p % 64) < 16)[:, None]
    put("cos", np.where(roped, np.cos(ang), 1.0))
    put("sin", np.where(roped, np.sin(ang), 0.0))
    for name, dim, h in (("perm64", 64, 8), ("perm128", 128, 16)):
        m = np.zeros((P, P))
        for d in range(P):
            if d % dim < h:
                m[d + h, d] = -1.0
            elif d % dim < 2 * h:
                m[d - h, d] = 1.0
        put(name, m)
    f = np.zeros((P, 2))
    inv128 = (np.float64(THETA) ** (-np.arange(16) * 2.0 / 32)).astype(np.float32)
    inv64 = (np.float64(THETA) ** (-np.arange(8) * 2.0 / 16)).astype(np.float32)
    f[:32, 0] = inv128[p[:32] % 16]
    f[:, 1] = np.where(p % 64 < 16, inv64[p % 8], 0.0)
    put("freq", f)
    i, j = p[:, None], p[None, :]
    lev = [((i // (2 * b) == j // (2 * b)) & (i // b > j // b)) for b in (1, 2, 4, 8, 16, 32)]
    put("levels", np.stack(lev, 1).astype(np.float64))
    same = i // CH == j // CH
    put("upper", (same & (j >= i)).astype(np.float64))
    put("strict", (same & (j > i)).astype(np.float64))
    sel = np.zeros((8, 8, P))
    sel[np.arange(8), np.arange(8)] = 1.0
    put("select", sel)
    return c


PHASES = []


@contextmanager
def phase(nc, names, tensors=(), banks=()):
    with ExitStack() as ctx:
        at = len(PHASES)
        PHASES.append(names)
        handles = [ctx.enter_context(nc.semaphore(n)) for n in names.split()]
        s = {n: h for n, h in zip(names.split(), handles)}
        b = {}
        for name, shape in tensors:
            b[name] = ctx.enter_context(nc.sbuf_tensor(f"{name}_{at}", shape, F32))
        for name, width in banks:
            b[name] = ctx.enter_context(nc.psum_tensor(f"{name}_{at}", [P, width], F32))
        with nc.Block() as block:
            yield block, s, b
        for h in handles:
            nc.gpsimd.sem_clear(h)
        nc.all_engine_barrier()


class Chain:

    def __init__(self, eng, sem):
        self.eng, self.sem, self.n = eng, sem, 0

    def step(self, ins):
        self.n += 1
        ins.then_inc(self.sem, 1)
        self.eng.wait_ge(self.sem, self.n)


class Ring:

    def __init__(self, nc, ctx, name, chunks, dram):
        self.buf = ctx.enter_context(nc.sbuf_tensor(f"{name}_ring", [P, SLOTS, SLOT_W], F32))
        self.loaded = [ctx.enter_context(nc.semaphore(f"{name}_loaded{i}")) for i in range(SLOTS)]
        self.product = ctx.enter_context(nc.semaphore(f"{name}_product"))
        self.where, self.width = offsets(chunks)
        self.names = [c[0] for c in chunks]
        self.dram = dram
        self.start()

    def start(self):
        self.sent, self.units, self.ended, self.last = 0, 0, {}, -1

    def plan(self, chunks_of_units):
        base = self.units
        for name in chunks_of_units:
            self.units += 1
            if name in self.where:
                self.ended[name] = self.units
                self.last = self.where[name][0]
        return base

    def view(self, name):
        n, _, k, c = self.where[name]
        return self.buf[:, n % SLOTS, 0:k * c].rearrange("p (k c) -> p k c", k=k)

    def send(self, sp, layer):
        upto = min(self.last + 1 + SLOTS, len(self.names))
        for n in range(self.sent, upto):
            _, at, k, c = self.where[self.names[n]]
            if n >= SLOTS:
                sp.wait_ge(self.product, self.ended[self.names[n - SLOTS]])
            sp.dma_start(self.buf[:, n % SLOTS, 0:k * c],
                         self.dram[bass.ds(layer, 1), :, at:at + k * c].rearrange("o p n -> (o p) n")
                         ).then_inc(self.loaded[n % SLOTS], 16)
        self.sent = upto

    def arrive(self, pe, name):
        n = self.where[name][0]
        pe.wait_ge(self.loaded[n % SLOTS], 16 * (n // SLOTS + 1))

    def clear(self, nc):
        assert self.sent == len(self.names) and self.last == len(self.names) - 1
        for h in [*self.loaded, self.product]:
            nc.gpsimd.sem_clear(h)
        nc.all_engine_barrier()
        self.start()


def unit_product(pe, bank, w, col, x, token_major=False):
    kt = w.shape[1]
    for i in range(2):
        for k in range(kt):
            if token_major:
                lhs, rhs = x[:, k, i * P:(i + 1) * P], w[:, k, col:col + 256]
            else:
                lhs, rhs = w[:, k, col + i * P:col + (i + 1) * P], x[:, k, :]
            mm = pe.matmul(bank[:, i * 256:(i + 1) * 256], lhs, rhs, start=(k == 0), stop=(k == kt - 1))
    return mm


def norm_phase(nc, K, src, dst, gain, bias, eps, rms, out=None, ring=None, layer=None):
    with phase(nc, "turned stats rooted inverted scaled back stored dve_step act_step",
               [("xn", [P, TT, D]), ("bn", [P, TT, 2, 6]), ("mv", [P, TT, 2]), ("ms", [P, TT]), ("sd", [P, TT]),
                ("rs", [P, TT])],
               [("tok0", D), ("tok1", D)] + [(f"bk{i}", HALF) for i in range(4)]) as (block, s, b):
        tok = [b["tok0"], b["tok1"]]
        bk = [b["bk0"], b["bk1"], b["bk2"], b["bk3"]]

        @block.sync
        def _(sp):
            if ring is not None:
                ring.send(sp, layer)
            if out is not None:
                for tt in range(TT):
                    sp.wait_ge(s["stored"], tt + 1)
                    sp.dma_start(out[tt * P:(tt + 1) * P, :], b["xn"][:, tt, :]).then_inc(s["back"], 16)
                sp.wait_ge(s["back"], 16 * TT)

        @block.tensor
        def _(pe):
            for tt in range(TT):
                for k in range(KD):
                    mm = pe.transpose(tok[tt][:, k * P:(k + 1) * P], src[:, k, tt * P:(tt + 1) * P], K("ident"))
                mm.then_inc(s["turned"], 1)
            if out is not None:
                return
            pe.wait_ge(s["scaled"], TT)
            for k in range(KD):
                for tt in range(TT):
                    mm = pe.transpose(bk[k // 2][:, (k % 2) * 256 + tt * P:(k % 2) * 256 + (tt + 1) * P],
                                      b["xn"][:, tt, k * P:(k + 1) * P], K("ident"))
                if k % 2:
                    mm.then_inc(s["back"], 1)

        @block.vector
        def _(dve):
            chain = Chain(dve, s["dve_step"])
            for tt in range(TT):
                dve.wait_ge(s["turned"], tt + 1)
                dve.bn_stats(b["bn"][:, tt, 0, :], tok[tt][:, 0:HALF])
                chain.step(dve.bn_stats(b["bn"][:, tt, 1, :], tok[tt][:, HALF:D]))
                chain.step(dve.bn_aggr(b["mv"][:, tt, :], b["bn"][:, tt, :, :]))
                if rms:
                    chain.step(dve.scalar_tensor_tensor(b["ms"][:, tt:tt + 1], b["mv"][:, tt, 0:1], b["mv"][:, tt, 0:1],
                                                        b["mv"][:, tt, 1:2], ALU.mult, ALU.add))
                    dve.tensor_scalar(b["ms"][:, tt:tt + 1], b["ms"][:, tt:tt + 1], eps, None, ALU.add).then_inc(s["stats"], 1)
                else:
                    dve.tensor_scalar(b["ms"][:, tt:tt + 1], b["mv"][:, tt, 1:2], eps, None, ALU.add).then_inc(s["stats"], 1)
            for tt in range(TT):
                dve.wait_ge(s["rooted"], tt + 1)
                chain.step(dve.reciprocal(b["rs"][:, tt:tt + 1], b["sd"][:, tt:tt + 1]))
                if rms:
                    ins = dve.tensor_scalar(b["xn"][:, tt, :], tok[tt][:, :], b["rs"][:, tt:tt + 1], None, ALU.mult)
                else:
                    ins = dve.tensor_scalar(b["xn"][:, tt, :], tok[tt][:, :], b["mv"][:, tt, 0:1], b["rs"][:, tt:tt + 1],
                                            ALU.subtract, ALU.mult)
                if out is None:
                    ins.then_inc(s["scaled"], 1)
                else:
                    chain.step(ins)
                    dve.tensor_tensor(b["xn"][:, tt, :], b["xn"][:, tt, :], gain, ALU.mult).then_inc(s["stored"], 1)
            if out is not None:
                return
            for k in (2, 3, 6, 7):
                dve.wait_ge(s["back"], k // 2 + 1)
                v = bk[k // 2][:, (k % 2) * 256:(k % 2) * 256 + 256]
                if bias is None:
                    dve.tensor_scalar(dst[:, k, :], v, gain[:, k:k + 1], None, ALU.mult)
                else:
                    dve.tensor_scalar(dst[:, k, :], v, gain[:, k:k + 1], bias[:, k:k + 1], ALU.mult, ALU.add)

        @block.scalar
        def _(act):
            for tt in range(TT):
                act.wait_ge(s["stats"], tt + 1)
                act.activation(b["sd"][:, tt:tt + 1], b["ms"][:, tt:tt + 1], ACT.Sqrt).then_inc(s["rooted"], 1)
            if out is not None:
                return
            for k in (0, 1, 4, 5):
                act.wait_ge(s["back"], k // 2 + 1)
                v = bk[k // 2][:, (k % 2) * 256:(k % 2) * 256 + 256]
                if bias is None:
                    act.activation(dst[:, k, :], v, ACT.Copy, scale=gain[:, k:k + 1])
                else:
                    act.activation(dst[:, k, :], v, ACT.Identity, scale=gain[:, k:k + 1], bias=bias[:, k:k + 1])


NB = 4


class U:

    def __init__(self, chunk, col, kind, dst, more=None, x=None, tokens=False):
        self.chunk, self.col, self.kind, self.dst, self.more, self.x, self.tokens = chunk, col, kind, dst, more, x, tokens


def product_phase(nc, ring, layer, units, x, params=None):
    base = ring.plan([u.chunk for u in units])
    conv = [n for n, u in enumerate(units) if u.kind == "conv"]
    with phase(nc, "affine finished gated " + " ".join(f"free{i}" for i in range(NB)) + " dve_step",
               [("cb", [P, 2, 2, 256])] if conv else [],
               [(f"mm{i}", HALF) for i in range(NB)]) as (block, s, b):
        bank = [b[f"mm{i}"] for i in range(NB)]
        free = [s[f"free{i}"] for i in range(NB)]

        @block.sync
        def _(sp):
            ring.send(sp, layer)

        @block.tensor
        def _(pe):
            for n, u in enumerate(units):
                if n >= NB:
                    pe.wait_ge(free[n % NB], n // NB)
                if u.chunk in ring.where:
                    ring.arrive(pe, u.chunk)
                    w = ring.view(u.chunk)
                else:
                    w = params[u.chunk]
                bk = bank[n % NB]
                xu = x if u.x is None else u.x
                if u.kind == "rows":
                    rows, quantities = u.more
                    for r in range(quantities):
                        for k in range(KD):
                            c = u.col + r * rows
                            mm = pe.matmul(bk[0:rows, r * 256:(r + 1) * 256], w[:, k, c:c + rows], xu[:, k, :],
                                           start=(k == 0), stop=(k == KD - 1))
                elif u.kind == "tile":
                    for k in range(KD):
                        mm = pe.matmul(bk[:, 0:256], w[:, k, u.col:u.col + P], xu[:, k, :],
                                       start=(k == 0), stop=(k == KD - 1))
                else:
                    mm = unit_product(pe, bk, w, u.col, xu, u.tokens)
                mm.then_inc(ring.product, 1)

        @block.scalar
        def _(act):
            for n, u in enumerate(units):
                if u.kind not in ("act", "rows", "tile", "conv"):
                    continue
                fr = free[n % NB]
                act.wait_ge(ring.product, base + n + 1)
                v = bank[n % NB][:, :].rearrange("p (i t) -> p i t", i=2)
                if u.kind == "tile":
                    act.activation(u.dst, v[:, 0, :], ACT.Copy).then_inc(fr, 1)
                elif u.kind == "rows":
                    rows, quantities = u.more
                    act.activation(u.dst, v[0:rows, 0:quantities, :], ACT.Copy).then_inc(fr, 1)
                elif u.kind == "act":
                    func, bias = u.more
                    if bias is None:
                        act.activation(u.dst, v, func).then_inc(fr, 1)
                    else:
                        act.activation(u.dst[:, 0, :], v[:, 0, :], func, bias=bias[:, 0:1])
                        act.activation(u.dst[:, 1, :], v[:, 1, :], func, bias=bias[:, 1:2]).then_inc(fr, 1)
                else:
                    taps, wts, bs, c0, finish = u.more
                    i = conv.index(n)
                    if i >= 2:
                        act.wait_ge(s["finished"], i - 1)
                    for j in range(2):
                        c = c0 + j
                        cb = b["cb"][:, i % 2, j, :]
                        if bs is None:
                            ins = act.activation(cb, v[:, j, :], ACT.Copy, scale=wts[:, taps - 1, c:c + 1])
                        else:
                            ins = act.activation(cb, v[:, j, :], ACT.Identity, scale=wts[:, taps - 1, c:c + 1],
                                                 bias=bs[:, c:c + 1])
                    ins.then_inc(s["affine"], 1)
                    if finish == "silu":
                        act.wait_ge(fr, n // NB + 1)
                        act.activation(u.dst, b["cb"][:, i % 2, :, :], ACT.Silu).then_inc(s["finished"], 1)

        @block.vector
        def _(dve):
            chain = Chain(dve, s["dve_step"])
            for n, u in enumerate(units):
                if u.kind not in ("times", "residual", "conv", "gate_first", "gate_add"):
                    continue
                fr = free[n % NB]
                v = bank[n % NB][:, :].rearrange("p (i t) -> p i t", i=2)
                if u.kind == "conv":
                    taps, wts, bs, c0, finish = u.more
                    i = conv.index(n)
                    dve.wait_ge(s["affine"], i + 1)
                    for tap in range(1, taps):
                        for j in range(2):
                            c = c0 + j
                            ins = dve.scalar_tensor_tensor(b["cb"][:, i % 2, j, tap:T], v[:, j, 0:T - tap],
                                                           wts[:, taps - 1 - tap, c:c + 1], b["cb"][:, i % 2, j, tap:T],
                                                           ALU.mult, ALU.add)
                        if tap < taps - 1:
                            chain.step(ins)
                        else:
                            ins.then_inc(fr, 1)
                    if finish == "times":
                        dve.wait_ge(fr, n // NB + 1)
                        if conv.index(n) >= 1:
                            dve.wait_ge(s["finished"], conv.index(n))
                        dve.tensor_tensor(u.dst, u.dst, b["cb"][:, i % 2, :, :], ALU.mult).then_inc(s["finished"], 1)
                    continue
                dve.wait_ge(ring.product, base + n + 1)
                if u.kind == "times":
                    first = next(m for m in range(n) if units[m].dst is u.dst)
                    dve.wait_ge(free[first % NB], first // NB + 1)
                    dve.tensor_tensor(u.dst, u.dst, v, ALU.mult).then_inc(fr, 1)
                elif u.kind == "residual":
                    dve.scalar_tensor_tensor(u.dst, u.dst, u.more, v, ALU.mult, ALU.add).then_inc(fr, 1)
                else:
                    gate = max(m for m in range(n) if units[m].dst is u.more)
                    dve.wait_ge(free[gate % NB], gate // NB + 1)
                    if u.kind == "gate_first":
                        dve.tensor_tensor(u.dst, u.more, v, ALU.mult).then_inc(fr, 1)
                    else:
                        dve.tensor_tensor(u.more, u.more, v, ALU.mult).then_inc(fr, 1)
                        dve.wait_ge(fr, n // NB + 1)
                        before = max(m for m in range(n) if units[m].dst is u.dst)
                        dve.wait_ge(s["gated"] if units[before].kind == "gate_add" else free[before % NB],
                                    1 + (sum(w.kind == "gate_add" for w in units[:before])
                                         if units[before].kind == "gate_add" else before // NB))
                        dve.tensor_tensor(u.dst, u.dst, u.more, ALU.add).then_inc(s["gated"], 1)


def down_phase(nc, ring, layer, names, h, x, scale):
    base = ring.plan(names)
    with phase(nc, "", (), [(f"y{i}", HALF) for i in range(4)]) as (block, s, b):
        y = [b["y0"], b["y1"], b["y2"], b["y3"]]

        @block.sync
        def _(sp):
            ring.send(sp, layer)

        @block.tensor
        def _(pe):
            k = 0
            for name in names:
                ring.arrive(pe, name)
                w = ring.view(name)
                for kk in range(w.shape[1]):
                    for j in range(KD):
                        mm = pe.matmul(y[j // 2][:, (j % 2) * 256:(j % 2) * 256 + 256], w[:, kk, j * P:(j + 1) * P],
                                       h[:, k, :], start=(k == 0 and j % 2 == 0), stop=(k == KF - 1),
                                       skip_group_check=True)
                    k += 1
                mm.then_inc(ring.product, 1)

        @block.vector
        def _(dve):
            dve.wait_ge(ring.product, base + len(names))
            for i in range(4):
                xs = x[:, 2 * i:2 * i + 2, :]
                dve.scalar_tensor_tensor(xs, xs, scale, y[i][:, :].rearrange("p (i t) -> p i t", i=2),
                                         ALU.mult, ALU.add)


def rope_phase(nc, K, jobs, ring=None, layer=None):
    with phase(nc, "rotated read0 read1 dve_step done", [("c0", [P, 2, 256]), ("c1", [P, 2, 256]), ("r", [P, 2, 2, 256])],
               [("rot0", HALF), ("rot1", HALF)]) as (block, s, b):
        rot, read, cb = [b["rot0"], b["rot1"]], [s["read0"], s["read1"]], [b["c0"], b["c1"]]

        @block.sync
        def _(sp):
            if ring is not None:
                ring.send(sp, layer)

        @block.tensor
        def _(pe):
            for n, (raw, perm, cos, sin) in enumerate(jobs):
                if n >= 2:
                    pe.wait_ge(read[n % 2], n // 2)
                w = raw.shape[1]
                pe.matmul(rot[n % 2][:, 0:w * 256], perm, raw.rearrange("p i t -> p (i t)"),
                          start=True, stop=True).then_inc(s["rotated"], 1)

        @block.vector
        def _(dve):
            chain = Chain(dve, s["dve_step"])
            for n, (raw, perm, cos, sin) in enumerate(jobs):
                w = raw.shape[1]
                dve.wait_ge(s["rotated"], n + 1)
                r = b["r"][:, n % 2, 0:w, :]
                dve.tensor_tensor(r, rot[n % 2][:, 0:w * 256].rearrange("p (i t) -> p i t", i=w),
                                  sin.unsqueeze(1).to_broadcast([P, w, 256]), ALU.mult).then_inc(read[n % 2], 1)
                chain.step(dve.tensor_tensor(raw, raw, cos.unsqueeze(1).to_broadcast([P, w, 256]), ALU.mult))
                dve.wait_ge(read[n % 2], n // 2 + 1)
                dve.tensor_tensor(raw, raw, r, ALU.add)


def pair_slot(h):
    return (h % 2) * 2 + h // 2


class Group:

    def __init__(self, nk, scale, pairs, slot, mask, value, place, dst):
        self.nk, self.scale, self.pairs, self.slot = nk, scale, pairs, slot
        self.mask, self.value, self.place, self.dst = mask, value, place, dst


def attention_phase(nc, K, groups, ring=None, layer=None):
    with phase(nc, "scored masked shifted exped normed turned turned_out pv read_s0 read_s1 copied dve_step act_step "
                   "p_free out_free",
               [("sm", [P, 2, 4, 256]), ("pt", [P, 2, 8, P]), ("mx", [P, 2, 4]), ("sum", [P, 2, 4]), ("rc", [P, 2, 4])],
               [("s0", 2 * HALF), ("s1", 2 * HALF), ("tp", 2 * HALF), ("o", 2 * HALF)]) as (block, s, b):
        sc = [b["s0"], b["s1"]]

        @block.sync
        def _(sp):
            if ring is not None:
                ring.send(sp, layer)

        @block.tensor
        def _(pe):
            def scores(n):
                g = groups[n]
                if n >= 2:
                    pe.wait_ge(s["masked"], n - 1)
                for h in range(4):
                    pairs = g.pairs(h)
                    at = g.slot(h) * 256
                    for i, (lhs, rhs) in enumerate(pairs):
                        mm = pe.matmul(sc[n % 2][:, at:at + g.nk], lhs, rhs,
                                       start=(i == 0), stop=(i == len(pairs) - 1))
                mm.then_inc(s["scored"], 1)

            scores(0)
            for n, g in enumerate(groups):
                if n + 1 < len(groups):
                    scores(n + 1)
                kts = g.nk // P
                pe.wait_ge(s["normed"], n + 1)
                if n:
                    pe.wait_ge(s["copied"], n)
                for h in range(4):
                    for kt in range(kts):
                        mm = pe.transpose(b["tp"][:, (h * 2 + kt) * P:(h * 2 + kt + 1) * P],
                                          b["sm"][:, n % 2, h, kt * P:(kt + 1) * P], K("ident"))
                mm.then_inc(s["turned"], 1)
                pe.wait_ge(s["copied"], n + 1)
                if n:
                    pe.wait_ge(s["out_free"], n)
                for h in range(4):
                    for i, region in enumerate(g.place(b["o"], h)):
                        for kt in range(kts):
                            mm = pe.matmul(region, g.value(h, kt)[i], b["pt"][:, n % 2, g.slot(h) * 2 + kt, :],
                                           start=(kt == 0), stop=(kt == kts - 1))
                mm.then_inc(s["pv"], 1)

        @block.vector
        def _(dve):
            chain = Chain(dve, s["dve_step"])

            def weigh(n):
                g = groups[n]
                sm = b["sm"][:, n % 2, :, 0:g.nk]
                v = sc[n % 2][:, :].rearrange("p (h k) -> p h k", h=4)[:, :, 0:g.nk]
                dve.wait_ge(s["scored"], n + 1)
                if n >= 2:
                    dve.wait_ge(s["turned"], n - 1)
                if g.mask is None:
                    ins = dve.tensor_copy(sm, v)
                else:
                    ins = dve.tensor_tensor(sm, v, g.mask if g.mask.shape[1] == 4 else g.mask.to_broadcast([P, 4, g.nk]),
                                            ALU.add)
                ins.then_inc(s["masked"], 1)
                dve.wait_ge(s["masked"], n + 1)
                chain.step(dve.tensor_reduce(b["mx"][:, n % 2, :], sm, AX_X, ALU.max))
                dve.tensor_scalar(b["mx"][:, n % 2, :], b["mx"][:, n % 2, :], -g.scale, None, ALU.mult).then_inc(s["shifted"], 1)

            def normalise(n):
                g = groups[n]
                sm = b["sm"][:, n % 2, :, 0:g.nk]
                dve.wait_ge(s["exped"], 4 * (n + 1))
                chain.step(dve.reciprocal(b["rc"][:, n % 2, :], b["sum"][:, n % 2, :]))
                dve.tensor_tensor(sm, sm, b["rc"][:, n % 2, :].unsqueeze(2).to_broadcast([P, 4, g.nk]),
                                  ALU.mult).then_inc(s["normed"], 1)

            weigh(0)
            for n, g in enumerate(groups):
                if n + 1 < len(groups):
                    weigh(n + 1)
                normalise(n)
                dve.wait_ge(s["pv"], n + 1)
                for i, (region, dst) in enumerate(g.dst(b["o"])):
                    ins = dve.tensor_copy(dst, region)
                ins.then_inc(s["out_free"], 1)

        @block.scalar
        def _(act):
            def exponentials(n):
                g = groups[n]
                act.wait_ge(s["shifted"], n + 1)
                for h in range(4):
                    act.activation(b["sm"][:, n % 2, h, 0:g.nk], b["sm"][:, n % 2, h, 0:g.nk], ACT.Exp,
                                   bias=b["mx"][:, n % 2, h:h + 1], scale=g.scale,
                                   accum_out=b["sum"][:, n % 2, h:h + 1]).then_inc(s["exped"], 1)

            exponentials(0)
            for n, g in enumerate(groups):
                if n + 1 < len(groups):
                    exponentials(n + 1)
                act.wait_ge(s["turned"], n + 1)
                if n >= 2:
                    act.wait_ge(s["pv"], n - 1)
                tp = b["tp"][:, :].rearrange("p (h k q) -> p h k q", h=4, k=2)[:, :, 0:g.nk // P, :]
                pt = b["pt"][:, n % 2, :, :].rearrange("p (h k) q -> p h k q", h=4)[:, :, 0:g.nk // P, :]
                act.activation(pt, tp, ACT.Copy).then_inc(s["copied"], 1)


def side_phase(nc, K, prm, sgu_rows, buf, ring, layer):
    c8 = 2 * 4
    with phase(nc, "negc spread tril gates exped logged summed rooted vn mixed band pooled pmix dve_step act_step",
               [("wT", [P, 4, P]), ("lf", [4, 3, T]), ("on", [4, T]), ("m", [P, c8]), ("ms", [P, c8]), ("sd", [P, c8]),
                ("cen", [P, c8, 64]), ("sq", [P, c8, 64]), ("pooled", [P, 2, 256])],
               [("mix", HALF), ("pb", HALF), ("pm", HALF), ("c", 2 * HALF)]) as (block, s, b):

        @block.sync
        def _(sp):
            ring.send(sp, layer)

        @block.gpsimd
        def _(pool):
            pool.affine_select(out=b["wT"][:, :, :], in_=prm("sgu_wT").rearrange("p (g t) -> p g t", g=4),
                               compare_op=ALU.is_ge, fill=0.0, base=0, pattern=[[0, 4], [1, P]],
                               channel_multiplier=-1).then_inc(s["tril"], 1)

        @block.vector
        def _(dve):
            chain = Chain(dve, s["dve_step"])
            y, ab, lf = b["lf"][:, 0, :], b["lf"][:, 1, :], b["lf"][:, 2, :]
            dve.memset(b["on"][:, :], 1.0)
            chain.step(dve.tensor_scalar(y, buf["bf"][:, :], prm("b_forget")[0:4, :], None, ALU.add))
            chain.step(dve.tensor_scalar(ab, y, -1.0, None, ALU.mult))
            dve.tensor_tensor(ab, y, ab, ALU.max).then_inc(s["gates"], 1)
            cv = buf["cv"].rearrange("p t (g c) -> p (t g) c", g=4)
            chain.step(dve.tensor_reduce(b["m"][:, :], cv, AX_X, ALU.add))
            chain.step(dve.tensor_scalar(b["m"][:, :], b["m"][:, :], 1.0 / 64, None, ALU.mult))
            chain.step(dve.tensor_tensor(b["cen"][:, :, :], cv, b["m"][:, :].unsqueeze(2).to_broadcast([P, c8, 64]),
                                         ALU.subtract))
            chain.step(dve.tensor_tensor(b["sq"][:, :, :], b["cen"][:, :, :], b["cen"][:, :, :], ALU.mult))
            chain.step(dve.tensor_reduce(b["ms"][:, :], b["sq"][:, :, :], AX_X, ALU.add))
            dve.tensor_scalar(b["ms"][:, :], b["ms"][:, :], 1.0 / 64, LN_EPS, ALU.mult, ALU.add).then_inc(s["summed"], 1)
            dve.wait_ge(s["logged"], 1)
            chain.step(dve.scalar_tensor_tensor(lf, y, 0.0, lf, ALU.min, ALU.subtract))
            chain.step(dve.tensor_tensor_scan(y, b["on"][:, :], lf, 0.0, ALU.mult, ALU.add))
            dve.tensor_scalar(buf["negc"][:, :], y, -8.0, None, ALU.mult).then_inc(s["negc"], 1)
            dve.wait_ge(s["rooted"], 1)
            chain.step(dve.reciprocal(b["sd"][:, :], b["sd"][:, :]))
            chain.step(dve.tensor_tensor(b["cen"][:, :, :], b["cen"][:, :, :],
                                         b["sd"][:, :].unsqueeze(2).to_broadcast([P, c8, 64]), ALU.mult))
            cen = b["cen"][:, :, :].rearrange("p (t g) c -> p t (g c)", t=2)
            chain.step(dve.tensor_tensor(cen, cen, sgu_rows[:, 0:256].unsqueeze(1).to_broadcast([P, 2, 256]), ALU.mult))
            dve.tensor_tensor(cen, cen, sgu_rows[:, 256:512].unsqueeze(1).to_broadcast([P, 2, 256]),
                              ALU.add).then_inc(s["vn"], 1)
            dve.wait_ge(s["spread"], 1)
            for q in range(TT):
                dve.tensor_tensor(buf["forget"][:, q, :, :], b["c"][:, :].rearrange("p (h k) -> p h k", h=4),
                                  K("causal").rearrange("p (q k) -> p q k", q=2)[:, q:q + 1, :].to_broadcast([P, 4, T]),
                                  ALU.add)
            dve.wait_ge(s["mixed"], 1)
            dve.tensor_tensor(buf["yT"][:, 4:6, :], buf["cu"], b["mix"][:, :].rearrange("p (i t) -> p i t", i=2), ALU.mult)

        @block.scalar
        def _(act):
            act.wait_ge(s["gates"], 1)
            act.activation(b["lf"][:, 2, :], b["lf"][:, 1, :], ACT.Exp, scale=-1.0).then_inc(s["exped"], 1)
            act.wait_ge(s["exped"], 1)
            act.activation(b["lf"][:, 2, :], b["lf"][:, 2, :], ACT.Ln, bias=1.0).then_inc(s["logged"], 1)
            act.wait_ge(s["summed"], 1)
            act.activation(b["sd"][:, :], b["ms"][:, :], ACT.Sqrt).then_inc(s["rooted"], 1)
            act.wait_ge(s["band"], 1)
            act.activation(b["pooled"][:, :, :], b["pb"][:, :].rearrange("p (i t) -> p i t", i=2), ACT.Copy).then_inc(s["pooled"], 1)
            act.wait_ge(s["pmix"], 1)
            for i in range(2):
                act.activation(buf["yT"][:, 6 + i, :], b["pm"][:, i * 256:(i + 1) * 256], ACT.Copy,
                               scale=prm("pool_scale")[:, i:i + 1])

        @block.tensor
        def _(pe):
            band = K("band").rearrange("p (s g t) -> p s g t", s=2, g=4)
            for g in range(4):
                r = slice((g % 2) * 64, (g % 2) * 64 + 64)
                for st in range(2):
                    mm = pe.matmul(b["pb"][r, (g // 2) * 256:(g // 2) * 256 + 256], buf["dp"][:, st, g * 64:(g + 1) * 64],
                                   band[:, st, g, :], start=(st == 0), stop=(st == 1))
            mm.then_inc(s["band"], 1)
            pe.wait_ge(s["pooled"], 1)
            pw = prm("pool_w").rearrange("p (i d) -> p i d", i=2)
            for g in range(4):
                r = slice((g % 2) * 64, (g % 2) * 64 + 64)
                mm = pe.matmul(b["pm"][r, (g // 2) * 256:(g // 2) * 256 + 256], pw[r, g // 2, :], b["pooled"][r, g // 2, :],
                               start=True, stop=True)
            mm.then_inc(s["pmix"], 1)
            pe.wait_ge(s["negc"], 1)
            for h in range(4):
                mm = pe.matmul(b["c"][:, pair_slot(h) * 256:(pair_slot(h) + 1) * 256],
                               K("select").rearrange("p (h m) -> p h m", h=8)[0:4, h, :], buf["negc"][:, :],
                               start=True, stop=True)
            mm.then_inc(s["spread"], 1)
            pe.wait_ge(s["tril"], 1)
            pe.wait_ge(s["vn"], 1)
            vn = b["cen"][:, :, :].rearrange("p (t g) c -> p t g c", t=2)
            for g in range(4):
                r = slice((g % 2) * 64, (g % 2) * 64 + 64)
                for tt in range(TT):
                    region = b["mix"][r, (g // 2) * 256 + tt * P:(g // 2) * 256 + (tt + 1) * P]
                    pe.matmul(region, vn[:, tt, g, :], b["wT"][:, g, :], start=True, stop=False)
                    mm = pe.matmul(region, K("ones")[0:1, 0:64], prm("sgu_b")[0:1, g * P:(g + 1) * P],
                                   start=False, stop=True)
            mm.then_inc(s["mixed"], 1)


def first_layer(nc, K, layer, x, ring, par_dram, rows_dram):
    with ExitStack() as ctx:
        par = ctx.enter_context(nc.sbuf_tensor("par1_sb", [P, NPC1], F32))
        rows = ctx.enter_context(nc.sbuf_tensor("rows1_sb", [P, 512], F32))
        yT = ctx.enter_context(nc.sbuf_tensor("yT", [P, KD, T], F32))[:, :, :]
        prm = lambda name: par[:, PC1[name]]
        with phase(nc, "params") as (block, s, b):
            @block.sync
            def _(sp):
                sp.dma_start(par[:, :], par_dram[bass.ds(layer, 1), :, :].rearrange("o p n -> (o p) n")
                             ).then_inc(s["params"], 16)
                sp.dma_start(rows[:, :], rows_dram[bass.ds(layer, 1), :].to_broadcast([P, 512])).then_inc(s["params"], 16)
                ring.send(sp, layer)
                sp.wait_ge(s["params"], 32)

        with ExitStack() as mix:
            def sb(name, shape):
                return mix.enter_context(nc.sbuf_tensor(name, shape, F32))

            buf = {"yT": yT}
            aqk, bqk = sb("aqk", [P, 4, T]), sb("bqk", [P, 4, T])
            av, bv = sb("av", [P, 2, 256]), sb("bv", [P, 2, 256])
            buf["bf"], buf["negc"], buf["forget"] = sb("bf", [4, T]), sb("negc", [4, T]), sb("forget", [P, 2, 4, T])
            buf["cu"], buf["cv"], buf["dp"] = (sb(n, [P, 2, 256])[:, :, :] for n in ("cu", "cv", "dp"))
            copy = (ACT.Copy, None)
            gelu = (ACT.Gelu, None)
            product_phase(nc, ring, layer, [
                U("in0", 0, "act", aqk[:, 0:2, :], copy), U("in0", 256, "act", aqk[:, 2:4, :], copy),
                U("in1", 0, "act", av[:, :, :], copy, tokens=True), U("in1", 256, "act", bqk[:, 0:2, :], copy),
                U("in2", 0, "act", bqk[:, 2:4, :], copy), U("in2", 256, "act", bv[:, :, :], copy, tokens=True),
                U("in3", 0, "rows", buf["bf"][:, :].unsqueeze(1), (4, 1)),
                U("in3", 4, "act", buf["cu"], gelu), U("in3", 260, "act", buf["cv"], gelu, tokens=True),
                U("in4", 0, "act", buf["dp"], copy, tokens=True)], x)
            rope_phase(nc, K, [(aqk[:, 2 * i:2 * i + 2, :], K("perm64"), K("cos"), K("sin")) for i in range(2)],
                       ring, layer)
            side_phase(nc, K, prm, rows, buf, ring, layer)

            def group(qk, v, y0, q0, forget):
                nk = q0 + P
                causal = K("causal").rearrange("p (q k) -> p q k", q=2)[:, q0 // P:q0 // P + 1, 0:nk]

                def pairs(h):
                    r = slice((h % 2) * 64, (h % 2) * 64 + 64)
                    return [(qk[r, h // 2, q0:q0 + P], qk[r, 2 + h // 2, 0:nk])]

                return Group(
                    nk=nk, scale=0.125, pairs=pairs, slot=pair_slot,
                    mask=buf["forget"][:, q0 // P, :, 0:nk] if forget else causal,
                    value=lambda h, kt: [v[:, kt, h * 64:(h + 1) * 64]],
                    place=lambda o, h: [o[(h % 2) * 64:(h % 2) * 64 + 64, (h // 2) * P:(h // 2 + 1) * P]],
                    dst=lambda o: [(o[:, 0:256].rearrange("p (i q) -> p i q", i=2), yT[:, y0:y0 + 2, q0:q0 + P])])

            attention_phase(nc, K, [group(aqk, av, 0, 0, False), group(aqk, av, 0, P, False),
                                    group(bqk, bv, 2, 0, True), group(bqk, bv, 2, P, True)], ring, layer)

        product_phase(nc, ring, layer,
                      [U(f"o{i // 2}", (i % 2) * 256, "residual", x[:, 2 * i:2 * i + 2, :], ALPHA) for i in range(4)], yT)
        norm_phase(nc, K, x, x, prm("ln1_g"), prm("ln1_b"), LN_EPS, False, ring=ring, layer=layer)
        with nc.sbuf_tensor("hid1", [P, KF, T], F32) as hid:
            taps = prm("conv_w").rearrange("p (j c) -> p j c", j=3)
            hv = [hid[:, 2 * i:2 * i + 2, :] for i in range(KF // 2)]
            product_phase(nc, ring, layer, [
                U(f"up{i // 2}", (i % 2) * 256, "conv", hv[i % 11],
                  (3, taps, prm("conv_b"), 2 * i, "silu" if i < 11 else "times")) for i in range(KF)], x)
            down_phase(nc, ring, layer, [f"down{i}" for i in range(6)], hid, x, ALPHA)
        norm_phase(nc, K, x, x, prm("ln2_g"), prm("ln2_b"), LN_EPS, False, ring=ring, layer=layer)
        ring.clear(nc)


def build_first(nc, xT_dram, w_dram, par_dram, rows_dram, const_dram, out_dram):
    with ExitStack() as ctx:
        const = ctx.enter_context(nc.sbuf_tensor("const_sb", [P, NCC], F32))
        x = ctx.enter_context(nc.sbuf_tensor("x_sb", [P, KD, T], F32))[:, :, :]
        K = lambda name: const[:, CC[name]]
        ring = Ring(nc, ctx, "w1", CHUNKS_1, w_dram)
        with phase(nc, "begin") as (block, s, b):
            @block.sync
            def _(sp):
                sp.dma_start(const[:, :], const_dram).then_inc(s["begin"], 16)
                sp.dma_start(x, xT_dram).then_inc(s["begin"], 16)
                sp.wait_ge(s["begin"], 32)
        with nc.Fori(0, DEPTH) as layer:
            first_layer(nc, K, layer, x, ring, par_dram, rows_dram)
        with phase(nc, "stored") as (block, s, b):
            @block.sync
            def _(sp):
                sp.dma_start(out_dram, x).then_inc(s["stored"], 16)
                sp.wait_ge(s["stored"], 16)


def chunked(w_parts, chunks):
    out = []
    for (name, k, c), (w, row, col) in zip(chunks, w_parts):
        a = w[:, row:row + k * P, col:col + c]
        out.append(a.reshape(a.shape[0], k, P, c).transpose(0, 2, 1, 3).reshape(a.shape[0], P, k * c))
    return np.ascontiguousarray(np.concatenate(out, axis=2))


def lay_first(i):
    w_in, w_o, w_up, w_down = i["w_in"], i["w_o"], i["w_up"], i["w_down"]
    parts = ([(w_in, 0, c) for c in (0, 512, 1024, 1536, 2052)] + [(w_o, 0, c) for c in (0, 512)]
             + [(w_up, 0, 512 * n) for n in range(11)] + [(w_down, 512 * n, 0) for n in range(6)])
    par = np.zeros((DEPTH, P, NPC1), np.float32)

    def cols(name, a):
        par[:, :, PC1[name]] = a.reshape(DEPTH, -1, P).transpose(0, 2, 1)

    for name in ("ln1_g", "ln1_b", "ln2_g", "ln2_b", "conv_b", "pool_scale"):
        cols(name, i[name])
    cols("conv_w", i["conv_w"].reshape(DEPTH, -1))
    par[:, 0:4, PC1["b_forget"]] = i["b_forget"][:, :, None]
    par[:, :, PC1["sgu_wT"]] = i["sgu_w"].transpose(0, 3, 1, 2).reshape(DEPTH, P, -1)
    par[:, 0, PC1["sgu_b"]] = i["sgu_b"].reshape(DEPTH, -1)
    par[:, :, PC1["pool_w"]] = i["pool_w"].reshape(DEPTH, 2, P, 64).transpose(0, 2, 1, 3).reshape(DEPTH, P, -1)
    rows = np.concatenate([i["sgu_ln_g"], i["sgu_ln_b"]], axis=1)
    return chunked(parts, CHUNKS_1), par, rows


def tiles_of(a):
    return np.ascontiguousarray(a.reshape(T, KD, P).transpose(2, 1, 0))


def angle_phase(nc, K, pos_dram, tables):
    magic = 1.5 * 2.0 ** 23
    c1 = 6.28125
    c2 = float(np.float32(2 * np.pi - c1).view(np.int32) // 4096 * 4096 and
               (np.float32(2 * np.pi - c1).view(np.int32) // 4096 * 4096).astype(np.int32).view(np.float32))
    c3 = 2 * np.pi - c1 - c2
    with phase(nc, "pos reduced sined dve_step",
               [("pos", [P, T]), ("k", [P, 2, T]), ("a", [P, 2, T]), ("h", [P, 2, T])]) as (block, s, b):
        posi = b["k"][:, 0, :].bitcast(I32)

        @block.sync
        def _(sp):
            sp.dma_start(posi, pos_dram.to_broadcast([P, T])).then_inc(s["pos"], 16)

        @block.vector
        def _(dve):
            chain = Chain(dve, s["dve_step"])
            dve.wait_ge(s["pos"], 16)
            chain.step(dve.tensor_copy(b["pos"][:, :], posi))
            for j in range(2):
                chain.step(dve.tensor_scalar(b["a"][:, j, :], b["pos"][:, :], K("freq")[:, j:j + 1], None, ALU.mult))
            a, k = b["a"][:, :, :], b["k"][:, :, :]
            chain.step(dve.tensor_scalar(k, a, 1.0 / (2 * np.pi), magic, ALU.mult, ALU.add))
            chain.step(dve.tensor_scalar(k, k, magic, None, ALU.subtract))
            for c in (c1, c2, c3):
                chain.step(dve.scalar_tensor_tensor(a, k, -c, a, ALU.mult, ALU.add))
            dve.tensor_scalar(a, a, 3.1415925, -3.1415925, ALU.min, ALU.max).then_inc(s["reduced"], 1)
            dve.wait_ge(s["sined"], 2)
            chain.step(dve.tensor_tensor(b["h"][:, :, :], b["h"][:, :, :], b["h"][:, :, :], ALU.mult))
            dve.tensor_scalar(tables[:, 0:2, :], b["h"][:, :, :], -2.0, 1.0, ALU.mult, ALU.add)

        @block.scalar
        def _(act):
            act.wait_ge(s["reduced"], 1)
            act.activation(tables[:, 2:4, :], b["a"][:, :, :], ACT.Sin).then_inc(s["sined"], 1)
            act.activation(b["h"][:, :, :], b["a"][:, :, :], ACT.Sin, scale=0.5).then_inc(s["sined"], 1)


QTY = 5


def decay_phase(nc, K, prm, small, ge, rowq, tokq, ring, layer):
    with phase(nc, "beta absed exped logged alog g gced ged rows turned dve_step act_step",
               [("y", [8, T]), ("ab", [8, T]), ("lf", [8, T]), ("on", [8, T]), ("ea", [8, 1])],
               [("tq", HALF)]) as (block, s, b):

        @block.sync
        def _(sp):
            ring.send(sp, layer)

        @block.vector
        def _(dve):
            chain = Chain(dve, s["dve_step"])
            y, ab, lf = b["y"][:, :], b["ab"][:, :], b["lf"][:, :]
            gc = rowq[:, 1, :]
            dve.memset(b["on"][:, :], 1.0)
            chain.step(dve.tensor_scalar(y, small[:, 1, :], prm("dt_bias")[0:8, :], None, ALU.add))
            chain.step(dve.tensor_scalar(ab, y, -1.0, None, ALU.mult))
            dve.tensor_tensor(ab, y, ab, ALU.max).then_inc(s["absed"], 1)
            dve.tensor_scalar(rowq[:, 4, :], small[:, 2, :], IDX_SCALE, None, ALU.mult)
            dve.wait_ge(s["logged"], 1)
            dve.wait_ge(s["alog"], 1)
            chain.step(dve.scalar_tensor_tensor(lf, y, 0.0, lf, ALU.max, ALU.add))
            chain.step(dve.tensor_scalar(lf, lf, b["ea"][:, 0:1], -1.0, ALU.mult, ALU.mult))
            for c in range(NCH):
                r = slice(c * CH, (c + 1) * CH)
                ins = dve.tensor_tensor_scan(rowq[:, 1, r], b["on"][:, r], lf[:, r], 0.0, ALU.mult, ALU.add)
            chain.step(ins)
            v = gc.rearrange("p (c i) -> p c i", c=NCH)
            dve.tensor_tensor(ab.rearrange("p (c i) -> p c i", c=NCH), v, v[:, :, CH - 1:CH].to_broadcast([8, NCH, CH]),
                              ALU.subtract).then_inc(s["gced"], 1)
            dve.wait_ge(s["ged"], 2)
            dve.wait_ge(s["beta"], 1)
            dve.tensor_tensor(rowq[:, 2, :], rowq[:, 0, :], ge, ALU.mult).then_inc(s["rows"], 1)
            dve.wait_ge(s["turned"], 1)
            dve.tensor_copy(tokq, b["tq"][:, 0:TT * QTY * 8].rearrange("p (t q h) -> p t q h", t=TT, q=QTY))

        @block.scalar
        def _(act):
            act.activation(rowq[:, 0, :], small[:, 0, :], ACT.Sigmoid).then_inc(s["beta"], 1)
            act.activation(b["ea"][:, :], prm("a_log")[0:8, :], ACT.Exp).then_inc(s["alog"], 1)
            act.wait_ge(s["absed"], 1)
            act.activation(b["lf"][:, :], b["ab"][:, :], ACT.Exp, scale=-1.0).then_inc(s["exped"], 1)
            act.wait_ge(s["exped"], 1)
            act.activation(b["lf"][:, :], b["lf"][:, :], ACT.Ln, bias=1.0).then_inc(s["logged"], 1)
            act.wait_ge(s["gced"], 1)
            act.activation(ge, rowq[:, 1, :], ACT.Exp).then_inc(s["ged"], 1)
            act.activation(rowq[:, 3, :], b["ab"][:, :], ACT.Exp, scale=-1.0).then_inc(s["ged"], 1)

        @block.tensor
        def _(pe):
            pe.wait_ge(s["rows"], 1)
            for tt in range(TT):
                for q in range(QTY):
                    at = (tt * QTY + q) * 8
                    mm = pe.transpose(b["tq"][:, at:at + 8], rowq[:, q, tt * P:(tt + 1) * P], K("ident")[0:8, 0:8])
            mm.then_inc(s["turned"], 1)


def unit_keys_phase(nc, K, q, k, eps, ring, layer):
    jobs = [(v, i, sc) for v, sc in ((q, P ** -0.5), (k, 1.0)) for i in range(0, KD, 2)]
    with phase(nc, "squared summed read0 read1 plus_eps rooted inverted scaled",
               [("sq", [P, 2, 2, T]), ("r", [P, 2, 2, T])], [("ss0", HALF), ("ss1", HALF)]) as (block, s, b):
        ss, read = [b["ss0"], b["ss1"]], [s["read0"], s["read1"]]

        @block.sync
        def _(sp):
            ring.send(sp, layer)

        @block.tensor
        def _(pe):
            for n, (v, i, sc) in enumerate(jobs):
                pe.wait_ge(s["squared"], n + 1)
                if n >= 2:
                    pe.wait_ge(s["plus_eps"], n - 1)
                pe.matmul(ss[n % 2][:, :], K("ones"), b["sq"][:, n % 2, :, :].rearrange("p i t -> p (i t)"),
                          start=True, stop=True).then_inc(s["summed"], 1)

        @block.scalar
        def _(act):
            for n, (v, i, sc) in enumerate(jobs):
                if n >= 2:
                    act.wait_ge(s["summed"], n - 1)
                act.activation(b["sq"][:, n % 2, :, :], v[:, i:i + 2, :], ACT.Square).then_inc(s["squared"], 1)
                if n >= 1:
                    act.wait_ge(s["plus_eps"], n)
                    r = b["r"][:, (n - 1) % 2, :, :]
                    act.activation(r, r, ACT.Sqrt).then_inc(s["rooted"], 1)
            act.wait_ge(s["plus_eps"], len(jobs))
            r = b["r"][:, (len(jobs) - 1) % 2, :, :]
            act.activation(r, r, ACT.Sqrt).then_inc(s["rooted"], 1)

        @block.vector
        def _(dve):
            def finish(n):
                v, i, sc = jobs[n]
                r = b["r"][:, n % 2, :, :]
                dve.wait_ge(s["rooted"], n + 1)
                dve.reciprocal(r, r).then_inc(s["inverted"], 1)
                dve.wait_ge(s["inverted"], n + 1)
                dve.scalar_tensor_tensor(v[:, i:i + 2, :], r, sc, v[:, i:i + 2, :], ALU.mult, ALU.mult
                                         ).then_inc(s["scaled"], 1)

            for n in range(len(jobs)):
                dve.wait_ge(s["summed"], n + 1)
                if n >= 2:
                    dve.wait_ge(s["scaled"], n - 1)
                dve.tensor_scalar(b["r"][:, n % 2, :, :], ss[n % 2][:, :].rearrange("p (i t) -> p i t", i=2), eps, None,
                                  ALU.add).then_inc(s["plus_eps"], 1)
                if n >= 1:
                    finish(n - 1)
            finish(len(jobs) - 1)


NP = 8


def delta_prepare_phase(nc, K, hf, q, k, v, ge, rowq, tokq, h, ring, layer):
    sel = K("select").rearrange("p (h m) -> p h m", h=8)
    upper, strict = K("upper"), K("strict")
    with phase(nc, "turned read spread_g spread_e spread_b bread grams diffed exped masked dve_step eb_read gread",
               [("e", [P, NP, P]), ("es", [P, NP, P])],
               [("g0", HALF), ("g1", HALF), ("e0", HALF), ("e1", HALF), ("t0", HALF), ("t1", HALF), ("m0", HALF),
                ("m1", HALF)]) as (block, s, b):
        g, e, t, m = [b["g0"], b["g1"]], [b["e0"], b["e1"]], [b["t0"], b["t1"]], [b["m0"], b["m1"]]

        @block.sync
        def _(sp):
            ring.send(sp, layer)

        @block.tensor
        def _(pe):
            for hh in range(4):
                pe.matmul(g[hh // 2][:, (hh % 2) * T:(hh % 2 + 1) * T], sel[0:8, 4 * hf + hh, :], rowq[:, 1, :],
                          start=True, stop=True).then_inc(s["spread_g"], 1)
            for hh in range(4):
                mm = pe.matmul(e[hh // 2][:, (hh % 2) * T:(hh % 2 + 1) * T], sel[0:8, 4 * hf + hh, :], ge,
                               start=True, stop=True)
            mm.then_inc(s["spread_e"], 1)
            for n, src in enumerate((k, v)):
                for tt in range(TT):
                    if n:
                        pe.wait_ge(s["read"], 1 + tt)
                    for hh in range(4):
                        mm = pe.transpose(t[tt][:, hh * P:(hh + 1) * P], src[:, 4 * hf + hh, tt * P:(tt + 1) * P],
                                          K("ident"))
                    mm.then_inc(s["turned"], 1)
            for n, other in enumerate((q, k)):
                for tt in range(TT):
                    if n:
                        pe.wait_ge(s["gread"], 1 + tt)
                    for hh in range(4):
                        hd, c = 4 * hf + hh, slice(tt * P, (tt + 1) * P)
                        mm = pe.matmul(m[tt][:, hh * P:(hh + 1) * P], k[:, hd, c], other[:, hd, c], start=True, stop=True)
                    mm.then_inc(s["grams"], 1)
            pe.wait_ge(s["diffed"], 1)
            for hh in range(4):
                mm = pe.matmul(g[hh // 2][:, (hh % 2) * T:(hh % 2 + 1) * T], sel[0:8, 4 * hf + hh, :], rowq[:, 0, :],
                               start=True, stop=True)
            mm.then_inc(s["spread_b"], 1)

        @block.vector
        def _(dve):
            chain = Chain(dve, s["dve_step"])
            for hh in range(4):
                dve.wait_ge(s["spread_g"], 4)
                for tt in range(TT):
                    ins = dve.tensor_scalar(b["e"][:, tt * 4 + hh, :],
                                            g[hh // 2][:, (hh % 2) * T + tt * P:(hh % 2) * T + (tt + 1) * P],
                                            tokq[:, tt, 1, 4 * hf + hh:4 * hf + hh + 1], 0.0, ALU.subtract, ALU.min)
            ins.then_inc(s["diffed"], 1)
            dve.wait_ge(s["spread_e"], 1)
            for i in range(2):
                ev = e[i][:, :].rearrange("p (h t) -> p h t", h=2)
                dve.tensor_copy(h["ge"][:, 2 * i:2 * i + 2, :], ev)
                dve.tensor_tensor(h["qd"][:, 2 * i:2 * i + 2, :], q[:, 4 * hf + 2 * i:4 * hf + 2 * i + 2, :], ev, ALU.mult)

            def token(qty, tt):
                return tokq[:, tt, qty, 4 * hf:4 * hf + 4].unsqueeze(2).to_broadcast([P, 4, P])

            for tt in range(TT):
                dve.wait_ge(s["turned"], tt + 1)
                tv = t[tt][:, :].rearrange("p (h d) -> p h d", h=4)
                pr = slice(tt * 4, tt * 4 + 4)
                dve.tensor_tensor(h["kb"][:, pr, :], tv, token(2, tt), ALU.mult)
                dve.tensor_tensor(h["kd"][:, pr, :], tv, token(3, tt), ALU.mult).then_inc(s["read"], 1)
            for tt in range(TT):
                dve.wait_ge(s["turned"], TT + tt + 1)
                dve.tensor_tensor(h["vb"][:, tt * 4:tt * 4 + 4, :], t[tt][:, :].rearrange("p (h d) -> p h d", h=4),
                                  token(0, tt), ALU.mult)
            dve.wait_ge(s["exped"], 1)
            chain.step(dve.tensor_tensor(b["e"][:, :, :], b["e"][:, :, :], upper.unsqueeze(1).to_broadcast([P, NP, P]), ALU.mult))
            dve.tensor_tensor(b["es"][:, :, :], b["e"][:, :, :], strict.unsqueeze(1).to_broadcast([P, NP, P]), ALU.mult)
            for tt in range(TT):
                dve.wait_ge(s["grams"], tt + 1)
                pr = slice(tt * 4, tt * 4 + 4)
                dve.tensor_tensor(h["at"][:, pr, :], m[tt][:, :].rearrange("p (h i) -> p h i", h=4), b["e"][:, pr, :],
                                  ALU.mult).then_inc(s["gread"], 1)
            dve.wait_ge(s["spread_b"], 1)
            for hh in range(4):
                for tt in range(TT):
                    es = b["es"][:, tt * 4 + hh, :]
                    ins = dve.tensor_tensor(es, es, g[hh // 2][:, (hh % 2) * T + tt * P:(hh % 2) * T + (tt + 1) * P],
                                            ALU.mult)
            chain.step(ins)
            for tt in range(TT):
                dve.wait_ge(s["grams"], TT + tt + 1)
                pr = slice(tt * 4, tt * 4 + 4)
                dve.tensor_tensor(h["mt"][:, pr, :], m[tt][:, :].rearrange("p (h i) -> p h i", h=4), b["es"][:, pr, :], ALU.mult)

        @block.scalar
        def _(act):
            act.wait_ge(s["diffed"], 1)
            act.activation(b["e"][:, :, :], b["e"][:, :, :], ACT.Exp).then_inc(s["exped"], 1)


def delta_solve_phase(nc, K, h, ring, layer):
    ident = K("ident").unsqueeze(1).to_broadcast([P, 4, P])
    lev = K("levels").rearrange("p (l i) -> p l i", l=6)
    with phase(nc, "begun lower0 lower1 masked0 masked1 cross0 cross1 kept0 kept1 solved dve_step",
               [("t", [P, NP, P]), ("y", [P, NP, P])],
               [(f"{n}{i}", HALF) for n in ("y_ps", "d_ps", "c_ps") for i in range(2)]) as (block, s, b):
        yp, dp, cp = [b["y_ps0"], b["y_ps1"]], [b["d_ps0"], b["d_ps1"]], [b["c_ps0"], b["c_ps1"]]
        lower, masked = [s["lower0"], s["lower1"]], [s["masked0"], s["masked1"]]
        cross, kept = [s["cross0"], s["cross1"]], [s["kept0"], s["kept1"]]

        @block.sync
        def _(sp):
            ring.send(sp, layer)

        @block.tensor
        def _(pe):
            pe.wait_ge(s["begun"], 4)
            for lv in range(6):
                for g in range(2):
                    if lv:
                        pe.wait_ge(kept[g], 2 * lv)
                    for n in range(4 * g, 4 * g + 4):
                        mm = pe.matmul(yp[g][:, (n % 4) * P:(n % 4 + 1) * P], h["mt"][:, n, :], b["t"][:, n, :],
                                       start=True, stop=True)
                    mm.then_inc(lower[g], 1)
                for g in range(2):
                    pe.wait_ge(masked[g], lv + 1)
                    for n in range(4 * g, 4 * g + 4):
                        c = slice((n % 4) * P, (n % 4 + 1) * P)
                        if lv < 5:
                            pe.matmul(dp[g][:, c], h["ti"][:, n, :], b["y"][:, n, :], start=True, stop=True)
                        mm = pe.matmul(cp[g][:, c], b["y"][:, n, :], h["ti"][:, n, :], start=True, stop=True)
                    mm.then_inc(cross[g], 1)
            for g in range(2):
                pe.wait_ge(kept[g], 11)
                for n in range(4 * g, 4 * g + 4):
                    c = slice((n % 4) * P, (n % 4 + 1) * P)
                    pe.matmul(yp[g][:, c], h["ti"][:, n, :], h["vb"][:, n, :], start=True, stop=True)
                    mm = pe.matmul(dp[g][:, c], h["kb"][:, n, :], h["ti"][:, n, :], start=True, stop=True)
                mm.then_inc(s["solved"], 1)

        @block.vector
        def _(dve):
            for g in range(2):
                pr = slice(4 * g, 4 * g + 4)
                dve.tensor_copy(b["t"][:, pr, :], ident).then_inc(s["begun"], 1)
                dve.tensor_copy(h["ti"][:, pr, :], ident).then_inc(s["begun"], 1)
            dve.wait_ge(s["begun"], 4)
            for lv in range(6):
                for g in range(2):
                    pr = slice(4 * g, 4 * g + 4)
                    dve.wait_ge(lower[g], lv + 1)
                    dve.tensor_tensor(b["y"][:, pr, :], yp[g][:, :].rearrange("p (n i) -> p n i", n=4),
                                      lev[:, lv:lv + 1, :].to_broadcast([P, 4, P]), ALU.mult).then_inc(masked[g], 1)
                for g in range(2):
                    pr = slice(4 * g, 4 * g + 4)
                    dve.wait_ge(cross[g], lv + 1)
                    if lv:
                        dve.wait_ge(kept[g], 2 * lv)
                    dve.tensor_tensor(h["ti"][:, pr, :], h["ti"][:, pr, :], cp[g][:, :].rearrange("p (n i) -> p n i", n=4),
                                      ALU.subtract).then_inc(kept[g], 1)
                    if lv < 5:
                        dve.tensor_tensor(b["t"][:, pr, :], b["t"][:, pr, :], dp[g][:, :].rearrange("p (n i) -> p n i", n=4),
                                          ALU.subtract).then_inc(kept[g], 1)
            for g in range(2):
                dve.wait_ge(s["solved"], g + 1)
                dve.tensor_copy(h["u"][:, 4 * g:4 * g + 4, :], yp[g][:, :].rearrange("p (n i) -> p n i", n=4))

        @block.scalar
        def _(act):
            for g in range(2):
                act.wait_ge(s["solved"], g + 1)
                act.activation(h["w"][:, 4 * g:4 * g + 4, :], dp[g][:, :].rearrange("p (n i) -> p n i", n=4), ACT.Copy)


def delta_scan_phase(nc, K, prm, hf, h, z, o_dn, ring, layer):
    with phase(nc, "zeroed ws vnew out state kept squared plus_eps rooted normed turned dve_step",
               [("st", [P, 4, P]), ("vn", [P, 4, P]), ("sq", [P, NP, P]), ("ms", [P, NP])],
               [("w_ps", HALF), ("o_ps", HALF), ("k_ps", HALF), ("t0", HALF), ("t1", HALF)]) as (block, s, b):
        tp = [b["t0"], b["t1"]]
        o = h["u"]

        @block.sync
        def _(sp):
            ring.send(sp, layer)

        @block.tensor
        def _(pe):
            for c in range(NCH):
                tt, r = c // 2, slice((c % 2) * CH, (c % 2 + 1) * CH)
                pe.wait_ge(s["state"], 4 * c + 1)
                for hh in range(4):
                    mm = pe.matmul(b["w_ps"][r, hh * P:(hh + 1) * P], h["w"][:, tt * 4 + hh, r], b["st"][:, hh, :],
                                   start=True, stop=True)
                mm.then_inc(s["ws"], 1)
                pe.wait_ge(s["vnew"], c + 1)
                if c:
                    pe.wait_ge(s["kept"], c)
                for hh in range(4):
                    n = tt * 4 + hh
                    mm = pe.matmul(b["k_ps"][:, hh * P:(hh + 1) * P], h["kd"][r, n, :], b["vn"][r, hh, :], start=True, stop=True)
                mm.then_inc(s["out"], 1)
                for hh in range(4):
                    n = tt * 4 + hh
                    cols = slice(hh * P, (hh + 1) * P)
                    pe.matmul(b["o_ps"][r, cols], h["qd"][:, hh, c * CH:(c + 1) * CH], b["st"][:, hh, :], start=True, stop=False)
                    mm = pe.matmul(b["o_ps"][r, cols], h["at"][r, n, r], b["vn"][r, hh, :], start=False, stop=True)
                mm.then_inc(s["out"], 1)
            for tt in range(TT):
                pe.wait_ge(s["normed"], 1)
                for hh in range(4):
                    mm = pe.transpose(tp[tt][:, hh * P:(hh + 1) * P], b["sq"][:, tt * 4 + hh, :], K("ident"))
                mm.then_inc(s["turned"], 1)

        @block.vector
        def _(dve):
            chain = Chain(dve, s["dve_step"])
            dve.memset(b["st"][:, :, :], 0.0).then_inc(s["state"], 1)
            for c in range(NCH):
                tt, r = c // 2, slice((c % 2) * CH, (c % 2 + 1) * CH)
                dve.wait_ge(s["ws"], c + 1)
                dve.tensor_tensor(b["vn"][r, :, :], h["u"][r, tt * 4:tt * 4 + 4, :],
                                  b["w_ps"][r, :].rearrange("p (h d) -> p h d", h=4), ALU.subtract).then_inc(s["vnew"], 1)
                if c + 1 < NCH:
                    dve.wait_ge(s["out"], 2 * c + 2)
                    dve.wait_ge(s["state"], 4 * c + 1)
                    for hh in range(4):
                        at = (c + 1) * CH - 1
                        dve.scalar_tensor_tensor(b["st"][:, hh, :], b["st"][:, hh, :], h["ge"][:, hh, at:at + 1],
                                                 b["k_ps"][:, hh * P:(hh + 1) * P], ALU.mult, ALU.add).then_inc(s["state"], 1)
            dve.wait_ge(s["squared"], 1)
            chain.step(dve.tensor_reduce(b["ms"][:, :], b["sq"][:, :, :], AX_X, ALU.add))
            dve.tensor_scalar(b["ms"][:, :], b["ms"][:, :], 1.0 / P, NORM_EPS, ALU.mult, ALU.add).then_inc(s["plus_eps"], 1)
            dve.wait_ge(s["rooted"], 1)
            chain.step(dve.reciprocal(b["ms"][:, :], b["ms"][:, :]))
            dve.tensor_tensor(b["sq"][:, :, :], o[:, :, :], b["ms"][:, :].unsqueeze(2).to_broadcast([P, NP, P]),
                              ALU.mult).then_inc(s["normed"], 1)
            for tt in range(TT):
                dve.wait_ge(s["turned"], tt + 1)
                c = slice(tt * P, (tt + 1) * P)
                dve.scalar_tensor_tensor(o_dn[:, 4 * hf:4 * hf + 4, c], tp[tt][:, :].rearrange("p (h t) -> p h t", h=4),
                                         prm("dn_norm"), z[:, 4 * hf:4 * hf + 4, c], ALU.mult, ALU.mult)

        @block.scalar
        def _(act):
            for c in range(NCH):
                tt, r = c // 2, slice((c % 2) * CH, (c % 2 + 1) * CH)
                act.wait_ge(s["out"], 2 * c + 2)
                act.activation(o[r, tt * 4:tt * 4 + 4, :], b["o_ps"][r, :].rearrange("p (h d) -> p h d", h=4),
                               ACT.Copy).then_inc(s["kept"], 1)
            act.wait_ge(s["kept"], NCH)
            act.activation(b["sq"][:, :, :], o[:, :, :], ACT.Square).then_inc(s["squared"], 1)
            act.wait_ge(s["plus_eps"], 1)
            act.activation(b["ms"][:, :], b["ms"][:, :], ACT.Sqrt).then_inc(s["rooted"], 1)


def index_phase(nc, K, iq, ik, tokq, masks, ring, layer):
    with phase(nc, "scored0 scored1 relued summed masked max8 dve_step",
               [("r", [P, 2, 8, T]), ("sc", [P, T]), ("wk", [P, T]), ("m8", [P, 8])],
               [("a0", 2 * HALF), ("b0", 2 * HALF), ("a1", 2 * HALF), ("b1", 2 * HALF)]) as (block, s, b):
        ps = [[b["a0"], b["b0"]], [b["a1"], b["b1"]]]
        scored = [s["scored0"], s["scored1"]]

        @block.sync
        def _(sp):
            ring.send(sp, layer)

        @block.tensor
        def _(pe):
            for qt in range(TT):
                nk = (qt + 1) * P
                for h in range(8):
                    r = slice((h % 2) * 64, (h % 2 + 1) * 64)
                    mm = pe.matmul(ps[qt][h % 2][:, (h // 2) * T:(h // 2) * T + nk], iq[r, h // 2, qt * P:(qt + 1) * P],
                                   ik[r, 0:nk], start=True, stop=True)
                mm.then_inc(scored[qt], 1)

        @block.scalar
        def _(act):
            for qt in range(TT):
                nk = (qt + 1) * P
                act.wait_ge(scored[qt], 1)
                for half in range(2):
                    act.activation(b["r"][:, qt, 4 * half:4 * half + 4, 0:nk],
                                   ps[qt][half][:, :].rearrange("p (h k) -> p h k", h=4)[:, :, 0:nk],
                                   ACT.Relu).then_inc(s["relued"], 1)

        @block.vector
        def _(dve):
            chain = Chain(dve, s["dve_step"])
            for qt in range(TT):
                nk = (qt + 1) * P
                sc, wk = b["sc"][:, 0:nk], b["wk"][:, 0:nk]
                dve.wait_ge(s["relued"], 2 * qt + 2)
                mask = K("chunk_causal").rearrange("p (q k) -> p q k", q=2)[:, qt, 0:nk]
                for h in range(8):
                    at = (h % 2) * 4 + h // 2
                    chain.step(dve.scalar_tensor_tensor(sc, b["r"][:, qt, at, 0:nk], tokq[:, qt, 4, h:h + 1],
                                                        mask if h == 0 else sc, ALU.mult, ALU.add))
                for i in range(TOPK // 8):
                    src = sc if i == 0 else wk
                    chain.step(dve.max(b["m8"][:, :], src))
                    chain.step(dve.match_replace(wk, b["m8"][:, :], src, TAKEN))
                chain.step(dve.tensor_scalar(wk, wk, TAKEN / 2, 1.0, ALU.is_le, ALU.subtract))
                dve.tensor_scalar(masks[:, qt, 0:nk], wk, -NEG, None, ALU.mult)


def second_layer(nc, K, layer, x, hT, mem_dram, ring, par_dram, tables):
    with ExitStack() as ctx:
        def sb(stack, name, shape):
            return stack.enter_context(nc.sbuf_tensor(name, shape, F32))

        par = sb(ctx, "par2_sb", [P, NPC2])
        prm = lambda name: par[:, PC2[name]]
        o_dn = sb(ctx, "o_dn", [P, KD, T])[:, :, :]
        tokq = sb(ctx, "tokq", [P, TT, QTY, 8])[:, :, :, :]
        ik = sb(ctx, "ik", [P, T])[:, :]
        copy = (ACT.Copy, None)
        with phase(nc, "params") as (block, s, b):
            @block.sync
            def _(sp):
                sp.dma_start(par[:, :], par_dram[bass.ds(layer, 1), :, :].rearrange("o p n -> (o p) n")
                             ).then_inc(s["params"], 16)
                ring.send(sp, layer)
                sp.wait_ge(s["params"], 16)

        norm_phase(nc, K, x, hT, prm("norm_mix"), None, NORM_EPS, True, ring=ring, layer=layer)

        with ExitStack() as st:
            q, k, v, z = (sb(st, n, [P, KD, T])[:, :, :] for n in ("dq", "dk", "dv", "dz"))
            small, rowq, ge = sb(st, "small", [8, 3, T]), sb(st, "rowq", [8, QTY, T])[:, :, :], sb(st, "ge_row", [8, T])[:, :]
            wsm = {"small": prm("w_small").rearrange("p (k c) -> p k c", k=KD)}
            taps = prm("conv_w").rearrange("p (j c) -> p j c", j=4)
            units = [U("small", 0, "rows", small[:, 0:2, :], (8, 2)), U("small", 16, "rows", small[:, 2:3, :], (8, 1)),
                     U("small", 24, "tile", ik)]
            for n in range(12):
                dst = (q, k, v)[n // 4][:, 2 * (n % 4):2 * (n % 4) + 2, :]
                units.append(U(f"dn{n // 2}", (n % 2) * 256, "conv", dst, (4, taps, None, 2 * n, "silu")))
            units += [U(f"dn{6 + n // 2}", (n % 2) * 256, "act", z[:, 2 * n:2 * n + 2, :], (ACT.Silu, None))
                      for n in range(4)]
            product_phase(nc, ring, layer, units, hT, wsm)
            decay_phase(nc, K, prm, small, ge, rowq, tokq, ring, layer)
            unit_keys_phase(nc, K, q, k, NORM_EPS, ring, layer)
            for hf in range(2):
                with ExitStack() as half:
                    h = {}
                    for n in ("kb", "kd", "vb", "at", "mt", "ti", "u", "w"):
                        h[n] = sb(half, f"{n}_{hf}", [P, NP, P])[:, :, :]
                    h["qd"], h["ge"] = (sb(half, f"{n}_{hf}", [P, 4, T])[:, :, :] for n in ("qd", "ge"))
                    delta_prepare_phase(nc, K, hf, q, k, v, ge, rowq, tokq, h, ring, layer)
                    delta_solve_phase(nc, K, h, ring, layer)
                    delta_scan_phase(nc, K, prm, hf, h, z, o_dn, ring, layer)

        o_sa, o_xa = (sb(ctx, n, [P, KD, T])[:, :, :] for n in ("o_sa", "o_xa"))

        with ExitStack() as st:
            sq, sk = sb(st, "sq_", [P, KD, T])[:, :, :], sb(st, "sk_", [P, KD, T])[:, :, :]
            sv, iq = sb(st, "sv_", [P, TT, D])[:, :, :], sb(st, "iq_", [P, 4, T])[:, :, :]
            masks = sb(st, "masks", [P, TT, T])[:, :, :]
            units = [U(f"sa{n // 2}", (n % 2) * 256, "act", (sq, sk)[n // 4][:, 2 * (n % 4):2 * (n % 4) + 2, :], copy)
                     for n in range(8)]
            units += [U(f"sa{4 + n // 2}", (n % 2) * 256, "act", sv[:, :, n * 256:(n + 1) * 256], copy, tokens=True)
                      for n in range(4)]
            units += [U("iq", n * 256, "act", iq[:, 2 * n:2 * n + 2, :], copy) for n in range(2)]
            product_phase(nc, ring, layer, units, hT)
            cs128, sn128 = tables[:, 0, :], tables[:, 2, :]
            cs64, sn64 = tables[:, 1, :], tables[:, 3, :]
            rope_phase(nc, K, [(t[:, 2 * i:2 * i + 2, :], K("perm128"), cs128, sn128) for t in (sq, sk) for i in range(4)]
                       + [(iq[:, 2 * i:2 * i + 2, :], K("perm64"), cs64, sn64) for i in range(2)]
                       + [(ik.unsqueeze(1), K("perm64"), cs64, sn64)], ring, layer)
            index_phase(nc, K, iq, ik, tokq, masks, ring, layer)

            def group(h0, qt):
                nk, c = (qt + 1) * P, slice(qt * P, (qt + 1) * P)
                return Group(
                    nk=nk, scale=128 ** -0.5, slot=lambda h: h, mask=masks[:, qt:qt + 1, 0:nk],
                    pairs=lambda h: [(sq[:, h0 + h, c], sk[:, h0 + h, 0:nk])],
                    value=lambda h, kt: [sv[:, kt, (h0 + h) * P:(h0 + h + 1) * P]],
                    place=lambda o, h: [o[:, h * P:(h + 1) * P]],
                    dst=lambda o: [(o[:, 0:HALF].rearrange("p (i q) -> p i q", i=4), o_sa[:, h0:h0 + 4, c])])

            attention_phase(nc, K, [group(h0, qt) for h0 in (0, 4) for qt in range(TT)], ring, layer)

        with ExitStack() as st:
            mem = sb(st, "mem_sb", [P, KD, T])[:, :, :]
            with phase(nc, "memory") as (block, s, b):
                @block.sync
                def _(sp):
                    sp.dma_start(mem, mem_dram).then_inc(s["memory"], 16)
                    sp.wait_ge(s["memory"], 16)
            mn, mk, xq = (sb(st, n, [P, KD, T])[:, :, :] for n in ("mem_n", "mk", "xq"))
            mv = sb(st, "mv_", [P, TT, D])[:, :, :]
            norm_phase(nc, K, mem, mn, prm("norm_mem"), None, NORM_EPS, True, ring=ring, layer=layer)
            units = [U(f"kv{n // 2}", (n % 2) * 256, "act", mk[:, 2 * n:2 * n + 2, :], copy, x=mn) for n in range(4)]
            units += [U(f"kv{2 + n // 2}", (n % 2) * 256, "act", mv[:, :, n * 256:(n + 1) * 256], copy, x=mn, tokens=True)
                      for n in range(4)]
            units += [U(f"xq{n // 2}", (n % 2) * 256, "act", xq[:, 2 * n:2 * n + 2, :], copy) for n in range(4)]
            product_phase(nc, ring, layer, units, hT)

            def group(qt):
                c = slice(qt * P, (qt + 1) * P)
                return Group(
                    nk=T, scale=256 ** -0.5, slot=lambda h: h, mask=None,
                    pairs=lambda h: [(xq[:, 2 * h + i, c], mk[:, 2 * h + i, :]) for i in range(2)],
                    value=lambda h, kt: [mv[:, kt, (2 * h + i) * P:(2 * h + i + 1) * P] for i in range(2)],
                    place=lambda o, h: [o[:, (2 * h + i) * P:(2 * h + i + 1) * P] for i in range(2)],
                    dst=lambda o: [(o[:, :].rearrange("p (i q) -> p i q", i=8), o_xa[:, :, c])])

            attention_phase(nc, K, [group(qt) for qt in range(TT)], ring, layer)

        with ExitStack() as st:
            merged = sb(st, "merged", [P, KD, T])[:, :, :]
            gates = sb(st, "gates", [P, 2, 3, 4, T])
            units = []
            bg = prm("b_gate")
            for c in range(2):
                pair = [merged[:, 4 * c + 2 * u:4 * c + 2 * u + 2, :] for u in range(2)]
                for i, o in enumerate((o_dn, o_sa, o_xa)):
                    g = [gates[:, c, i, 2 * u:2 * u + 2, :] for u in range(2)]
                    at = 8 * i + 4 * c
                    units += [U(f"gl{i}{c}", u * 256, "act", g[u],
                                (ACT.Sigmoid, bg[:, at + 2 * u:at + 2 * u + 2])) for u in range(2)]
                    units += [U(f"wb{i}{c}", u * 256, "gate_add" if i else "gate_first", pair[u], g[u], x=o)
                              for u in range(2)]
            product_phase(nc, ring, layer, units, hT)
            product_phase(nc, ring, layer, [U(f"out{i // 2}", (i % 2) * 256, "residual", x[:, 2 * i:2 * i + 2, :], 1.0)
                                            for i in range(4)], merged)

        norm_phase(nc, K, x, hT, prm("norm_ffn"), None, NORM_EPS, True, ring=ring, layer=layer)
        with nc.sbuf_tensor("hid2", [P, KF, T], F32) as hid:
            hv = [hid[:, 2 * i:2 * i + 2, :] for i in range(KF // 2)]
            product_phase(nc, ring, layer,
                          [U(f"fin{i // 2}", (i % 2) * 256, "act" if i < 11 else "times", hv[i % 11], (ACT.Silu, None))
                           for i in range(KF)], hT)
            down_phase(nc, ring, layer, [f"fout{i}" for i in range(6)], hid, x, 1.0)
        ring.clear(nc)


def build(nc, a, out_dram):
    with ExitStack() as ctx:
        const = ctx.enter_context(nc.sbuf_tensor("const_sb", [P, NCC], F32))
        x = ctx.enter_context(nc.sbuf_tensor("x_sb", [P, KD, T], F32))[:, :, :]
        K = lambda name: const[:, CC[name]]
        with phase(nc, "begin") as (block, s, b):
            @block.sync
            def _(sp):
                sp.dma_start(const[:, :], a["const"]).then_inc(s["begin"], 16)
                sp.dma_start(x, a["xT"]).then_inc(s["begin"], 16)
                sp.wait_ge(s["begin"], 32)
        if "w1" in a:
            with ExitStack() as first:
                ring = Ring(nc, first, "w1", CHUNKS_1, a["w1"])
                with nc.Fori(0, DEPTH) as layer:
                    first_layer(nc, K, layer, x, ring, a["par1"], a["rows1"])
        gain = ctx.enter_context(nc.sbuf_tensor("final_gain", [P, D], F32))
        with ExitStack() as second:
            def sb(name, shape):
                return second.enter_context(nc.sbuf_tensor(name, shape, F32))

            ring = Ring(nc, second, "w2", CHUNKS_2, a["w2"])
            hT, tables = sb("hT", [P, KD, T])[:, :, :], sb("tables", [P, 4, T])[:, :, :]
            with phase(nc, "begin") as (block, s, b):
                @block.sync
                def _(sp):
                    sp.dma_start(gain[:, :], a["norm_final"].to_broadcast([P, D])).then_inc(s["begin"], 16)
                    sp.wait_ge(s["begin"], 16)
            angle_phase(nc, K, a["positions"], tables)
            with nc.Fori(0, DEPTH) as layer:
                second_layer(nc, K, layer, x, hT, a["memT"], ring, a["par2"], tables)
        norm_phase(nc, K, x, None, gain[:, :], None, NORM_EPS, True, out=out_dram)


def lay_second(i):
    w = i["w_in_2"]
    at = dict(zip("dq dk dv dz db da sq sk sv iq ik iw xq gl".split(),
                  np.cumsum([0, D, D, D, D, 8, 8, D, D, D, 512, 64, 8, D]).tolist()))
    wb = i["w_branch_2"].reshape(DEPTH, 3 * D, D)
    parts = ([(w, 0, 512 * n) for n in range(8)] + [(w, 0, at["sq"] + 512 * n) for n in range(6)] + [(w, 0, at["iq"])]
             + [(i["w_mem_kv_2"], 0, 512 * n) for n in range(4)] + [(w, 0, at["xq"] + 512 * n) for n in range(2)]
             + [p for c in range(2) for b in range(3) for p in ((w, 0, at["gl"] + D * b + 512 * c), (wb, D * b, 512 * c))]
             + [(i["w_out_2"], 0, 512 * n) for n in range(2)] + [(i["w_ffn_in_2"], 0, 512 * n) for n in range(11)]
             + [(i["w_ffn_out_2"], 512 * n, 0) for n in range(6)])
    par = np.zeros((DEPTH, P, NPC2), np.float32)
    for name in ("norm_mix", "norm_mem", "norm_ffn", "b_gate", "conv_w", "dn_norm"):
        par[:, :, PC2[name]] = i[name + "_2"].reshape(DEPTH, -1, P).transpose(0, 2, 1)
    for name in ("a_log", "dt_bias"):
        par[:, 0:8, PC2[name]] = i[name + "_2"][:, :, None]
    db, iw, ik = (w[:, :, c:c + n] for c, n in ((at["db"], 16), (at["iw"], 8), (at["ik"], 64)))
    sm = np.concatenate([db, iw, ik, ik], axis=2)
    par[:, :, PC2["w_small"]] = sm.reshape(DEPTH, KD, P, 152).transpose(0, 2, 1, 3).reshape(DEPTH, P, -1)
    return chunked(parts, CHUNKS_2), par


def kernel(**inputs):
    import concourse.bacc as bacc
    from concourse.bass_utils import run_bass_kernel_spmd as run

    i = {name: np.asarray(v) for name, v in inputs.items()}
    w1, par1, rows1 = lay_first(i)
    w2, par2 = lay_second(i)
    arrays = {"xT": tiles_of(i["x"][0]), "w1": w1, "par1": par1, "rows1": rows1, "w2": w2, "par2": par2,
              "memT": tiles_of(i["mem_2"][0]), "positions": i["positions_2"],
              "norm_final": i["norm_final_2"].reshape(1, D), "const": constants()}
    nc = bacc.Bacc("TRN2", target_bir_lowering=False, num_devices=1)
    dram = {n: nc.dram_tensor(n, v.shape, mybir.dt.from_np(v.dtype), kind="ExternalInput").ap() for n, v in arrays.items()}
    out = nc.dram_tensor("out", (T, D), F32, kind="ExternalOutput").ap()
    build(nc, dram, out)
    r = run(nc, [arrays], core_ids=[0])
    return r.results[0]["out"].reshape(1, T, D)
```

```python
from contextlib import ExitStack, contextmanager

import numpy as np

import concourse.bass as bass
from concourse import mybir

F32 = mybir.dt.float32
F32R = mybir.dt.float32r
I32 = mybir.dt.int32
ALU = mybir.AluOpType
ACT = mybir.ActivationFunctionType
AX_X = mybir.AxisListType.X

P = 128
T = 256
TT = T // P
D = 1024
KD = D // P
DEPTH = 2
FF = 2816
KF = FF // P
HALF = 512
NEG = -1.0e30
TAKEN = -3.0e38
ALPHA = (2 * DEPTH) ** 0.25
LN_EPS = 1e-5
NORM_EPS = 1e-6
CH = 64
NCH = T // CH
TOPK = T // 4
WINDOWS = (2, 4, 8, 16)
THETA = 500000.0
IDX_SCALE = 8 ** -0.5 * 64 ** -0.5
SLOTS = 3
SPLIT_SLOTS = 2
CHUNK_W = 8 * 256
DVE_PART = 5 * 256


CHUNKS_1 = ([f"in{i}" for i in range(6)] + ["gate_row"] + [f"in{i}" for i in range(6, 9)]
            + [f"o{i}" for i in range(4)] + [f"up{i}" for i in range(22)] + [f"down{i}" for i in range(11)])
CHUNKS_2 = (["small"] + [f"dn{i}" for i in range(16)] + [f"sa{i}" for i in range(12)] + ["iq0", "iq1"]
            + [f"kv{i}" for i in range(8)] + [f"xq{i}" for i in range(4)]
            + [f"{b}{i}_{2 * c + u}" for c in range(2) for i in range(3) for b in ("gl", "wb") for u in range(2)]
            + [f"out{i}" for i in range(4)] + [f"fin{i}" for i in range(22)] + [f"fout{i}" for i in range(11)])


def columns_of(name):
    return (2, D) if name.startswith(("down", "fout")) else (KD, P) if name == "gate_row" else (KD, 256)


def columns(spec):
    at, out = 0, {}
    for name, n in spec:
        out[name] = slice(at, at + n)
        at += n
    return out, at


PC1, NPC1 = columns([("ln1_g", 8), ("ln1_b", 8), ("ln2_g", 8), ("ln2_b", 8), ("conv_w", 3 * 44), ("conv_b", 44),
                     ("pool_scale", 2), ("b_forget", 1), ("sgu_wT", 4 * 128), ("sgu_b", 4 * 128), ("pool_w", 2 * 64)])
PC2, NPC2 = columns([("norm_mix", 8), ("norm_mem", 8), ("norm_ffn", 8), ("b_gate", 24), ("conv_w", 4 * 24),
                     ("dn_norm", 1), ("a_log", 1), ("dt_bias", 1)])
CC, NCC = columns([("ident", 128), ("ones", 128), ("perm64", 128), ("select", 8 * 128), ("eps", 1),
                   ("chunk_causal", 2 * 256), ("perm128", 128), ("freq", 2), ("levels", 6 * 128), ("upper", 128),
                   ("strict", 128),
                   ("causal", 2 * 256), ("band", 2 * 4 * 256), ("cos", 256), ("sin", 256)])
NCC2 = CC["causal"].start


def constants():
    c = np.zeros((P, NCC), np.float32)
    p = np.arange(P)
    t = np.arange(T)

    def put(name, a):
        c[:a.shape[0], CC[name]] = a.reshape(a.shape[0], -1)

    put("ident", np.eye(P))
    put("eps", np.full((P, 1), NORM_EPS))
    put("ones", np.ones((P, P)))
    q = p[:, None] + P * np.arange(TT)[None, :]
    put("causal", np.where(t[None, None, :] <= q[:, :, None], 0.0, NEG))
    put("chunk_causal", np.where(t[None, None, :] // CH <= q[:, :, None] // CH, 0.0, NEG))
    s = q[:, :, None, None]
    win = np.array(WINDOWS)[None, None, :, None]
    at = t[None, None, None, :]
    inside = (s <= at) & (s > at - win)
    put("band", inside / np.minimum(at + 1, win) - (s == at))
    half = 8
    inv = (np.float64(THETA) ** (-np.arange(0, 16, 2) / 16)).astype(np.float32)
    ang = t[None, :].astype(np.float32) * inv[p % half][:, None]
    roped = ((p % 64) < 16)[:, None]
    put("cos", np.where(roped, np.cos(ang), 1.0))
    put("sin", np.where(roped, np.sin(ang), 0.0))
    for name, dim, h in (("perm64", 64, 8), ("perm128", 128, 16)):
        m = np.zeros((P, P))
        for d in range(P):
            if d % dim < h:
                m[d + h, d] = -1.0
            elif d % dim < 2 * h:
                m[d - h, d] = 1.0
        put(name, m)
    f = np.zeros((P, 2))
    inv128 = (np.float64(THETA) ** (-np.arange(16) * 2.0 / 32)).astype(np.float32)
    inv64 = (np.float64(THETA) ** (-np.arange(8) * 2.0 / 16)).astype(np.float32)
    f[:32, 0] = inv128[p[:32] % 16]
    f[:, 1] = np.where(p % 64 < 16, inv64[p % 8], 0.0)
    put("freq", f)
    i, j = p[:, None], p[None, :]
    lev = [((i // (2 * b) == j // (2 * b)) & (i // b > j // b)) for b in (1, 2, 4, 8, 16, 32)]
    put("levels", np.stack(lev, 1).astype(np.float64))
    same = i // CH == j // CH
    put("upper", (same & (j >= i)).astype(np.float64))
    put("strict", (same & (j > i)).astype(np.float64))
    sel = np.zeros((8, 8, P))
    sel[np.arange(8), np.arange(8)] = 1.0
    put("select", sel)
    return c


PHASES = []


@contextmanager
def phase(nc, names, tensors=(), banks=()):
    with ExitStack() as ctx:
        at = len(PHASES)
        PHASES.append(names)
        handles = [ctx.enter_context(nc.semaphore(n)) for n in names.split()]
        s = {n: h for n, h in zip(names.split(), handles)}
        b = {}
        for name, shape in tensors:
            b[name] = ctx.enter_context(nc.sbuf_tensor(f"{name}_{at}", shape, F32))
        for name, width in banks:
            b[name] = ctx.enter_context(nc.psum_tensor(f"{name}_{at}", [P, width], F32))
        with nc.Block() as block:
            yield block, s, b
        for h in handles:
            nc.gpsimd.sem_clear(h)
        nc.all_engine_barrier()


class Chain:

    def __init__(self, eng, sem):
        self.eng, self.sem, self.n = eng, sem, 0

    def step(self, ins):
        self.n += 1
        ins.then_inc(self.sem, 1)
        self.eng.wait_ge(self.sem, self.n)


class Ring:

    def __init__(self, nc, ctx, name, chunks, dram):
        def sb(part, n, dt):
            return ctx.enter_context(nc.sbuf_tensor(f"{name}_{part}", [P, n, CHUNK_W], dt))

        self.raw, self.hi, self.lo = sb("raw", SLOTS, F32), sb("hi", SPLIT_SLOTS, F32R), sb("lo", SPLIT_SLOTS, F32R)
        self.loaded = [ctx.enter_context(nc.semaphore(f"{name}_loaded{i}")) for i in range(SLOTS)]
        self.high, self.low_dve, self.low_pool, self.product = (
            ctx.enter_context(nc.semaphore(f"{name}_{n}")) for n in ("high", "low_dve", "low_pool", "product"))
        self.names, self.dram = chunks, dram
        self.width = [k * c for k, c in (columns_of(n) for n in chunks)]
        self.start()

    def start(self):
        self.sent, self.units, self.split = 0, 0, 0

    def plan(self, names):
        base = self.units
        assert self.names[base:base + len(names)] == names, (self.names[base:base + len(names)], names)
        self.units += len(names)
        todo = range(self.split, min(self.units + 1, len(self.names)))
        self.split = todo.stop
        return base, todo

    def send(self, sp, layer):
        upto = min(self.split + SLOTS, len(self.names))
        for n in range(self.sent, upto):
            at = sum(self.width[:n])
            if n >= SLOTS:
                sp.wait_ge(self.low_dve, n - SLOTS + 1)
                sp.wait_ge(self.low_pool, n - SLOTS + 1)
            sp.dma_start(self.raw[:, n % SLOTS, 0:self.width[n]],
                         self.dram[bass.ds(layer, 1), :, at:at + self.width[n]].rearrange("o p n -> (o p) n")
                         ).then_inc(self.loaded[n % SLOTS], 16)
        self.sent = upto

    def split_high(self, act, n):
        w = self.width[n]
        act.wait_ge(self.loaded[n % SLOTS], 16 * (n // SLOTS + 1))
        if n >= SPLIT_SLOTS:
            act.wait_ge(self.product, n - SPLIT_SLOTS + 1)
        act.activation(self.hi[:, n % SPLIT_SLOTS, 0:w], self.raw[:, n % SLOTS, 0:w], ACT.Copy).then_inc(self.high, 1)

    def split_low(self, eng, n):
        dve = eng.engine == mybir.EngineType.DVE
        mid = self.width[n] * DVE_PART // CHUNK_W
        c = slice(0, mid) if dve else slice(mid, self.width[n])
        eng.wait_ge(self.high, n + 1)
        eng.tensor_tensor(self.lo[:, n % SPLIT_SLOTS, c], self.raw[:, n % SLOTS, c],
                          self.hi[:, n % SPLIT_SLOTS, c].bitcast(F32), ALU.subtract
                          ).then_inc(self.low_dve if dve else self.low_pool, 1)

    def arrive(self, pe, n):
        pe.wait_ge(self.low_dve, n + 1)
        pe.wait_ge(self.low_pool, n + 1)
        k, c = columns_of(self.names[n])
        return [part[:, n % SPLIT_SLOTS, 0:k * c].rearrange("p (k c) -> p k c", k=k) for part in (self.hi, self.lo)]

    def clear(self, nc):
        assert self.sent == self.units == self.split == len(self.names)
        for sem in [*self.loaded, self.high, self.low_dve, self.low_pool, self.product]:
            nc.gpsimd.sem_clear(sem)
        nc.all_engine_barrier()
        self.start()


def passes(pe, out, lhs, rhs, start, stop, skip=False):
    pe.matmul(out, lhs[0], rhs[0], start=start, stop=False, skip_group_check=skip)
    pe.matmul(out, lhs[0], rhs[1], start=False, stop=False, skip_group_check=skip)
    return pe.matmul(out, lhs[1], rhs[0], start=False, stop=stop, skip_group_check=skip)


def unit_product(pe, bank, w, x, token_major=False):
    kt, cols = w[0].shape[1], w[0].shape[2]
    for i in range(2 if token_major else cols // P):
        for k in range(kt):
            if token_major:
                lhs, rhs = [v[:, k, i * P:(i + 1) * P] for v in x], [v[:, k, :] for v in w]
            else:
                lhs, rhs = [v[:, k, i * P:(i + 1) * P] for v in w], [v[:, k, :] for v in x]
            mm = passes(pe, bank[:, i * 256:(i + 1) * 256], lhs, rhs, k == 0, k == kt - 1)
    return mm


def norm_phase(nc, K, src, dst, gain, bias, eps, rms, pair=None, out=None, ring=None, layer=None):
    with phase(nc, "turned stats rooted scaled back stored high dve_step",
               [("xn", [P, TT, D]), ("bn", [P, TT, 2, 6]), ("mv", [P, TT, 2]), ("ms", [P, TT]), ("sd", [P, TT]),
                ("rs", [P, TT])],
               [("tok0", D), ("tok1", D)] + [(f"bk{i}", HALF) for i in range(4)]) as (block, s, b):
        tok = [b["tok0"], b["tok1"]]
        bk = [b["bk0"], b["bk1"], b["bk2"], b["bk3"]]

        @block.sync
        def _(sp):
            if ring is not None:
                ring.send(sp, layer)
            if out is not None:
                for tt in range(TT):
                    sp.wait_ge(s["stored"], tt + 1)
                    sp.dma_start(out[tt * P:(tt + 1) * P, :], b["xn"][:, tt, :]).then_inc(s["back"], 16)
                sp.wait_ge(s["back"], 16 * TT)

        @block.tensor
        def _(pe):
            for tt in range(TT):
                for k in range(KD):
                    mm = pe.transpose(tok[tt][:, k * P:(k + 1) * P], src[:, k, tt * P:(tt + 1) * P], K("ident"))
                mm.then_inc(s["turned"], 1)
            if out is not None:
                return
            pe.wait_ge(s["scaled"], TT)
            for k in range(KD):
                for tt in range(TT):
                    mm = pe.transpose(bk[k // 2][:, (k % 2) * 256 + tt * P:(k % 2) * 256 + (tt + 1) * P],
                                      b["xn"][:, tt, k * P:(k + 1) * P], K("ident"))
                if k % 2:
                    mm.then_inc(s["back"], 1)

        @block.vector
        def _(dve):
            chain = Chain(dve, s["dve_step"])
            for tt in range(TT):
                dve.wait_ge(s["turned"], tt + 1)
                dve.bn_stats(b["bn"][:, tt, 0, :], tok[tt][:, 0:HALF])
                chain.step(dve.bn_stats(b["bn"][:, tt, 1, :], tok[tt][:, HALF:D]))
                chain.step(dve.bn_aggr(b["mv"][:, tt, :], b["bn"][:, tt, :, :]))
                if rms:
                    chain.step(dve.scalar_tensor_tensor(b["ms"][:, tt:tt + 1], b["mv"][:, tt, 0:1], b["mv"][:, tt, 0:1],
                                                        b["mv"][:, tt, 1:2], ALU.mult, ALU.add))
                    dve.tensor_scalar(b["ms"][:, tt:tt + 1], b["ms"][:, tt:tt + 1], eps, None, ALU.add).then_inc(s["stats"], 1)
                else:
                    dve.tensor_scalar(b["ms"][:, tt:tt + 1], b["mv"][:, tt, 1:2], eps, None, ALU.add).then_inc(s["stats"], 1)
            for tt in range(TT):
                dve.wait_ge(s["rooted"], tt + 1)
                chain.step(dve.reciprocal(b["rs"][:, tt:tt + 1], b["sd"][:, tt:tt + 1]))
                if rms:
                    ins = dve.tensor_scalar(b["xn"][:, tt, :], tok[tt][:, :], b["rs"][:, tt:tt + 1], None, ALU.mult)
                else:
                    ins = dve.tensor_scalar(b["xn"][:, tt, :], tok[tt][:, :], b["mv"][:, tt, 0:1], b["rs"][:, tt:tt + 1],
                                            ALU.subtract, ALU.mult)
                if out is None:
                    ins.then_inc(s["scaled"], 1)
                else:
                    chain.step(ins)
                    dve.tensor_tensor(b["xn"][:, tt, :], b["xn"][:, tt, :], gain, ALU.mult).then_inc(s["stored"], 1)
            if out is not None:
                return
            for i in (0, 1, 2, 3):
                ks = (2 * i, 2 * i + 1)
                v = bk[i][:, :].rearrange("p (i t) -> p i t", i=2)
                if dst is not None:
                    dve.wait_ge(s["back"], i + 1)
                    for j, k in enumerate(ks):
                        ins = dve.tensor_scalar(dst[:, k, :], v[:, j, :], gain[:, k:k + 1], bias[:, k:k + 1], ALU.mult, ALU.add)
                    ins.then_inc(s["stored"], 1)
                else:
                    dve.wait_ge(s["high"], i + 1)
                    for j, k in enumerate(ks):
                        dve.scalar_tensor_tensor(pair[1][:, k, :], v[:, j, :], gain[:, k:k + 1],
                                                 pair[0][:, k, :].bitcast(F32), ALU.mult, ALU.subtract)
            if dst is not None and pair is not None:
                for i in range(4):
                    dve.wait_ge(s["high"], i + 1)
                    c = slice(2 * i, 2 * i + 2)
                    dve.tensor_tensor(pair[1][:, c, :], dst[:, c, :], pair[0][:, c, :].bitcast(F32), ALU.subtract)

        @block.scalar
        def _(act):
            for tt in range(TT):
                act.wait_ge(s["stats"], tt + 1)
                act.activation(b["sd"][:, tt:tt + 1], b["ms"][:, tt:tt + 1], ACT.Sqrt).then_inc(s["rooted"], 1)
            if out is not None or pair is None:
                return
            for i in range(4):
                c = slice(2 * i, 2 * i + 2)
                if dst is not None:
                    act.wait_ge(s["stored"], i + 1)
                    ins = act.activation(pair[0][:, c, :], dst[:, c, :], ACT.Copy)
                else:
                    act.wait_ge(s["back"], i + 1)
                    for k in (2 * i, 2 * i + 1):
                        ins = act.activation(pair[0][:, k, :], bk[i][:, (k % 2) * 256:(k % 2) * 256 + 256], ACT.Copy,
                                             scale=gain[:, k:k + 1])
                ins.then_inc(s["high"], 1)


NB = 4


class U:

    def __init__(self, chunk, kind, dst, more=None, x=None, tokens=False, pair=None):
        self.chunk, self.kind, self.dst, self.more, self.x, self.tokens, self.pair = chunk, kind, dst, more, x, tokens, pair


def product_phase(nc, ring, layer, units, x, splits=()):
    base, todo = ring.plan([u.chunk for u in units])
    conv = [n for n, u in enumerate(units) if u.kind == "conv"]
    paired = [n for n, u in enumerate(units) if u.pair is not None]
    with phase(nc, "affine finished gated x_high x_low timed pair_high " + " ".join(f"free{i}" for i in range(NB)) + " dve_step",
               [("cb", [P, 2, 2, 256])] if conv else [],
               [(f"mm{i}", HALF) for i in range(NB)]) as (block, s, b):
        bank = [b[f"mm{i}"] for i in range(NB)]
        free = [s[f"free{i}"] for i in range(NB)]

        def view(n):
            return bank[n % NB][:, :].rearrange("p (i t) -> p i t", i=2)

        first = [c for c in todo if c <= base]
        after = [[c for c in todo if c == base + n + 1] for n in range(len(units))]

        @block.sync
        def _(sp):
            ring.send(sp, layer)

        def low(pool, n):
            u = units[n]
            pool.wait_ge(s["pair_high"], paired.index(n) + 1)
            pool.tensor_tensor(u.pair[1], u.dst, u.pair[0].bitcast(F32), ALU.subtract)

        @block.gpsimd
        def _(pool):
            for c in first:
                ring.split_low(pool, c)
            for n, u in enumerate(units):
                for c in after[n]:
                    ring.split_low(pool, c)
                if n - 1 in paired:
                    low(pool, n - 1)
            if len(units) - 1 in paired:
                low(pool, len(units) - 1)

        @block.tensor
        def _(pe):
            if splits:
                pe.wait_ge(s["x_low"], 1)
            for n, u in enumerate(units):
                if n >= NB:
                    pe.wait_ge(free[n % NB], n // NB)
                if splits and n == 2:
                    pe.wait_ge(s["x_low"], len(splits))
                w = ring.arrive(pe, base + n)
                unit_product(pe, bank[n % NB], w, x if u.x is None else u.x, u.tokens).then_inc(ring.product, 1)

        @block.scalar
        def _(act):
            def early(n):
                u = units[n]
                fr = free[n % NB]
                if u.kind in ("act", "rows", "conv"):
                    act.wait_ge(ring.product, base + n + 1)
                v = view(n)
                if u.kind == "rows":
                    for p0, count, dst in u.more:
                        ins = act.activation(dst, v[p0:p0 + count, 0, :], ACT.Copy)
                    if u.dst is not None:
                        ins = act.activation(u.dst, v[:, 1, :], ACT.Copy)
                    ins.then_inc(fr, 1)
                elif u.kind == "act":
                    func, bias = u.more
                    if bias is None:
                        act.activation(u.dst, v, func).then_inc(fr, 1)
                    else:
                        act.activation(u.dst[:, 0, :], v[:, 0, :], func, bias=bias[:, 0:1])
                        act.activation(u.dst[:, 1, :], v[:, 1, :], func, bias=bias[:, 1:2]).then_inc(fr, 1)
                elif u.kind == "conv":
                    taps, wts, bs, c0, finish = u.more
                    i = conv.index(n)
                    if i >= 2:
                        act.wait_ge(s["finished"], i - 1)
                    for j in range(2):
                        c = c0 + j
                        cb = b["cb"][:, i % 2, j, :]
                        if bs is None:
                            ins = act.activation(cb, v[:, j, :], ACT.Copy, scale=wts[:, taps - 1, c:c + 1])
                        else:
                            ins = act.activation(cb, v[:, j, :], ACT.Identity, scale=wts[:, taps - 1, c:c + 1],
                                                 bias=bs[:, c:c + 1])
                    ins.then_inc(s["affine"], 1)

            def late(n):
                u = units[n]
                if u.kind == "conv" and u.more[4] == "silu":
                    act.wait_ge(free[n % NB], n // NB + 1)
                    act.activation(u.dst, b["cb"][:, conv.index(n) % 2, :, :], ACT.Silu).then_inc(s["finished"], 1)
                if u.pair is not None:
                    act.wait_ge(s["timed"], paired.index(n) + 1)
                    act.activation(u.pair[0], u.dst, ACT.Copy).then_inc(s["pair_high"], 1)

            for src, pair in splits[:1]:
                act.activation(pair[0], src, ACT.Copy).then_inc(s["x_high"], 1)
            for c in first:
                ring.split_high(act, c)
            for n in range(len(units)):
                if n:
                    early(n - 1)
                for c in after[n]:
                    ring.split_high(act, c)
                if n == 0:
                    for src, pair in splits[1:]:
                        act.activation(pair[0], src, ACT.Copy).then_inc(s["x_high"], 1)
                if n:
                    late(n - 1)
            early(len(units) - 1)
            late(len(units) - 1)

        @block.vector
        def _(dve):
            chain = Chain(dve, s["dve_step"])

            def empty(n):
                u = units[n]
                fr = free[n % NB]
                v = view(n)
                if u.kind == "conv":
                    taps, wts, bs, c0, finish = u.more
                    i = conv.index(n)
                    dve.wait_ge(s["affine"], i + 1)
                    for tap in range(1, taps):
                        for j in range(2):
                            c = c0 + j
                            ins = dve.scalar_tensor_tensor(b["cb"][:, i % 2, j, tap:T], v[:, j, 0:T - tap],
                                                           wts[:, taps - 1 - tap, c:c + 1], b["cb"][:, i % 2, j, tap:T],
                                                           ALU.mult, ALU.add)
                        if tap < taps - 1:
                            chain.step(ins)
                        else:
                            ins.then_inc(fr, 1)
                    if finish == "times":
                        dve.wait_ge(fr, n // NB + 1)
                        dve.wait_ge(s["finished"], i)
                        dve.tensor_tensor(u.dst, u.dst, b["cb"][:, i % 2, :, :], ALU.mult).then_inc(s["finished"], 1)
                        if u.pair is not None:
                            dve.wait_ge(s["finished"], i + 1)
                            dve.sem_inc(s["timed"], 1)
                elif u.kind == "times":
                    dve.wait_ge(ring.product, base + n + 1)
                    gate = next(m for m in range(n) if units[m].dst is u.dst)
                    dve.wait_ge(free[gate % NB], gate // NB + 1)
                    dve.tensor_tensor(u.dst, u.dst, v, ALU.mult).then_inc(fr, 1)
                    if u.pair is not None:
                        dve.wait_ge(fr, n // NB + 1)
                        dve.sem_inc(s["timed"], 1)
                elif u.kind == "residual":
                    dve.wait_ge(ring.product, base + n + 1)
                    dve.scalar_tensor_tensor(u.dst, u.dst, u.more, v, ALU.mult, ALU.add).then_inc(fr, 1)
                elif u.kind in ("gate_first", "gate_add"):
                    dve.wait_ge(ring.product, base + n + 1)
                    gate = max(m for m in range(n) if units[m].dst is u.more)
                    dve.wait_ge(free[gate % NB], gate // NB + 1)
                    if u.kind == "gate_first":
                        chain.step(dve.tensor_tensor(u.dst, u.more, v, ALU.mult))
                        dve.sem_inc(fr, 1)
                    else:
                        chain.step(dve.tensor_tensor(u.more, u.more, v, ALU.mult))
                        dve.sem_inc(fr, 1)
                        chain.step(dve.tensor_tensor(u.dst, u.dst, u.more, ALU.add))

            for i, (src, pair) in enumerate(splits[:1]):
                dve.wait_ge(s["x_high"], 1)
                dve.tensor_tensor(pair[1], src, pair[0].bitcast(F32), ALU.subtract).then_inc(s["x_low"], 1)
            for c in first:
                ring.split_low(dve, c)
            for n in range(len(units)):
                if n:
                    empty(n - 1)
                for c in after[n]:
                    ring.split_low(dve, c)
                if n == 0:
                    for i, (src, pair) in enumerate(splits[1:]):
                        dve.wait_ge(s["x_high"], i + 2)
                        dve.tensor_tensor(pair[1], src, pair[0].bitcast(F32), ALU.subtract).then_inc(s["x_low"], 1)
            empty(len(units) - 1)


def down_phase(nc, ring, layer, names, h, x, scale):
    base, todo = ring.plan(names)
    with phase(nc, "", (), [(f"y{i}", HALF) for i in range(4)]) as (block, s, b):
        y = [b["y0"], b["y1"], b["y2"], b["y3"]]

        @block.sync
        def _(sp):
            ring.send(sp, layer)

        @block.scalar
        def _(act):
            for c in todo:
                ring.split_high(act, c)

        @block.gpsimd
        def _(pool):
            for c in todo:
                ring.split_low(pool, c)

        @block.tensor
        def _(pe):
            for n in range(len(names)):
                w = ring.arrive(pe, base + n)
                for kk in range(2):
                    k = 2 * n + kk
                    for j in range(KD):
                        mm = passes(pe, y[j // 2][:, (j % 2) * 256:(j % 2) * 256 + 256],
                                    [v[:, kk, j * P:(j + 1) * P] for v in w], [v[:, k, :] for v in h],
                                    k == 0 and j % 2 == 0, k == KF - 1, True)
                mm.then_inc(ring.product, 1)

        @block.vector
        def _(dve):
            for c in todo:
                ring.split_low(dve, c)
            dve.wait_ge(ring.product, base + len(names))
            for i in range(4):
                xs = x[:, 2 * i:2 * i + 2, :]
                dve.scalar_tensor_tensor(xs, xs, scale, y[i][:, :].rearrange("p (i t) -> p i t", i=2),
                                         ALU.mult, ALU.add)


def rope_phase(nc, K, jobs, ring=None, layer=None):
    with phase(nc, "rotated read0 read1 dve_step done", [("c0", [P, 2, 256]), ("c1", [P, 2, 256]), ("r", [P, 2, 2, 256])],
               [("rot0", HALF), ("rot1", HALF)]) as (block, s, b):
        rot, read, cb = [b["rot0"], b["rot1"]], [s["read0"], s["read1"]], [b["c0"], b["c1"]]

        @block.sync
        def _(sp):
            if ring is not None:
                ring.send(sp, layer)

        @block.tensor
        def _(pe):
            for n, (raw, perm, cos, sin) in enumerate(jobs):
                if n >= 2:
                    pe.wait_ge(read[n % 2], n // 2)
                w = raw.shape[1]
                pe.matmul(rot[n % 2][:, 0:w * 256], perm, raw.rearrange("p i t -> p (i t)"),
                          start=True, stop=True).then_inc(s["rotated"], 1)

        @block.vector
        def _(dve):
            chain = Chain(dve, s["dve_step"])
            for n, (raw, perm, cos, sin) in enumerate(jobs):
                w = raw.shape[1]
                dve.wait_ge(s["rotated"], n + 1)
                r = b["r"][:, n % 2, 0:w, :]
                dve.tensor_tensor(r, rot[n % 2][:, 0:w * 256].rearrange("p (i t) -> p i t", i=w),
                                  sin.unsqueeze(1).to_broadcast([P, w, 256]), ALU.mult).then_inc(read[n % 2], 1)
                chain.step(dve.tensor_tensor(raw, raw, cos.unsqueeze(1).to_broadcast([P, w, 256]), ALU.mult))
                dve.wait_ge(read[n % 2], n // 2 + 1)
                dve.tensor_tensor(raw, raw, r, ALU.add)


def pair_slot(h):
    return (h % 2) * 2 + h // 2


class Group:

    def __init__(self, nk, scale, pairs, slot, mask, value, place, dst):
        self.nk, self.scale, self.pairs, self.slot = nk, scale, pairs, slot
        self.mask, self.value, self.place, self.dst = mask, value, place, dst


def attention_phase(nc, K, groups, ring=None, layer=None):
    with phase(nc, "scored masked shifted exped normed turned turned_out pv read_s0 read_s1 copied dve_step act_step "
                   "p_free out_free",
               [("sm", [P, 2, 4, 256]), ("pt", [P, 2, 8, P]), ("mx", [P, 2, 4]), ("sum", [P, 2, 4]), ("rc", [P, 2, 4])],
               [("s0", 2 * HALF), ("s1", 2 * HALF), ("tp", 2 * HALF), ("o", 2 * HALF)]) as (block, s, b):
        sc = [b["s0"], b["s1"]]

        @block.sync
        def _(sp):
            if ring is not None:
                ring.send(sp, layer)

        @block.tensor
        def _(pe):
            def scores(n):
                g = groups[n]
                if n >= 2:
                    pe.wait_ge(s["masked"], n - 1)
                for h in range(4):
                    pairs = g.pairs(h)
                    at = g.slot(h) * 256
                    for i, (lhs, rhs) in enumerate(pairs):
                        mm = pe.matmul(sc[n % 2][:, at:at + g.nk], lhs, rhs,
                                       start=(i == 0), stop=(i == len(pairs) - 1))
                mm.then_inc(s["scored"], 1)

            scores(0)
            for n, g in enumerate(groups):
                if n + 1 < len(groups):
                    scores(n + 1)
                kts = g.nk // P
                pe.wait_ge(s["normed"], n + 1)
                if n:
                    pe.wait_ge(s["copied"], n)
                for h in range(4):
                    for kt in range(kts):
                        mm = pe.transpose(b["tp"][:, (h * 2 + kt) * P:(h * 2 + kt + 1) * P],
                                          b["sm"][:, n % 2, h, kt * P:(kt + 1) * P], K("ident"))
                mm.then_inc(s["turned"], 1)
                pe.wait_ge(s["copied"], n + 1)
                if n:
                    pe.wait_ge(s["out_free"], n)
                for h in range(4):
                    for i, region in enumerate(g.place(b["o"], h)):
                        for kt in range(kts):
                            mm = pe.matmul(region, g.value(h, kt)[i], b["pt"][:, n % 2, g.slot(h) * 2 + kt, :],
                                           start=(kt == 0), stop=(kt == kts - 1))
                mm.then_inc(s["pv"], 1)

        @block.vector
        def _(dve):
            chain = Chain(dve, s["dve_step"])

            def weigh(n):
                g = groups[n]
                sm = b["sm"][:, n % 2, :, 0:g.nk]
                v = sc[n % 2][:, :].rearrange("p (h k) -> p h k", h=4)[:, :, 0:g.nk]
                dve.wait_ge(s["scored"], n + 1)
                if n >= 2:
                    dve.wait_ge(s["turned"], n - 1)
                if g.mask is None:
                    ins = dve.tensor_copy(sm, v)
                else:
                    ins = dve.tensor_tensor(sm, v, g.mask if g.mask.shape[1] == 4 else g.mask.to_broadcast([P, 4, g.nk]),
                                            ALU.add)
                ins.then_inc(s["masked"], 1)
                dve.wait_ge(s["masked"], n + 1)
                chain.step(dve.tensor_reduce(b["mx"][:, n % 2, :], sm, AX_X, ALU.max))
                dve.tensor_scalar(b["mx"][:, n % 2, :], b["mx"][:, n % 2, :], -g.scale, None, ALU.mult).then_inc(s["shifted"], 1)

            def normalise(n):
                g = groups[n]
                sm = b["sm"][:, n % 2, :, 0:g.nk]
                dve.wait_ge(s["exped"], 4 * (n + 1))
                chain.step(dve.reciprocal(b["rc"][:, n % 2, :], b["sum"][:, n % 2, :]))
                dve.tensor_tensor(sm, sm, b["rc"][:, n % 2, :].unsqueeze(2).to_broadcast([P, 4, g.nk]),
                                  ALU.mult).then_inc(s["normed"], 1)

            weigh(0)
            for n, g in enumerate(groups):
                if n + 1 < len(groups):
                    weigh(n + 1)
                normalise(n)
                dve.wait_ge(s["pv"], n + 1)
                for i, (region, dst) in enumerate(g.dst(b["o"])):
                    ins = dve.tensor_copy(dst, region)
                ins.then_inc(s["out_free"], 1)

        @block.scalar
        def _(act):
            def exponentials(n):
                g = groups[n]
                act.wait_ge(s["shifted"], n + 1)
                for h in range(4):
                    act.activation(b["sm"][:, n % 2, h, 0:g.nk], b["sm"][:, n % 2, h, 0:g.nk], ACT.Exp,
                                   bias=b["mx"][:, n % 2, h:h + 1], scale=g.scale,
                                   accum_out=b["sum"][:, n % 2, h:h + 1]).then_inc(s["exped"], 1)

            exponentials(0)
            for n, g in enumerate(groups):
                if n + 1 < len(groups):
                    exponentials(n + 1)
                act.wait_ge(s["turned"], n + 1)
                if n >= 2:
                    act.wait_ge(s["pv"], n - 1)
                tp = b["tp"][:, :].rearrange("p (h k q) -> p h k q", h=4, k=2)[:, :, 0:g.nk // P, :]
                pt = b["pt"][:, n % 2, :, :].rearrange("p (h k) q -> p h k q", h=4)[:, :, 0:g.nk // P, :]
                act.activation(pt, tp, ACT.Copy).then_inc(s["copied"], 1)


def side_phase(nc, K, prm, sgu_rows, buf, ring, layer):
    c8 = 2 * 4
    with phase(nc, "negc spread tril gates exped logged summed rooted vn mixed band pooled pmix dve_step act_step",
               [("wT", [P, 4, P]), ("lf", [4, 3, T]), ("on", [4, T]), ("m", [P, c8]), ("ms", [P, c8]), ("sd", [P, c8]),
                ("cen", [P, c8, 64]), ("sq", [P, c8, 64]), ("pooled", [P, 2, 256])],
               [("mix", HALF), ("pb", HALF), ("pm", HALF), ("c", 2 * HALF)]) as (block, s, b):

        @block.sync
        def _(sp):
            ring.send(sp, layer)

        @block.gpsimd
        def _(pool):
            pool.affine_select(out=b["wT"][:, :, :], in_=prm("sgu_wT").rearrange("p (g t) -> p g t", g=4),
                               compare_op=ALU.is_ge, fill=0.0, base=0, pattern=[[0, 4], [1, P]],
                               channel_multiplier=-1).then_inc(s["tril"], 1)

        @block.vector
        def _(dve):
            chain = Chain(dve, s["dve_step"])
            y, ab, lf = b["lf"][:, 0, :], b["lf"][:, 1, :], b["lf"][:, 2, :]
            dve.memset(b["on"][:, :], 1.0)
            chain.step(dve.tensor_scalar(y, buf["bf"][:, :], prm("b_forget")[0:4, :], None, ALU.add))
            chain.step(dve.tensor_scalar(ab, y, -1.0, None, ALU.mult))
            dve.tensor_tensor(ab, y, ab, ALU.max).then_inc(s["gates"], 1)
            cv = buf["cv"].rearrange("p t (g c) -> p (t g) c", g=4)
            chain.step(dve.tensor_reduce(b["m"][:, :], cv, AX_X, ALU.add))
            chain.step(dve.tensor_scalar(b["m"][:, :], b["m"][:, :], 1.0 / 64, None, ALU.mult))
            chain.step(dve.tensor_tensor(b["cen"][:, :, :], cv, b["m"][:, :].unsqueeze(2).to_broadcast([P, c8, 64]),
                                         ALU.subtract))
            chain.step(dve.tensor_tensor(b["sq"][:, :, :], b["cen"][:, :, :], b["cen"][:, :, :], ALU.mult))
            chain.step(dve.tensor_reduce(b["ms"][:, :], b["sq"][:, :, :], AX_X, ALU.add))
            dve.tensor_scalar(b["ms"][:, :], b["ms"][:, :], 1.0 / 64, LN_EPS, ALU.mult, ALU.add).then_inc(s["summed"], 1)
            dve.wait_ge(s["logged"], 1)
            chain.step(dve.scalar_tensor_tensor(lf, y, 0.0, lf, ALU.min, ALU.subtract))
            chain.step(dve.tensor_tensor_scan(y, b["on"][:, :], lf, 0.0, ALU.mult, ALU.add))
            dve.tensor_scalar(buf["negc"][:, :], y, -8.0, None, ALU.mult).then_inc(s["negc"], 1)
            dve.wait_ge(s["rooted"], 1)
            chain.step(dve.reciprocal(b["sd"][:, :], b["sd"][:, :]))
            chain.step(dve.tensor_tensor(b["cen"][:, :, :], b["cen"][:, :, :],
                                         b["sd"][:, :].unsqueeze(2).to_broadcast([P, c8, 64]), ALU.mult))
            cen = b["cen"][:, :, :].rearrange("p (t g) c -> p t (g c)", t=2)
            chain.step(dve.tensor_tensor(cen, cen, sgu_rows[:, 0:256].unsqueeze(1).to_broadcast([P, 2, 256]), ALU.mult))
            dve.tensor_tensor(cen, cen, sgu_rows[:, 256:512].unsqueeze(1).to_broadcast([P, 2, 256]),
                              ALU.add).then_inc(s["vn"], 1)
            dve.wait_ge(s["spread"], 1)
            for q in range(TT):
                dve.tensor_tensor(buf["forget"][:, q, :, :], b["c"][:, :].rearrange("p (h k) -> p h k", h=4),
                                  K("causal").rearrange("p (q k) -> p q k", q=2)[:, q:q + 1, :].to_broadcast([P, 4, T]),
                                  ALU.add)
            dve.wait_ge(s["mixed"], 1)
            dve.tensor_tensor(buf["yT"][:, 4:6, :], buf["cu"], b["mix"][:, :].rearrange("p (i t) -> p i t", i=2), ALU.mult)

        @block.scalar
        def _(act):
            act.wait_ge(s["gates"], 1)
            act.activation(b["lf"][:, 2, :], b["lf"][:, 1, :], ACT.Exp, scale=-1.0).then_inc(s["exped"], 1)
            act.wait_ge(s["exped"], 1)
            act.activation(b["lf"][:, 2, :], b["lf"][:, 2, :], ACT.Ln, bias=1.0).then_inc(s["logged"], 1)
            act.wait_ge(s["summed"], 1)
            act.activation(b["sd"][:, :], b["ms"][:, :], ACT.Sqrt).then_inc(s["rooted"], 1)
            act.wait_ge(s["band"], 1)
            act.activation(b["pooled"][:, :, :], b["pb"][:, :].rearrange("p (i t) -> p i t", i=2), ACT.Copy).then_inc(s["pooled"], 1)
            act.wait_ge(s["pmix"], 1)
            for i in range(2):
                act.activation(buf["yT"][:, 6 + i, :], b["pm"][:, i * 256:(i + 1) * 256], ACT.Copy,
                               scale=prm("pool_scale")[:, i:i + 1])

        @block.tensor
        def _(pe):
            band = K("band").rearrange("p (s g t) -> p s g t", s=2, g=4)
            for g in range(4):
                r = slice((g % 2) * 64, (g % 2) * 64 + 64)
                for st in range(2):
                    mm = pe.matmul(b["pb"][r, (g // 2) * 256:(g // 2) * 256 + 256], buf["dp"][:, st, g * 64:(g + 1) * 64],
                                   band[:, st, g, :], start=(st == 0), stop=(st == 1))
            mm.then_inc(s["band"], 1)
            pe.wait_ge(s["pooled"], 1)
            pw = prm("pool_w").rearrange("p (i d) -> p i d", i=2)
            for g in range(4):
                r = slice((g % 2) * 64, (g % 2) * 64 + 64)
                mm = pe.matmul(b["pm"][r, (g // 2) * 256:(g // 2) * 256 + 256], pw[r, g // 2, :], b["pooled"][r, g // 2, :],
                               start=True, stop=True)
            mm.then_inc(s["pmix"], 1)
            pe.wait_ge(s["negc"], 1)
            for h in range(4):
                mm = pe.matmul(b["c"][:, pair_slot(h) * 256:(pair_slot(h) + 1) * 256],
                               K("select").rearrange("p (h m) -> p h m", h=8)[0:4, h, :], buf["negc"][:, :],
                               start=True, stop=True)
            mm.then_inc(s["spread"], 1)
            pe.wait_ge(s["tril"], 1)
            pe.wait_ge(s["vn"], 1)
            vn = b["cen"][:, :, :].rearrange("p (t g) c -> p t g c", t=2)
            for g in range(4):
                r = slice((g % 2) * 64, (g % 2) * 64 + 64)
                for tt in range(TT):
                    region = b["mix"][r, (g // 2) * 256 + tt * P:(g // 2) * 256 + (tt + 1) * P]
                    pe.matmul(region, vn[:, tt, g, :], b["wT"][:, g, :], start=True, stop=False)
                    mm = pe.matmul(region, K("ones")[0:1, 0:64], prm("sgu_b")[0:1, g * P:(g + 1) * P],
                                   start=False, stop=True)
            mm.then_inc(s["mixed"], 1)


def pair_of(nc, ctx, name, tiles):
    return [ctx.enter_context(nc.sbuf_tensor(f"{name}_{part}", [P, tiles, T], F32R))[:, :, :] for part in ("hi", "lo")]


def first_layer(nc, K, layer, x, xs, ring, par_dram, rows_dram):
    with ExitStack() as ctx:
        par = ctx.enter_context(nc.sbuf_tensor("par1_sb", [P, NPC1], F32))
        rows = ctx.enter_context(nc.sbuf_tensor("rows1_sb", [P, 512], F32))
        yT = ctx.enter_context(nc.sbuf_tensor("yT", [P, KD, T], F32))[:, :, :]
        prm = lambda name: par[:, PC1[name]]
        with phase(nc, "params") as (block, s, b):
            @block.sync
            def _(sp):
                sp.dma_start(par[:, :], par_dram[bass.ds(layer, 1), :, :].rearrange("o p n -> (o p) n")
                             ).then_inc(s["params"], 16)
                sp.dma_start(rows[:, :], rows_dram[bass.ds(layer, 1), :].to_broadcast([P, 512])).then_inc(s["params"], 16)
                ring.send(sp, layer)
                sp.wait_ge(s["params"], 32)

        with ExitStack() as mix:
            def sb(name, shape):
                return mix.enter_context(nc.sbuf_tensor(name, shape, F32))

            buf = {"yT": yT}
            aqk, bqk = sb("aqk", [P, 4, T]), sb("bqk", [P, 4, T])
            av, bv = sb("av", [P, 2, 256]), sb("bv", [P, 2, 256])
            buf["bf"], buf["negc"], buf["forget"] = sb("bf", [4, T]), sb("negc", [4, T]), sb("forget", [P, 2, 4, T])
            buf["cu"], buf["cv"], buf["dp"] = (sb(n, [P, 2, 256])[:, :, :] for n in ("cu", "cv", "dp"))
            copy = (ACT.Copy, None)
            gelu = (ACT.Gelu, None)
            product_phase(nc, ring, layer, [
                U("in0", "act", aqk[:, 0:2, :], copy), U("in1", "act", aqk[:, 2:4, :], copy),
                U("in2", "act", av[:, :, :], copy, tokens=True), U("in3", "act", bqk[:, 0:2, :], copy),
                U("in4", "act", bqk[:, 2:4, :], copy), U("in5", "act", bv[:, :, :], copy, tokens=True),
                U("gate_row", "rows", None, [(0, 4, buf["bf"][:, :])]),
                U("in6", "act", buf["cu"], gelu), U("in7", "act", buf["cv"], gelu, tokens=True),
                U("in8", "act", buf["dp"], copy, tokens=True)], xs)
            rope_phase(nc, K, [(aqk[:, 2 * i:2 * i + 2, :], K("perm64"), K("cos"), K("sin")) for i in range(2)],
                       ring, layer)
            side_phase(nc, K, prm, rows, buf, ring, layer)

            def group(qk, v, y0, q0, forget):
                nk = q0 + P
                causal = K("causal").rearrange("p (q k) -> p q k", q=2)[:, q0 // P:q0 // P + 1, 0:nk]

                def pairs(h):
                    r = slice((h % 2) * 64, (h % 2) * 64 + 64)
                    return [(qk[r, h // 2, q0:q0 + P], qk[r, 2 + h // 2, 0:nk])]

                return Group(
                    nk=nk, scale=0.125, pairs=pairs, slot=pair_slot,
                    mask=buf["forget"][:, q0 // P, :, 0:nk] if forget else causal,
                    value=lambda h, kt: [v[:, kt, h * 64:(h + 1) * 64]],
                    place=lambda o, h: [o[(h % 2) * 64:(h % 2) * 64 + 64, (h // 2) * P:(h // 2 + 1) * P]],
                    dst=lambda o: [(o[:, 0:256].rearrange("p (i q) -> p i q", i=2), yT[:, y0:y0 + 2, q0:q0 + P])])

            attention_phase(nc, K, [group(aqk, av, 0, 0, False), group(aqk, av, 0, P, False),
                                    group(bqk, bv, 2, 0, True), group(bqk, bv, 2, P, True)], ring, layer)

        with ExitStack() as st:
            ys = pair_of(nc, st, "y_split", KD)
            product_phase(nc, ring, layer, [U(f"o{i}", "residual", x[:, 2 * i:2 * i + 2, :], ALPHA) for i in range(4)], ys,
                          splits=[(yT, ys)])
        norm_phase(nc, K, x, x, prm("ln1_g"), prm("ln1_b"), LN_EPS, False, pair=xs, ring=ring, layer=layer)
        with ExitStack() as st:
            hid = st.enter_context(nc.sbuf_tensor("hid1", [P, KF, T], F32))
            hs = pair_of(nc, st, "hid1_split", KF)
            taps = prm("conv_w").rearrange("p (j c) -> p j c", j=3)
            hv = [hid[:, 2 * i:2 * i + 2, :] for i in range(KF // 2)]
            hp = [[v[:, 2 * i:2 * i + 2, :] for v in hs] for i in range(KF // 2)]
            product_phase(nc, ring, layer, [
                U(f"up{i}", "conv", hv[i % 11], (3, taps, prm("conv_b"), 2 * i, "silu" if i < 11 else "times"),
                  pair=hp[i % 11] if i >= 11 else None) for i in range(KF)], xs)
            down_phase(nc, ring, layer, [f"down{i}" for i in range(11)], hs, x, ALPHA)
        norm_phase(nc, K, x, x, prm("ln2_g"), prm("ln2_b"), LN_EPS, False, pair=xs, ring=ring, layer=layer)
        ring.clear(nc)


def split_phase(nc, src, pair):
    with phase(nc, "high") as (block, s, b):
        @block.scalar
        def _(act):
            act.activation(pair[0], src, ACT.Copy).then_inc(s["high"], 1)

        @block.vector
        def _(dve):
            dve.wait_ge(s["high"], 1)
            dve.tensor_tensor(pair[1], src, pair[0].bitcast(F32), ALU.subtract)


def chunked(parts, chunks):
    out = []
    for name, (w, row, col) in zip(chunks, parts):
        k, c = columns_of(name)
        a = w[:, row:row + k * P, col:col + c]
        out.append(a.reshape(a.shape[0], k, P, c).transpose(0, 2, 1, 3).reshape(a.shape[0], P, k * c))
    return np.ascontiguousarray(np.concatenate(out, axis=2))


def lay_first(i):
    w_in, w_o, w_up, w_down = i["w_in"], i["w_o"], i["w_up"], i["w_down"]
    gate = np.zeros((DEPTH, D, P), np.float32)
    gate[:, :, 0:4] = w_in[:, :, 1536:1540]
    parts = ([(w_in, 0, 256 * n) for n in range(6)] + [(gate, 0, 0)] + [(w_in, 0, 1540 + 256 * n) for n in range(3)]
             + [(w_o, 0, 256 * n) for n in range(4)] + [(w_up, 0, 256 * n) for n in range(22)]
             + [(w_down, 256 * n, 0) for n in range(11)])
    par = np.zeros((DEPTH, P, NPC1), np.float32)

    def cols(name, a):
        par[:, :, PC1[name]] = a.reshape(DEPTH, -1, P).transpose(0, 2, 1)

    for name in ("ln1_g", "ln1_b", "ln2_g", "ln2_b", "conv_b", "pool_scale"):
        cols(name, i[name])
    cols("conv_w", i["conv_w"].reshape(DEPTH, -1))
    par[:, 0:4, PC1["b_forget"]] = i["b_forget"][:, :, None]
    par[:, :, PC1["sgu_wT"]] = i["sgu_w"].transpose(0, 3, 1, 2).reshape(DEPTH, P, -1)
    par[:, 0, PC1["sgu_b"]] = i["sgu_b"].reshape(DEPTH, -1)
    par[:, :, PC1["pool_w"]] = i["pool_w"].reshape(DEPTH, 2, P, 64).transpose(0, 2, 1, 3).reshape(DEPTH, P, -1)
    rows = np.concatenate([i["sgu_ln_g"], i["sgu_ln_b"]], axis=1)
    return chunked(parts, CHUNKS_1), par, rows


def tiles_of(a):
    return np.ascontiguousarray(a.reshape(T, KD, P).transpose(2, 1, 0))


def angle_phase(nc, K, pos_dram, tables):
    magic = 1.5 * 2.0 ** 23
    c1 = 6.28125
    c2 = float(np.float32(2 * np.pi - c1).view(np.int32) // 4096 * 4096 and
               (np.float32(2 * np.pi - c1).view(np.int32) // 4096 * 4096).astype(np.int32).view(np.float32))
    c3 = 2 * np.pi - c1 - c2
    with phase(nc, "pos reduced sined dve_step",
               [("pos", [P, T]), ("k", [P, 2, T]), ("a", [P, 2, T]), ("h", [P, 2, T])]) as (block, s, b):
        posi = b["k"][:, 0, :].bitcast(I32)

        @block.sync
        def _(sp):
            sp.dma_start(posi, pos_dram.to_broadcast([P, T])).then_inc(s["pos"], 16)

        @block.vector
        def _(dve):
            chain = Chain(dve, s["dve_step"])
            dve.wait_ge(s["pos"], 16)
            chain.step(dve.tensor_copy(b["pos"][:, :], posi))
            for j in range(2):
                chain.step(dve.tensor_scalar(b["a"][:, j, :], b["pos"][:, :], K("freq")[:, j:j + 1], None, ALU.mult))
            a, k = b["a"][:, :, :], b["k"][:, :, :]
            chain.step(dve.tensor_scalar(k, a, 1.0 / (2 * np.pi), magic, ALU.mult, ALU.add))
            chain.step(dve.tensor_scalar(k, k, magic, None, ALU.subtract))
            for c in (c1, c2, c3):
                chain.step(dve.scalar_tensor_tensor(a, k, -c, a, ALU.mult, ALU.add))
            dve.tensor_scalar(a, a, 3.1415925, -3.1415925, ALU.min, ALU.max).then_inc(s["reduced"], 1)
            dve.wait_ge(s["sined"], 2)
            chain.step(dve.tensor_tensor(b["h"][:, :, :], b["h"][:, :, :], b["h"][:, :, :], ALU.mult))
            dve.tensor_scalar(tables[:, 0:2, :], b["h"][:, :, :], -2.0, 1.0, ALU.mult, ALU.add)

        @block.scalar
        def _(act):
            act.wait_ge(s["reduced"], 1)
            act.activation(tables[:, 2:4, :], b["a"][:, :, :], ACT.Sin).then_inc(s["sined"], 1)
            act.activation(b["h"][:, :, :], b["a"][:, :, :], ACT.Sin, scale=0.5).then_inc(s["sined"], 1)


QTY = 5


def decay_phase(nc, K, prm, small, ge, rowq, tokq, ring, layer):
    with phase(nc, "beta absed exped logged alog g gced ged rows turned dve_step act_step",
               [("y", [8, T]), ("ab", [8, T]), ("lf", [8, T]), ("on", [8, T]), ("ea", [8, 1])],
               [("tq", HALF)]) as (block, s, b):

        @block.sync
        def _(sp):
            ring.send(sp, layer)

        @block.vector
        def _(dve):
            chain = Chain(dve, s["dve_step"])
            y, ab, lf = b["y"][:, :], b["ab"][:, :], b["lf"][:, :]
            gc = rowq[:, 1, :]
            dve.memset(b["on"][:, :], 1.0)
            chain.step(dve.tensor_scalar(y, small[:, 1, :], prm("dt_bias")[0:8, :], None, ALU.add))
            chain.step(dve.tensor_scalar(ab, y, -1.0, None, ALU.mult))
            dve.tensor_tensor(ab, y, ab, ALU.max).then_inc(s["absed"], 1)
            dve.tensor_scalar(rowq[:, 4, :], small[:, 2, :], IDX_SCALE, None, ALU.mult)
            dve.wait_ge(s["logged"], 1)
            dve.wait_ge(s["alog"], 1)
            chain.step(dve.scalar_tensor_tensor(lf, y, 0.0, lf, ALU.max, ALU.add))
            chain.step(dve.tensor_scalar(lf, lf, b["ea"][:, 0:1], -1.0, ALU.mult, ALU.mult))
            for c in range(NCH):
                r = slice(c * CH, (c + 1) * CH)
                ins = dve.tensor_tensor_scan(rowq[:, 1, r], b["on"][:, r], lf[:, r], 0.0, ALU.mult, ALU.add)
            chain.step(ins)
            v = gc.rearrange("p (c i) -> p c i", c=NCH)
            dve.tensor_tensor(ab.rearrange("p (c i) -> p c i", c=NCH), v, v[:, :, CH - 1:CH].to_broadcast([8, NCH, CH]),
                              ALU.subtract).then_inc(s["gced"], 1)
            dve.wait_ge(s["ged"], 2)
            dve.wait_ge(s["beta"], 1)
            dve.tensor_tensor(rowq[:, 2, :], rowq[:, 0, :], ge, ALU.mult).then_inc(s["rows"], 1)
            dve.wait_ge(s["turned"], 1)
            dve.tensor_copy(tokq, b["tq"][:, 0:TT * QTY * 8].rearrange("p (t q h) -> p t q h", t=TT, q=QTY))

        @block.scalar
        def _(act):
            act.activation(rowq[:, 0, :], small[:, 0, :], ACT.Sigmoid).then_inc(s["beta"], 1)
            act.activation(b["ea"][:, :], prm("a_log")[0:8, :], ACT.Exp).then_inc(s["alog"], 1)
            act.wait_ge(s["absed"], 1)
            act.activation(b["lf"][:, :], b["ab"][:, :], ACT.Exp, scale=-1.0).then_inc(s["exped"], 1)
            act.wait_ge(s["exped"], 1)
            act.activation(b["lf"][:, :], b["lf"][:, :], ACT.Ln, bias=1.0).then_inc(s["logged"], 1)
            act.wait_ge(s["gced"], 1)
            act.activation(ge, rowq[:, 1, :], ACT.Exp).then_inc(s["ged"], 1)
            act.activation(rowq[:, 3, :], b["ab"][:, :], ACT.Exp, scale=-1.0).then_inc(s["ged"], 1)

        @block.tensor
        def _(pe):
            pe.wait_ge(s["rows"], 1)
            for tt in range(TT):
                for q in range(QTY):
                    at = (tt * QTY + q) * 8
                    mm = pe.transpose(b["tq"][:, at:at + 8], rowq[:, q, tt * P:(tt + 1) * P], K("ident")[0:8, 0:8])
            mm.then_inc(s["turned"], 1)


def unit_keys_phase(nc, K, q, k, ring, layer):
    jobs = [(v, i, sc) for v, sc in ((q, P ** -0.5), (k, 1.0)) for i in range(0, KD, 2)]
    with phase(nc, "squared summed logged inverted scaled",
               [("sq", [P, 2, 2, T]), ("r", [P, 2, 2, T])], [("ss0", HALF), ("ss1", HALF)]) as (block, s, b):
        ss = [b["ss0"], b["ss1"]]

        @block.sync
        def _(sp):
            ring.send(sp, layer)

        @block.tensor
        def _(pe):
            for n in range(len(jobs)):
                pe.wait_ge(s["squared"], n + 1)
                if n >= 2:
                    pe.wait_ge(s["logged"], n - 1)
                pe.matmul(ss[n % 2][:, :], K("ones"), b["sq"][:, n % 2, :, :].rearrange("p i t -> p (i t)"),
                          start=True, stop=True).then_inc(s["summed"], 1)

        @block.gpsimd
        def _(pool):
            for n, (v, i, sc) in enumerate(jobs):
                if n >= 2:
                    pool.wait_ge(s["summed"], n - 1)
                pool.tensor_tensor(b["sq"][:, n % 2, :, :], v[:, i:i + 2, :], v[:, i:i + 2, :], ALU.mult
                                   ).then_inc(s["squared"], 1)

        @block.scalar
        def _(act):
            for n in range(len(jobs)):
                r = b["r"][:, n % 2, :, :]
                act.wait_ge(s["summed"], n + 1)
                if n >= 2:
                    act.wait_ge(s["scaled"], n - 1)
                act.activation(r, ss[n % 2][:, :].rearrange("p (i t) -> p i t", i=2), ACT.Ln, bias=K("eps")
                               ).then_inc(s["logged"], 1)
                act.wait_ge(s["logged"], n + 1)
                act.activation(r, r, ACT.Exp, scale=-0.5).then_inc(s["inverted"], 1)

        @block.vector
        def _(dve):
            for n, (v, i, sc) in enumerate(jobs):
                dve.wait_ge(s["inverted"], n + 1)
                dve.scalar_tensor_tensor(v[:, i:i + 2, :], b["r"][:, n % 2, :, :], sc, v[:, i:i + 2, :],
                                         ALU.mult, ALU.mult).then_inc(s["scaled"], 1)


NP = 8


def delta_prepare_phase(nc, K, hf, q, k, v, ge, rowq, tokq, h, ring, layer):
    sel = K("select").rearrange("p (h m) -> p h m", h=8)
    upper, strict = K("upper"), K("strict")
    with phase(nc, "turned read spread_g spread_e spread_b bread grams diffed exped masked dve_step eb_read gread",
               [("e", [P, NP, P]), ("es", [P, NP, P])],
               [("g0", HALF), ("g1", HALF), ("e0", HALF), ("e1", HALF), ("t0", HALF), ("t1", HALF), ("m0", HALF),
                ("m1", HALF)]) as (block, s, b):
        g, e, t, m = [b["g0"], b["g1"]], [b["e0"], b["e1"]], [b["t0"], b["t1"]], [b["m0"], b["m1"]]

        @block.sync
        def _(sp):
            ring.send(sp, layer)

        @block.tensor
        def _(pe):
            for hh in range(4):
                pe.matmul(g[hh // 2][:, (hh % 2) * T:(hh % 2 + 1) * T], sel[0:8, 4 * hf + hh, :], rowq[:, 1, :],
                          start=True, stop=True).then_inc(s["spread_g"], 1)
            for hh in range(4):
                mm = pe.matmul(e[hh // 2][:, (hh % 2) * T:(hh % 2 + 1) * T], sel[0:8, 4 * hf + hh, :], ge,
                               start=True, stop=True)
            mm.then_inc(s["spread_e"], 1)
            for n, src in enumerate((k, v)):
                for tt in range(TT):
                    if n:
                        pe.wait_ge(s["read"], 1 + tt)
                    for hh in range(4):
                        mm = pe.transpose(t[tt][:, hh * P:(hh + 1) * P], src[:, 4 * hf + hh, tt * P:(tt + 1) * P],
                                          K("ident"))
                    mm.then_inc(s["turned"], 1)
            for n, other in enumerate((q, k)):
                for tt in range(TT):
                    if n:
                        pe.wait_ge(s["gread"], 1 + tt)
                    for hh in range(4):
                        hd, c = 4 * hf + hh, slice(tt * P, (tt + 1) * P)
                        mm = pe.matmul(m[tt][:, hh * P:(hh + 1) * P], k[:, hd, c], other[:, hd, c], start=True, stop=True)
                    mm.then_inc(s["grams"], 1)
            pe.wait_ge(s["diffed"], 1)
            for hh in range(4):
                mm = pe.matmul(g[hh // 2][:, (hh % 2) * T:(hh % 2 + 1) * T], sel[0:8, 4 * hf + hh, :], rowq[:, 0, :],
                               start=True, stop=True)
            mm.then_inc(s["spread_b"], 1)

        @block.vector
        def _(dve):
            chain = Chain(dve, s["dve_step"])
            for hh in range(4):
                dve.wait_ge(s["spread_g"], 4)
                for tt in range(TT):
                    ins = dve.tensor_scalar(b["e"][:, tt * 4 + hh, :],
                                            g[hh // 2][:, (hh % 2) * T + tt * P:(hh % 2) * T + (tt + 1) * P],
                                            tokq[:, tt, 1, 4 * hf + hh:4 * hf + hh + 1], 0.0, ALU.subtract, ALU.min)
            ins.then_inc(s["diffed"], 1)
            dve.wait_ge(s["spread_e"], 1)
            for i in range(2):
                ev = e[i][:, :].rearrange("p (h t) -> p h t", h=2)
                dve.tensor_copy(h["ge"][:, 2 * i:2 * i + 2, :], ev)
                dve.tensor_tensor(h["qd"][:, 2 * i:2 * i + 2, :], q[:, 4 * hf + 2 * i:4 * hf + 2 * i + 2, :], ev, ALU.mult)

            def token(qty, tt):
                return tokq[:, tt, qty, 4 * hf:4 * hf + 4].unsqueeze(2).to_broadcast([P, 4, P])

            for tt in range(TT):
                dve.wait_ge(s["turned"], tt + 1)
                tv = t[tt][:, :].rearrange("p (h d) -> p h d", h=4)
                pr = slice(tt * 4, tt * 4 + 4)
                dve.tensor_tensor(h["kb"][:, pr, :], tv, token(2, tt), ALU.mult)
                dve.tensor_tensor(h["kd"][:, pr, :], tv, token(3, tt), ALU.mult).then_inc(s["read"], 1)
            for tt in range(TT):
                dve.wait_ge(s["turned"], TT + tt + 1)
                dve.tensor_tensor(h["vb"][:, tt * 4:tt * 4 + 4, :], t[tt][:, :].rearrange("p (h d) -> p h d", h=4),
                                  token(0, tt), ALU.mult)
            dve.wait_ge(s["exped"], 1)
            chain.step(dve.tensor_tensor(b["e"][:, :, :], b["e"][:, :, :], upper.unsqueeze(1).to_broadcast([P, NP, P]), ALU.mult))
            dve.tensor_tensor(b["es"][:, :, :], b["e"][:, :, :], strict.unsqueeze(1).to_broadcast([P, NP, P]), ALU.mult)
            for tt in range(TT):
                dve.wait_ge(s["grams"], tt + 1)
                pr = slice(tt * 4, tt * 4 + 4)
                dve.tensor_tensor(h["at"][:, pr, :], m[tt][:, :].rearrange("p (h i) -> p h i", h=4), b["e"][:, pr, :],
                                  ALU.mult).then_inc(s["gread"], 1)
            dve.wait_ge(s["spread_b"], 1)
            for hh in range(4):
                for tt in range(TT):
                    es = b["es"][:, tt * 4 + hh, :]
                    ins = dve.tensor_tensor(es, es, g[hh // 2][:, (hh % 2) * T + tt * P:(hh % 2) * T + (tt + 1) * P],
                                            ALU.mult)
            chain.step(ins)
            for tt in range(TT):
                dve.wait_ge(s["grams"], TT + tt + 1)
                pr = slice(tt * 4, tt * 4 + 4)
                dve.tensor_tensor(h["mt"][:, pr, :], m[tt][:, :].rearrange("p (h i) -> p h i", h=4), b["es"][:, pr, :], ALU.mult)

        @block.scalar
        def _(act):
            act.wait_ge(s["diffed"], 1)
            act.activation(b["e"][:, :, :], b["e"][:, :, :], ACT.Exp).then_inc(s["exped"], 1)


def delta_solve_phase(nc, K, h, ring, layer):
    ident = K("ident").unsqueeze(1).to_broadcast([P, 4, P])
    lev = K("levels").rearrange("p (l i) -> p l i", l=6)
    with phase(nc, "begun lower0 lower1 masked0 masked1 cross0 cross1 kept0 kept1 solved dve_step",
               [("t", [P, NP, P]), ("y", [P, NP, P])],
               [(f"{n}{i}", HALF) for n in ("y_ps", "d_ps", "c_ps") for i in range(2)]) as (block, s, b):
        yp, dp, cp = [b["y_ps0"], b["y_ps1"]], [b["d_ps0"], b["d_ps1"]], [b["c_ps0"], b["c_ps1"]]
        lower, masked = [s["lower0"], s["lower1"]], [s["masked0"], s["masked1"]]
        cross, kept = [s["cross0"], s["cross1"]], [s["kept0"], s["kept1"]]

        @block.sync
        def _(sp):
            ring.send(sp, layer)

        @block.tensor
        def _(pe):
            pe.wait_ge(s["begun"], 4)
            for lv in range(6):
                for g in range(2):
                    if lv:
                        pe.wait_ge(kept[g], 2 * lv)
                    for n in range(4 * g, 4 * g + 4):
                        mm = pe.matmul(yp[g][:, (n % 4) * P:(n % 4 + 1) * P], h["mt"][:, n, :], b["t"][:, n, :],
                                       start=True, stop=True)
                    mm.then_inc(lower[g], 1)
                for g in range(2):
                    pe.wait_ge(masked[g], lv + 1)
                    for n in range(4 * g, 4 * g + 4):
                        c = slice((n % 4) * P, (n % 4 + 1) * P)
                        if lv < 5:
                            pe.matmul(dp[g][:, c], h["ti"][:, n, :], b["y"][:, n, :], start=True, stop=True)
                        mm = pe.matmul(cp[g][:, c], b["y"][:, n, :], h["ti"][:, n, :], start=True, stop=True)
                    mm.then_inc(cross[g], 1)
            for g in range(2):
                pe.wait_ge(kept[g], 11)
                for n in range(4 * g, 4 * g + 4):
                    c = slice((n % 4) * P, (n % 4 + 1) * P)
                    pe.matmul(yp[g][:, c], h["ti"][:, n, :], h["vb"][:, n, :], start=True, stop=True)
                    mm = pe.matmul(dp[g][:, c], h["kb"][:, n, :], h["ti"][:, n, :], start=True, stop=True)
                mm.then_inc(s["solved"], 1)

        @block.vector
        def _(dve):
            for g in range(2):
                pr = slice(4 * g, 4 * g + 4)
                dve.tensor_copy(b["t"][:, pr, :], ident).then_inc(s["begun"], 1)
                dve.tensor_copy(h["ti"][:, pr, :], ident).then_inc(s["begun"], 1)
            dve.wait_ge(s["begun"], 4)
            for lv in range(6):
                for g in range(2):
                    pr = slice(4 * g, 4 * g + 4)
                    dve.wait_ge(lower[g], lv + 1)
                    dve.tensor_tensor(b["y"][:, pr, :], yp[g][:, :].rearrange("p (n i) -> p n i", n=4),
                                      lev[:, lv:lv + 1, :].to_broadcast([P, 4, P]), ALU.mult).then_inc(masked[g], 1)
                for g in range(2):
                    pr = slice(4 * g, 4 * g + 4)
                    dve.wait_ge(cross[g], lv + 1)
                    if lv:
                        dve.wait_ge(kept[g], 2 * lv)
                    dve.tensor_tensor(h["ti"][:, pr, :], h["ti"][:, pr, :], cp[g][:, :].rearrange("p (n i) -> p n i", n=4),
                                      ALU.subtract).then_inc(kept[g], 1)
                    if lv < 5:
                        dve.tensor_tensor(b["t"][:, pr, :], b["t"][:, pr, :], dp[g][:, :].rearrange("p (n i) -> p n i", n=4),
                                          ALU.subtract).then_inc(kept[g], 1)
            for g in range(2):
                dve.wait_ge(s["solved"], g + 1)
                dve.tensor_copy(h["u"][:, 4 * g:4 * g + 4, :], yp[g][:, :].rearrange("p (n i) -> p n i", n=4))

        @block.scalar
        def _(act):
            for g in range(2):
                act.wait_ge(s["solved"], g + 1)
                act.activation(h["w"][:, 4 * g:4 * g + 4, :], dp[g][:, :].rearrange("p (n i) -> p n i", n=4), ACT.Copy)


def delta_scan_phase(nc, K, prm, hf, h, z, o_dn, ring, layer):
    with phase(nc, "zeroed ws vnew out state kept squared plus_eps rooted normed turned dve_step",
               [("st", [P, 4, P]), ("vn", [P, 4, P]), ("sq", [P, NP, P]), ("ms", [P, NP])],
               [("w_ps", HALF), ("o_ps", HALF), ("k_ps", HALF), ("t0", HALF), ("t1", HALF)]) as (block, s, b):
        tp = [b["t0"], b["t1"]]
        o = h["u"]

        @block.sync
        def _(sp):
            ring.send(sp, layer)

        @block.tensor
        def _(pe):
            for c in range(NCH):
                tt, r = c // 2, slice((c % 2) * CH, (c % 2 + 1) * CH)
                pe.wait_ge(s["state"], 4 * c + 1)
                for hh in range(4):
                    mm = pe.matmul(b["w_ps"][r, hh * P:(hh + 1) * P], h["w"][:, tt * 4 + hh, r], b["st"][:, hh, :],
                                   start=True, stop=True)
                mm.then_inc(s["ws"], 1)
                pe.wait_ge(s["vnew"], c + 1)
                if c:
                    pe.wait_ge(s["kept"], c)
                for hh in range(4):
                    n = tt * 4 + hh
                    mm = pe.matmul(b["k_ps"][:, hh * P:(hh + 1) * P], h["kd"][r, n, :], b["vn"][r, hh, :], start=True, stop=True)
                mm.then_inc(s["out"], 1)
                for hh in range(4):
                    n = tt * 4 + hh
                    cols = slice(hh * P, (hh + 1) * P)
                    pe.matmul(b["o_ps"][r, cols], h["qd"][:, hh, c * CH:(c + 1) * CH], b["st"][:, hh, :], start=True, stop=False)
                    mm = pe.matmul(b["o_ps"][r, cols], h["at"][r, n, r], b["vn"][r, hh, :], start=False, stop=True)
                mm.then_inc(s["out"], 1)
            for tt in range(TT):
                pe.wait_ge(s["normed"], 1)
                for hh in range(4):
                    mm = pe.transpose(tp[tt][:, hh * P:(hh + 1) * P], b["sq"][:, tt * 4 + hh, :], K("ident"))
                mm.then_inc(s["turned"], 1)

        @block.vector
        def _(dve):
            chain = Chain(dve, s["dve_step"])
            dve.memset(b["st"][:, :, :], 0.0).then_inc(s["state"], 1)
            for c in range(NCH):
                tt, r = c // 2, slice((c % 2) * CH, (c % 2 + 1) * CH)
                dve.wait_ge(s["ws"], c + 1)
                dve.tensor_tensor(b["vn"][r, :, :], h["u"][r, tt * 4:tt * 4 + 4, :],
                                  b["w_ps"][r, :].rearrange("p (h d) -> p h d", h=4), ALU.subtract).then_inc(s["vnew"], 1)
                if c + 1 < NCH:
                    dve.wait_ge(s["out"], 2 * c + 2)
                    dve.wait_ge(s["state"], 4 * c + 1)
                    for hh in range(4):
                        at = (c + 1) * CH - 1
                        dve.scalar_tensor_tensor(b["st"][:, hh, :], b["st"][:, hh, :], h["ge"][:, hh, at:at + 1],
                                                 b["k_ps"][:, hh * P:(hh + 1) * P], ALU.mult, ALU.add).then_inc(s["state"], 1)
            dve.wait_ge(s["squared"], 1)
            chain.step(dve.tensor_reduce(b["ms"][:, :], b["sq"][:, :, :], AX_X, ALU.add))
            dve.tensor_scalar(b["ms"][:, :], b["ms"][:, :], 1.0 / P, NORM_EPS, ALU.mult, ALU.add).then_inc(s["plus_eps"], 1)
            dve.wait_ge(s["rooted"], 1)
            chain.step(dve.reciprocal(b["ms"][:, :], b["ms"][:, :]))
            dve.tensor_tensor(b["sq"][:, :, :], o[:, :, :], b["ms"][:, :].unsqueeze(2).to_broadcast([P, NP, P]),
                              ALU.mult).then_inc(s["normed"], 1)
            for tt in range(TT):
                dve.wait_ge(s["turned"], tt + 1)
                c = slice(tt * P, (tt + 1) * P)
                dve.scalar_tensor_tensor(o_dn[:, 4 * hf:4 * hf + 4, c], tp[tt][:, :].rearrange("p (h t) -> p h t", h=4),
                                         prm("dn_norm"), z[:, 4 * hf:4 * hf + 4, c], ALU.mult, ALU.mult)

        @block.scalar
        def _(act):
            for c in range(NCH):
                tt, r = c // 2, slice((c % 2) * CH, (c % 2 + 1) * CH)
                act.wait_ge(s["out"], 2 * c + 2)
                act.activation(o[r, tt * 4:tt * 4 + 4, :], b["o_ps"][r, :].rearrange("p (h d) -> p h d", h=4),
                               ACT.Copy).then_inc(s["kept"], 1)
            act.wait_ge(s["kept"], NCH)
            act.activation(b["sq"][:, :, :], o[:, :, :], ACT.Square).then_inc(s["squared"], 1)
            act.wait_ge(s["plus_eps"], 1)
            act.activation(b["ms"][:, :], b["ms"][:, :], ACT.Sqrt).then_inc(s["rooted"], 1)


def index_phase(nc, K, iq, ik, tokq, masks, ring, layer):
    with phase(nc, "scored0 scored1 relued summed masked max8 dve_step",
               [("r", [P, 2, 8, T]), ("sc", [P, T]), ("wk", [P, T]), ("m8", [P, 8])],
               [("a0", 2 * HALF), ("b0", 2 * HALF), ("a1", 2 * HALF), ("b1", 2 * HALF)]) as (block, s, b):
        ps = [[b["a0"], b["b0"]], [b["a1"], b["b1"]]]
        scored = [s["scored0"], s["scored1"]]

        @block.sync
        def _(sp):
            ring.send(sp, layer)

        @block.tensor
        def _(pe):
            for qt in range(TT):
                nk = (qt + 1) * P
                for h in range(8):
                    r = slice((h % 2) * 64, (h % 2 + 1) * 64)
                    mm = pe.matmul(ps[qt][h % 2][:, (h // 2) * T:(h // 2) * T + nk], iq[r, h // 2, qt * P:(qt + 1) * P],
                                   ik[r, 0:nk], start=True, stop=True)
                mm.then_inc(scored[qt], 1)

        @block.scalar
        def _(act):
            for qt in range(TT):
                nk = (qt + 1) * P
                act.wait_ge(scored[qt], 1)
                for half in range(2):
                    act.activation(b["r"][:, qt, 4 * half:4 * half + 4, 0:nk],
                                   ps[qt][half][:, :].rearrange("p (h k) -> p h k", h=4)[:, :, 0:nk],
                                   ACT.Relu).then_inc(s["relued"], 1)

        @block.vector
        def _(dve):
            chain = Chain(dve, s["dve_step"])
            for qt in range(TT):
                nk = (qt + 1) * P
                sc, wk = b["sc"][:, 0:nk], b["wk"][:, 0:nk]
                dve.wait_ge(s["relued"], 2 * qt + 2)
                mask = K("chunk_causal").rearrange("p (q k) -> p q k", q=2)[:, qt, 0:nk]
                for h in range(8):
                    at = (h % 2) * 4 + h // 2
                    chain.step(dve.scalar_tensor_tensor(sc, b["r"][:, qt, at, 0:nk], tokq[:, qt, 4, h:h + 1],
                                                        mask if h == 0 else sc, ALU.mult, ALU.add))
                for i in range(TOPK // 8):
                    src = sc if i == 0 else wk
                    chain.step(dve.max(b["m8"][:, :], src))
                    chain.step(dve.match_replace(wk, b["m8"][:, :], src, TAKEN))
                chain.step(dve.tensor_scalar(wk, wk, TAKEN / 2, 1.0, ALU.is_le, ALU.subtract))
                dve.tensor_scalar(masks[:, qt, 0:nk], wk, -NEG, None, ALU.mult)


def second_layer(nc, K, layer, x, hs, mem_dram, ring, par_dram, tables):
    with ExitStack() as ctx:
        def sb(stack, name, shape):
            return stack.enter_context(nc.sbuf_tensor(name, shape, F32))

        par = sb(ctx, "par2_sb", [P, NPC2])
        prm = lambda name: par[:, PC2[name]]
        o_dn = sb(ctx, "o_dn", [P, KD, T])[:, :, :]
        tokq = sb(ctx, "tokq", [P, TT, QTY, 8])[:, :, :, :]
        ik = sb(ctx, "ik", [P, T])[:, :]
        copy = (ACT.Copy, None)
        with phase(nc, "params") as (block, s, b):
            @block.sync
            def _(sp):
                sp.dma_start(par[:, :], par_dram[bass.ds(layer, 1), :, :].rearrange("o p n -> (o p) n")
                             ).then_inc(s["params"], 16)
                ring.send(sp, layer)
                sp.wait_ge(s["params"], 16)

        norm_phase(nc, K, x, None, prm("norm_mix"), None, NORM_EPS, True, pair=hs, ring=ring, layer=layer)

        with ExitStack() as st:
            q, k, v, z = (sb(st, n, [P, KD, T])[:, :, :] for n in ("dq", "dk", "dv", "dz"))
            small, rowq, ge = sb(st, "small", [8, 3, T]), sb(st, "rowq", [8, QTY, T])[:, :, :], sb(st, "ge_row", [8, T])[:, :]
            taps = prm("conv_w").rearrange("p (j c) -> p j c", j=4)
            units = [U("small", "rows", ik, [(32 * n, 8, small[:, n, :]) for n in range(3)])]
            for n in range(12):
                dst = (q, k, v)[n // 4][:, 2 * (n % 4):2 * (n % 4) + 2, :]
                units.append(U(f"dn{n}", "conv", dst, (4, taps, None, 2 * n, "silu")))
            units += [U(f"dn{12 + n}", "act", z[:, 2 * n:2 * n + 2, :], (ACT.Silu, None)) for n in range(4)]
            product_phase(nc, ring, layer, units, hs)
            decay_phase(nc, K, prm, small, ge, rowq, tokq, ring, layer)
            unit_keys_phase(nc, K, q, k, ring, layer)
            for hf in range(2):
                with ExitStack() as half:
                    h = {}
                    for n in ("kb", "kd", "vb", "at", "mt", "ti", "u", "w"):
                        h[n] = sb(half, f"{n}_{hf}", [P, NP, P])[:, :, :]
                    h["qd"], h["ge"] = (sb(half, f"{n}_{hf}", [P, 4, T])[:, :, :] for n in ("qd", "ge"))
                    delta_prepare_phase(nc, K, hf, q, k, v, ge, rowq, tokq, h, ring, layer)
                    delta_solve_phase(nc, K, h, ring, layer)
                    delta_scan_phase(nc, K, prm, hf, h, z, o_dn, ring, layer)

        o_sa, o_xa = (sb(ctx, n, [P, KD, T])[:, :, :] for n in ("o_sa", "o_xa"))

        with ExitStack() as st:
            sq, sk = sb(st, "sq_", [P, KD, T])[:, :, :], sb(st, "sk_", [P, KD, T])[:, :, :]
            sv, iq = sb(st, "sv_", [P, TT, D])[:, :, :], sb(st, "iq_", [P, 4, T])[:, :, :]
            masks = sb(st, "masks", [P, TT, T])[:, :, :]
            units = [U(f"sa{n}", "act", (sq, sk)[n // 4][:, 2 * (n % 4):2 * (n % 4) + 2, :], copy) for n in range(8)]
            units += [U(f"sa{8 + n}", "act", sv[:, :, n * 256:(n + 1) * 256], copy, tokens=True) for n in range(4)]
            units += [U(f"iq{n}", "act", iq[:, 2 * n:2 * n + 2, :], copy) for n in range(2)]
            product_phase(nc, ring, layer, units, hs)
            cs128, sn128 = tables[:, 0, :], tables[:, 2, :]
            cs64, sn64 = tables[:, 1, :], tables[:, 3, :]
            rope_phase(nc, K, [(t[:, 2 * i:2 * i + 2, :], K("perm128"), cs128, sn128) for t in (sq, sk) for i in range(4)]
                       + [(iq[:, 2 * i:2 * i + 2, :], K("perm64"), cs64, sn64) for i in range(2)]
                       + [(ik.unsqueeze(1), K("perm64"), cs64, sn64)], ring, layer)
            index_phase(nc, K, iq, ik, tokq, masks, ring, layer)

            def group(h0, qt):
                nk, c = (qt + 1) * P, slice(qt * P, (qt + 1) * P)
                return Group(
                    nk=nk, scale=128 ** -0.5, slot=lambda h: h, mask=masks[:, qt:qt + 1, 0:nk],
                    pairs=lambda h: [(sq[:, h0 + h, c], sk[:, h0 + h, 0:nk])],
                    value=lambda h, kt: [sv[:, kt, (h0 + h) * P:(h0 + h + 1) * P]],
                    place=lambda o, h: [o[:, h * P:(h + 1) * P]],
                    dst=lambda o: [(o[:, 0:HALF].rearrange("p (i q) -> p i q", i=4), o_sa[:, h0:h0 + 4, c])])

            attention_phase(nc, K, [group(h0, qt) for h0 in (0, 4) for qt in range(TT)], ring, layer)

        with ExitStack() as st:
            mem = sb(st, "mem_sb", [P, KD, T])[:, :, :]
            with phase(nc, "memory") as (block, s, b):
                @block.sync
                def _(sp):
                    sp.dma_start(mem, mem_dram).then_inc(s["memory"], 16)
                    sp.wait_ge(s["memory"], 16)
            mk, xq = (sb(st, n, [P, KD, T])[:, :, :] for n in ("mk", "xq"))
            mn = pair_of(nc, st, "mem_split", KD)
            mv = sb(st, "mv_", [P, TT, D])[:, :, :]
            norm_phase(nc, K, mem, None, prm("norm_mem"), None, NORM_EPS, True, pair=mn, ring=ring, layer=layer)
            units = [U(f"kv{n}", "act", mk[:, 2 * n:2 * n + 2, :], copy, x=mn) for n in range(4)]
            units += [U(f"kv{4 + n}", "act", mv[:, :, n * 256:(n + 1) * 256], copy, x=mn, tokens=True) for n in range(4)]
            units += [U(f"xq{n}", "act", xq[:, 2 * n:2 * n + 2, :], copy) for n in range(4)]
            product_phase(nc, ring, layer, units, hs)

            def group(qt):
                c = slice(qt * P, (qt + 1) * P)
                return Group(
                    nk=T, scale=256 ** -0.5, slot=lambda h: h, mask=None,
                    pairs=lambda h: [(xq[:, 2 * h + i, c], mk[:, 2 * h + i, :]) for i in range(2)],
                    value=lambda h, kt: [mv[:, kt, (2 * h + i) * P:(2 * h + i + 1) * P] for i in range(2)],
                    place=lambda o, h: [o[:, (2 * h + i) * P:(2 * h + i + 1) * P] for i in range(2)],
                    dst=lambda o: [(o[:, :].rearrange("p (i q) -> p i q", i=8), o_xa[:, :, c])])

            attention_phase(nc, K, [group(qt) for qt in range(TT)], ring, layer)

        merged = sb(ctx, "merged", [P, KD, T])[:, :, :]
        with ExitStack() as st:
            gates = sb(st, "gates", [P, 2, 3, 4, T])
            split = [pair_of(nc, st, f"o{i}_split", KD) for i in range(3)]
            units = []
            bg = prm("b_gate")
            for c in range(2):
                pair = [merged[:, 4 * c + 2 * u:4 * c + 2 * u + 2, :] for u in range(2)]
                for i in range(3):
                    g = [gates[:, c, i, 2 * u:2 * u + 2, :] for u in range(2)]
                    at = 8 * i + 4 * c
                    units += [U(f"gl{i}_{2 * c + u}", "act", g[u],
                                (ACT.Sigmoid, bg[:, at + 2 * u:at + 2 * u + 2])) for u in range(2)]
                    units += [U(f"wb{i}_{2 * c + u}", "gate_add" if i else "gate_first", pair[u], g[u], x=split[i])
                              for u in range(2)]
            product_phase(nc, ring, layer, units, hs, splits=list(zip((o_dn, o_sa, o_xa), split)))
        with ExitStack() as st:
            ms = pair_of(nc, st, "merged_split", KD)
            product_phase(nc, ring, layer, [U(f"out{i}", "residual", x[:, 2 * i:2 * i + 2, :], 1.0) for i in range(4)], ms,
                          splits=[(merged, ms)])

        norm_phase(nc, K, x, None, prm("norm_ffn"), None, NORM_EPS, True, pair=hs, ring=ring, layer=layer)
        with ExitStack() as st:
            hid = st.enter_context(nc.sbuf_tensor("hid2", [P, KF, T], F32))
            fs = pair_of(nc, st, "hid2_split", KF)
            hv = [hid[:, 2 * i:2 * i + 2, :] for i in range(KF // 2)]
            hp = [[v[:, 2 * i:2 * i + 2, :] for v in fs] for i in range(KF // 2)]
            product_phase(nc, ring, layer,
                          [U(f"fin{i}", "act" if i < 11 else "times", hv[i % 11], (ACT.Silu, None),
                             pair=hp[i % 11] if i >= 11 else None) for i in range(KF)], hs)
            down_phase(nc, ring, layer, [f"fout{i}" for i in range(11)], fs, x, 1.0)
        ring.clear(nc)


def build(nc, a, out_dram):
    with ExitStack() as ctx:
        const = ctx.enter_context(nc.sbuf_tensor("const_sb", [P, NCC2], F32))
        x = ctx.enter_context(nc.sbuf_tensor("x_sb", [P, KD, T], F32))[:, :, :]
        xs = pair_of(nc, ctx, "x_split", KD)
        with phase(nc, "begin") as (block, s, b):
            @block.sync
            def _(sp):
                sp.dma_start(const[:, :], a["const"][:, 0:NCC2]).then_inc(s["begin"], 16)
                sp.dma_start(x, a["xT"]).then_inc(s["begin"], 16)
                sp.wait_ge(s["begin"], 32)
        if "w1" in a:
            with ExitStack() as first:
                more = first.enter_context(nc.sbuf_tensor("const1_sb", [P, NCC - NCC2], F32))
                ring = Ring(nc, first, "w1", CHUNKS_1, a["w1"])

                def K(name):
                    c = CC[name]
                    return const[:, c] if c.stop <= NCC2 else more[:, c.start - NCC2:c.stop - NCC2]

                with phase(nc, "begin") as (block, s, b):
                    @block.sync
                    def _(sp):
                        sp.dma_start(more[:, :], a["const"][:, NCC2:NCC]).then_inc(s["begin"], 16)
                        sp.wait_ge(s["begin"], 16)
                split_phase(nc, x, xs)
                with nc.Fori(0, DEPTH) as layer:
                    first_layer(nc, K, layer, x, xs, ring, a["par1"], a["rows1"])
        K = lambda name: const[:, CC[name]]
        gain = ctx.enter_context(nc.sbuf_tensor("final_gain", [P, D], F32))
        if "w2" not in a:
            with phase(nc, "stored") as (block, s, b):
                @block.sync
                def _(sp):
                    sp.dma_start(out_dram, x).then_inc(s["stored"], 16)
                    sp.wait_ge(s["stored"], 16)
            return
        with ExitStack() as second:
            ring = Ring(nc, second, "w2", CHUNKS_2, a["w2"])
            tables = second.enter_context(nc.sbuf_tensor("tables", [P, 4, T], F32))[:, :, :]
            angle_phase(nc, K, a["positions"], tables)
            with nc.Fori(0, DEPTH) as layer:
                second_layer(nc, K, layer, x, xs, a["memT"], ring, a["par2"], tables)
        with phase(nc, "gain") as (block, s, b):
            @block.sync
            def _(sp):
                sp.dma_start(gain[:, :], a["norm_final"].to_broadcast([P, D])).then_inc(s["gain"], 16)
                sp.wait_ge(s["gain"], 16)
        norm_phase(nc, K, x, None, gain[:, :], None, NORM_EPS, True, out=out_dram)


def lay_second(i):
    w = i["w_in_2"]
    at = dict(zip("dq dk dv dz db da sq sk sv iq ik iw xq gl".split(),
                  np.cumsum([0, D, D, D, D, 8, 8, D, D, D, 512, 64, 8, D]).tolist()))
    wb = i["w_branch_2"].reshape(DEPTH, 3 * D, D)
    small = np.zeros((DEPTH, D, 256), np.float32)
    for n, name in enumerate(("db", "da", "iw")):
        small[:, :, 32 * n:32 * n + 8] = w[:, :, at[name]:at[name] + 8]
    for n in range(2):
        small[:, :, P + 64 * n:P + 64 * (n + 1)] = w[:, :, at["ik"]:at["ik"] + 64]
    parts = ([(small, 0, 0)] + [(w, 0, 256 * n) for n in range(16)] + [(w, 0, at["sq"] + 256 * n) for n in range(12)]
             + [(w, 0, at["iq"] + 256 * n) for n in range(2)] + [(i["w_mem_kv_2"], 0, 256 * n) for n in range(8)]
             + [(w, 0, at["xq"] + 256 * n) for n in range(4)]
             + [p for c in range(2) for b in range(3) for p in
                [(w, 0, at["gl"] + D * b + 512 * c + 256 * u) for u in range(2)]
                + [(wb, D * b, 512 * c + 256 * u) for u in range(2)]]
             + [(i["w_out_2"], 0, 256 * n) for n in range(4)] + [(i["w_ffn_in_2"], 0, 256 * n) for n in range(22)]
             + [(i["w_ffn_out_2"], 256 * n, 0) for n in range(11)])
    par = np.zeros((DEPTH, P, NPC2), np.float32)
    for name in ("norm_mix", "norm_mem", "norm_ffn", "b_gate", "conv_w", "dn_norm"):
        par[:, :, PC2[name]] = i[name + "_2"].reshape(DEPTH, -1, P).transpose(0, 2, 1)
    for name in ("a_log", "dt_bias"):
        par[:, 0:8, PC2[name]] = i[name + "_2"][:, :, None]
    return chunked(parts, CHUNKS_2), par


def kernel(**inputs):
    import concourse.bacc as bacc
    from concourse.bass_utils import run_bass_kernel_spmd as run

    i = {name: np.asarray(v) for name, v in inputs.items()}
    w1, par1, rows1 = lay_first(i)
    w2, par2 = lay_second(i)
    arrays = {"xT": tiles_of(i["x"][0]), "w1": w1, "par1": par1, "rows1": rows1, "w2": w2, "par2": par2,
              "memT": tiles_of(i["mem_2"][0]), "positions": i["positions_2"],
              "norm_final": i["norm_final_2"].reshape(1, D), "const": constants()}
    nc = bacc.Bacc("TRN2", target_bir_lowering=False, num_devices=1)
    dram = {n: nc.dram_tensor(n, v.shape, mybir.dt.from_np(v.dtype), kind="ExternalInput").ap() for n, v in arrays.items()}
    out = nc.dram_tensor("out", (T, D), F32, kind="ExternalOutput").ap()
    build(nc, dram, out)
    r = run(nc, [arrays], core_ids=[0])
    return r.results[0]["out"].reshape(1, T, D)
```

```python
from contextlib import ExitStack, contextmanager

import numpy as np

import concourse.bass as bass
from concourse import mybir

F32 = mybir.dt.float32
F32R = mybir.dt.float32r
I32 = mybir.dt.int32
ALU = mybir.AluOpType
ACT = mybir.ActivationFunctionType
AX_X = mybir.AxisListType.X

P = 128
T = 256
TT = T // P
D = 1024
KD = D // P
DEPTH = 2
FF = 2816
KF = FF // P
HALF = 512
NEG = -1.0e30
TAKEN = -3.0e38
ALPHA = (2 * DEPTH) ** 0.25
LN_EPS = 1e-5
NORM_EPS = 1e-6
CH = 64
NCH = T // CH
TOPK = T // 4
WINDOWS = (2, 4, 8, 16)
THETA = 500000.0
IDX_SCALE = 8 ** -0.5 * 64 ** -0.5
SLOTS = 3
SPLIT_SLOTS = 2
CHUNK_W = 8 * 256
DVE_PART = 5 * 256


CHUNKS_1 = ([f"in{i}" for i in range(6)] + ["gate_row"] + [f"in{i}" for i in range(6, 9)]
            + [f"o{i}" for i in range(4)] + [f"up{i}" for i in range(22)] + [f"down{i}" for i in range(11)])
CHUNKS_2 = (["small"] + [f"dn{i}" for i in range(16)] + [f"sa{i}" for i in range(12)] + ["iq0", "iq1"]
            + [f"xq{i}" for i in range(4)] + [f"kv{i}" for i in range(8)]
            + [f"{b}{i}_{2 * c + u}" for c in range(2) for i in range(3) for b in ("gl", "wb") for u in range(2)]
            + [f"out{i}" for i in range(4)] + [f"fin{i}" for i in range(22)] + [f"fout{i}" for i in range(11)])


def columns_of(name):
    return (2, D) if name.startswith(("down", "fout")) else (KD, P) if name == "gate_row" else (KD, 256)


def columns(spec):
    at, out = 0, {}
    for name, n in spec:
        out[name] = slice(at, at + n)
        at += n
    return out, at


PC1, NPC1 = columns([("ln1_g", 8), ("ln1_b", 8), ("ln2_g", 8), ("ln2_b", 8), ("conv_w", 3 * 44), ("conv_b", 44),
                     ("pool_scale", 2), ("b_forget", 1), ("sgu_wT", 4 * 128), ("sgu_b", 4 * 128), ("pool_w", 2 * 64)])
PC2, NPC2 = columns([("norm_mix", 8), ("norm_mem", 8), ("norm_ffn", 8), ("b_gate", 24), ("conv_w", 4 * 24),
                     ("dn_norm", 1), ("a_log", 1), ("dt_bias", 1)])
CC, NCC = columns([("ident", 128), ("ones", 128), ("perm64", 128), ("select", 8 * 128), ("eps", 1),
                   ("chunk_causal", 2 * 256), ("perm128", 128), ("freq", 2), ("levels", 6 * 128), ("upper", 128),
                   ("strict", 128), ("level0T", 128),
                   ("causal", 2 * 256), ("band", 2 * 4 * 256), ("cos", 256), ("sin", 256)])
NCC2 = CC["causal"].start


def constants():
    c = np.zeros((P, NCC), np.float32)
    p = np.arange(P)
    t = np.arange(T)

    def put(name, a):
        c[:a.shape[0], CC[name]] = a.reshape(a.shape[0], -1)

    put("ident", np.eye(P))
    put("eps", np.full((P, 1), NORM_EPS))
    put("ones", np.ones((P, P)))
    q = p[:, None] + P * np.arange(TT)[None, :]
    put("causal", np.where(t[None, None, :] <= q[:, :, None], 0.0, NEG))
    put("chunk_causal", np.where(t[None, None, :] // CH <= q[:, :, None] // CH, 0.0, NEG))
    s = q[:, :, None, None]
    win = np.array(WINDOWS)[None, None, :, None]
    at = t[None, None, None, :]
    inside = (s <= at) & (s > at - win)
    put("band", inside / np.minimum(at + 1, win) - (s == at))
    half = 8
    inv = (np.float64(THETA) ** (-np.arange(0, 16, 2) / 16)).astype(np.float32)
    ang = t[None, :].astype(np.float32) * inv[p % half][:, None]
    roped = ((p % 64) < 16)[:, None]
    put("cos", np.where(roped, np.cos(ang), 1.0))
    put("sin", np.where(roped, np.sin(ang), 0.0))
    for name, dim, h in (("perm64", 64, 8), ("perm128", 128, 16)):
        m = np.zeros((P, P))
        for d in range(P):
            if d % dim < h:
                m[d + h, d] = -1.0
            elif d % dim < 2 * h:
                m[d - h, d] = 1.0
        put(name, m)
    f = np.zeros((P, 2))
    inv128 = (np.float64(THETA) ** (-np.arange(16) * 2.0 / 32)).astype(np.float32)
    inv64 = (np.float64(THETA) ** (-np.arange(8) * 2.0 / 16)).astype(np.float32)
    f[:32, 0] = inv128[p[:32] % 16]
    f[:, 1] = np.where(p % 64 < 16, inv64[p % 8], 0.0)
    put("freq", f)
    i, j = p[:, None], p[None, :]
    lev = [((i // (2 * b) == j // (2 * b)) & (i // b > j // b)) for b in (1, 2, 4, 8, 16, 32)]
    put("levels", np.stack(lev, 1).astype(np.float64))
    put("level0T", lev[0].T.astype(np.float64))
    same = i // CH == j // CH
    put("upper", (same & (j >= i)).astype(np.float64))
    put("strict", (same & (j > i)).astype(np.float64))
    sel = np.zeros((8, 8, P))
    sel[np.arange(8), np.arange(8)] = 1.0
    put("select", sel)
    return c


PHASES = []


@contextmanager
def phase(nc, names, tensors=(), banks=()):
    with ExitStack() as ctx:
        at = len(PHASES)
        PHASES.append(names)
        handles = [ctx.enter_context(nc.semaphore(n)) for n in names.split()]
        s = {n: h for n, h in zip(names.split(), handles)}
        b = {}
        for name, shape in tensors:
            b[name] = ctx.enter_context(nc.sbuf_tensor(f"{name}_{at}", shape, F32))
        for name, width in banks:
            b[name] = ctx.enter_context(nc.psum_tensor(f"{name}_{at}", [P, width], F32))
        with nc.Block() as block:
            yield block, s, b
        for h in handles:
            nc.gpsimd.sem_clear(h)
        nc.all_engine_barrier()


class Chain:

    def __init__(self, eng, sem):
        self.eng, self.sem, self.n = eng, sem, 0

    def step(self, ins):
        self.n += 1
        ins.then_inc(self.sem, 1)
        self.eng.wait_ge(self.sem, self.n)


class Ring:

    def __init__(self, nc, ctx, name, chunks, dram, head=None):
        def sb(part, n, dt):
            return ctx.enter_context(nc.sbuf_tensor(f"{name}_{part}", [P, n, CHUNK_W], dt))

        self.raw, self.hi, self.lo = sb("raw", SLOTS, F32), sb("hi", SPLIT_SLOTS, F32R), sb("lo", SPLIT_SLOTS, F32R)
        self.loaded = [ctx.enter_context(nc.semaphore(f"{name}_loaded{i}")) for i in range(SLOTS)]
        self.high, self.low_dve, self.low_pool, self.product = (
            ctx.enter_context(nc.semaphore(f"{name}_{n}")) for n in ("high", "low_dve", "low_pool", "product"))
        self.names, self.dram, self.head = chunks, dram, head
        self.width = [k * c for k, c in (columns_of(n) for n in chunks)]
        self.skipped = sum(self.width[:SLOTS]) if head is not None else 0
        self.start()

    def start(self):
        self.sent, self.units, self.split = 0, 0, 0

    def resume(self):
        self.sent, self.units, self.split = SLOTS, 0, 1

    def plan(self, names):
        base = self.units
        assert self.names[base:base + len(names)] == names, (self.names[base:base + len(names)], names)
        self.units += len(names)
        todo = range(self.split, min(self.units + 1, len(self.names)))
        self.split = todo.stop
        return base, todo

    def send(self, sp, layer, loads=(), sem=None, after=6):
        upto = min(self.split + SLOTS, len(self.names))
        for n in range(self.sent, upto):
            if n == after:
                for dst, src in loads:
                    sp.dma_start(dst, src).then_inc(sem, 16)
            at = sum(self.width[:n]) - self.skipped
            if n >= SLOTS:
                sp.wait_ge(self.low_dve, n - SLOTS + 1)
                sp.wait_ge(self.low_pool, n - SLOTS + 1)
            sp.dma_start(self.raw[:, n % SLOTS, 0:self.width[n]],
                         self.dram[bass.ds(layer, 1), :, at:at + self.width[n]].rearrange("o p n -> (o p) n")
                         ).then_inc(self.loaded[n % SLOTS], 16)
        self.sent = upto

    def send_head(self, sp, layer, upto=SLOTS):
        for n in range(self.sent, upto):
            at = sum(self.width[:n])
            sp.dma_start(self.raw[:, n, 0:self.width[n]],
                         self.head[bass.ds(layer, 1), :, at:at + self.width[n]].rearrange("o p n -> (o p) n")
                         ).then_inc(self.loaded[n], 16)
        self.sent = upto

    def settle(self, nc):
        with phase(nc, "") as (block, s, b):
            @block.sync
            def _(sp):
                for n in range(SLOTS):
                    sp.wait_ge(self.loaded[n], 16)
        for sem in [*self.loaded, self.high, self.low_dve, self.low_pool]:
            nc.gpsimd.sem_clear(sem)
        nc.all_engine_barrier()

    def split_high(self, act, n):
        w = self.width[n]
        act.wait_ge(self.loaded[n % SLOTS], 16 * (n // SLOTS + 1))
        if n >= SPLIT_SLOTS:
            act.wait_ge(self.product, n - SPLIT_SLOTS + 1)
        act.activation(self.hi[:, n % SPLIT_SLOTS, 0:w], self.raw[:, n % SLOTS, 0:w], ACT.Copy).then_inc(self.high, 1)

    def split_low(self, eng, n):
        dve = eng.engine == mybir.EngineType.DVE
        mid = self.width[n] * DVE_PART // CHUNK_W
        c = slice(0, mid) if dve else slice(mid, self.width[n])
        eng.wait_ge(self.high, n + 1)
        eng.tensor_tensor(self.lo[:, n % SPLIT_SLOTS, c], self.raw[:, n % SLOTS, c],
                          self.hi[:, n % SPLIT_SLOTS, c].bitcast(F32), ALU.subtract
                          ).then_inc(self.low_dve if dve else self.low_pool, 1)

    def split_low_all(self, pool, n):
        mid = self.width[n] * DVE_PART // CHUNK_W
        pool.wait_ge(self.high, n + 1)
        for c, sem in ((slice(0, mid), self.low_dve), (slice(mid, self.width[n]), self.low_pool)):
            pool.tensor_tensor(self.lo[:, n % SPLIT_SLOTS, c], self.raw[:, n % SLOTS, c],
                               self.hi[:, n % SPLIT_SLOTS, c].bitcast(F32), ALU.subtract).then_inc(sem, 1)

    def arrive(self, pe, n):
        pe.wait_ge(self.low_dve, n + 1)
        pe.wait_ge(self.low_pool, n + 1)
        k, c = columns_of(self.names[n])
        return [part[:, n % SPLIT_SLOTS, 0:k * c].rearrange("p (k c) -> p k c", k=k) for part in (self.hi, self.lo)]

    def clear(self, nc):
        assert self.sent == self.units == self.split == len(self.names)
        for sem in [*self.loaded, self.high, self.low_dve, self.low_pool, self.product]:
            nc.gpsimd.sem_clear(sem)
        nc.all_engine_barrier()
        self.start()


def passes(pe, out, lhs, rhs, start, stop, skip=False):
    pe.matmul(out, lhs[0], rhs[0], start=start, stop=False, skip_group_check=skip)
    pe.matmul(out, lhs[0], rhs[1], start=False, stop=False, skip_group_check=skip)
    return pe.matmul(out, lhs[1], rhs[0], start=False, stop=stop, skip_group_check=skip)


def unit_product(pe, bank, w, x, token_major=False, before=None):
    kt, cols = w[0].shape[1], w[0].shape[2]
    for i in range(2 if token_major else cols // P):
        for k in range(kt):
            if before is not None and i == 0:
                before(k)
            if token_major:
                lhs, rhs = [v[:, k, i * P:(i + 1) * P] for v in x], [v[:, k, :] for v in w]
            else:
                lhs, rhs = [v[:, k, i * P:(i + 1) * P] for v in w], [v[:, k, :] for v in x]
            mm = passes(pe, bank[:, i * 256:(i + 1) * 256], lhs, rhs, k == 0, k == kt - 1)
    return mm


def norm_phase(nc, K, src, dst, gain, bias, eps, rms, pair=None, out=None, ring=None, layer=None, head=False):
    todo = ring.plan([])[1] if head else ()
    with phase(nc, "turned stats rooted scaled back stored high dve_step",
               [("xn", [P, TT, D]), ("bn", [P, TT, 2, 6]), ("mv", [P, TT, 2]), ("ms", [P, TT]), ("sd", [P, TT]),
                ("rs", [P, TT])],
               [("tok0", D), ("tok1", D)] + [(f"bk{i}", HALF) for i in range(4)]) as (block, s, b):
        tok = [b["tok0"], b["tok1"]]
        bk = [b["bk0"], b["bk1"], b["bk2"], b["bk3"]]

        @block.sync
        def _(sp):
            if head:
                ring.send_head(sp, layer)
            elif ring is not None:
                ring.send(sp, layer)
            if out is not None:
                for tt in range(TT):
                    sp.wait_ge(s["stored"], tt + 1)
                    sp.dma_start(out[tt * P:(tt + 1) * P, :], b["xn"][:, tt, :]).then_inc(s["back"], 16)
                sp.wait_ge(s["back"], 16 * TT)

        @block.gpsimd
        def _(pool):
            for c in todo:
                ring.split_low_all(pool, c)

        @block.tensor
        def _(pe):
            for tt in range(TT):
                for k in range(KD):
                    mm = pe.transpose(tok[tt][:, k * P:(k + 1) * P], src[:, k, tt * P:(tt + 1) * P], K("ident"))
                mm.then_inc(s["turned"], 1)
            if out is not None:
                return
            pe.wait_ge(s["scaled"], TT)
            for k in range(KD):
                for tt in range(TT):
                    mm = pe.transpose(bk[k // 2][:, (k % 2) * 256 + tt * P:(k % 2) * 256 + (tt + 1) * P],
                                      b["xn"][:, tt, k * P:(k + 1) * P], K("ident"))
                if k % 2:
                    mm.then_inc(s["back"], 1)

        @block.vector
        def _(dve):
            chain = Chain(dve, s["dve_step"])
            for tt in range(TT):
                dve.wait_ge(s["turned"], tt + 1)
                dve.bn_stats(b["bn"][:, tt, 0, :], tok[tt][:, 0:HALF])
                chain.step(dve.bn_stats(b["bn"][:, tt, 1, :], tok[tt][:, HALF:D]))
                chain.step(dve.bn_aggr(b["mv"][:, tt, :], b["bn"][:, tt, :, :]))
                if rms:
                    chain.step(dve.scalar_tensor_tensor(b["ms"][:, tt:tt + 1], b["mv"][:, tt, 0:1], b["mv"][:, tt, 0:1],
                                                        b["mv"][:, tt, 1:2], ALU.mult, ALU.add))
                    dve.tensor_scalar(b["ms"][:, tt:tt + 1], b["ms"][:, tt:tt + 1], eps, None, ALU.add).then_inc(s["stats"], 1)
                else:
                    dve.tensor_scalar(b["ms"][:, tt:tt + 1], b["mv"][:, tt, 1:2], eps, None, ALU.add).then_inc(s["stats"], 1)
            for tt in range(TT):
                dve.wait_ge(s["rooted"], tt + 1)
                chain.step(dve.reciprocal(b["rs"][:, tt:tt + 1], b["sd"][:, tt:tt + 1]))
                if rms:
                    ins = dve.tensor_scalar(b["xn"][:, tt, :], tok[tt][:, :], b["rs"][:, tt:tt + 1], None, ALU.mult)
                else:
                    ins = dve.tensor_scalar(b["xn"][:, tt, :], tok[tt][:, :], b["mv"][:, tt, 0:1], b["rs"][:, tt:tt + 1],
                                            ALU.subtract, ALU.mult)
                if out is None:
                    ins.then_inc(s["scaled"], 1)
                else:
                    chain.step(ins)
                    dve.tensor_tensor(b["xn"][:, tt, :], b["xn"][:, tt, :], gain, ALU.mult).then_inc(s["stored"], 1)
            if out is not None:
                return
            for i in (0, 1, 2, 3):
                ks = (2 * i, 2 * i + 1)
                v = bk[i][:, :].rearrange("p (i t) -> p i t", i=2)
                if dst is not None:
                    dve.wait_ge(s["back"], i + 1)
                    for j, k in enumerate(ks):
                        ins = dve.tensor_scalar(dst[:, k, :], v[:, j, :], gain[:, k:k + 1], bias[:, k:k + 1], ALU.mult, ALU.add)
                    ins.then_inc(s["stored"], 1)
                else:
                    dve.wait_ge(s["high"], i + 1)
                    for j, k in enumerate(ks):
                        dve.scalar_tensor_tensor(pair[1][:, k, :], v[:, j, :], gain[:, k:k + 1],
                                                 pair[0][:, k, :].bitcast(F32), ALU.mult, ALU.subtract)
            if dst is not None and pair is not None:
                for i in range(4):
                    dve.wait_ge(s["high"], i + 1)
                    c = slice(2 * i, 2 * i + 2)
                    dve.tensor_tensor(pair[1][:, c, :], dst[:, c, :], pair[0][:, c, :].bitcast(F32), ALU.subtract)

        @block.scalar
        def _(act):
            for tt in range(TT):
                act.wait_ge(s["stats"], tt + 1)
                act.activation(b["sd"][:, tt:tt + 1], b["ms"][:, tt:tt + 1], ACT.Sqrt).then_inc(s["rooted"], 1)
            for c in todo:
                ring.split_high(act, c)
            if out is not None or pair is None:
                return
            for i in range(4):
                c = slice(2 * i, 2 * i + 2)
                if dst is not None:
                    act.wait_ge(s["stored"], i + 1)
                    ins = act.activation(pair[0][:, c, :], dst[:, c, :], ACT.Copy)
                else:
                    act.wait_ge(s["back"], i + 1)
                    for k in (2 * i, 2 * i + 1):
                        ins = act.activation(pair[0][:, k, :], bk[i][:, (k % 2) * 256:(k % 2) * 256 + 256], ACT.Copy,
                                             scale=gain[:, k:k + 1])
                ins.then_inc(s["high"], 1)


def rms_phase(nc, K, src, gain, pair, ring, layer, units=(), x=None, params=None):
    with phase(nc, "params squared_act squared_dve summed logged inverted scaled high" + Fill.names,
               [("sq", [P, KD, T]), ("h", [P, KD, T]), ("r", [P, T])], [("sum", HALF)] + Fill.banks) as (block, s, b):
        fill = Fill(ring, units, x, s, b)
        own = [[0, 1, 2, 6], [3, 4, 5, 7]]

        @block.sync
        def _(sp):
            if params is not None:
                sp.dma_start(params[0], params[1]).then_inc(s["params"], 16)
            ring.send(sp, layer)

        @block.gpsimd
        def _(pool):
            fill.pool(pool)

        @block.tensor
        def _(pe):
            order = [k for pair_of_tiles in zip(*own) for k in pair_of_tiles]
            for n, k in enumerate(order):
                pe.wait_ge(s["squared_dve" if n % 2 else "squared_act"], n // 2 + 1)
                mm = pe.matmul(b["sum"][:, 0:T], K("ones"), b["sq"][:, k, :], start=(n == 0), stop=(n == KD - 1))
            mm.then_inc(s["summed"], 1)
            fill.pe(pe)

        @block.scalar
        def _(act):
            for k in own[0]:
                act.activation(b["sq"][:, k, :], src[:, k, :], ACT.Square).then_inc(s["squared_act"], 1)
            fill.first_chunk(act)
            act.preload_act_table_set("natural_log_exp_and_others")
            act.wait_ge(s["summed"], 1)
            act.activation(b["r"][:, :], b["sum"][:, 0:T], ACT.Ln, scale=1.0 / D, bias=K("eps")).then_inc(s["logged"], 1)
            act.wait_ge(s["logged"], 1)
            act.activation(b["r"][:, :], b["r"][:, :], ACT.Exp, scale=-0.5).then_inc(s["inverted"], 1)
            for i in range(4):
                act.wait_ge(s["scaled"], 2 * i + 2)
                c = slice(2 * i, 2 * i + 2)
                act.activation(pair[0][:, c, :], b["h"][:, c, :], ACT.Copy).then_inc(s["high"], 1)
                if i == 0:
                    fill.act(act, 1)
            fill.act(act, last=True)

        @block.vector
        def _(dve):
            for k in own[1]:
                dve.tensor_tensor(b["sq"][:, k, :], src[:, k, :], src[:, k, :], ALU.mult).then_inc(s["squared_dve"], 1)
            if params is not None:
                dve.wait_ge(s["params"], 16)
            dve.wait_ge(s["inverted"], 1)
            for k in range(KD):
                dve.scalar_tensor_tensor(b["h"][:, k, :], src[:, k, :], gain[:, k:k + 1], b["r"][:, :],
                                         ALU.mult, ALU.mult).then_inc(s["scaled"], 1)
            for i in range(4):
                dve.wait_ge(s["high"], i + 1)
                c = slice(2 * i, 2 * i + 2)
                dve.tensor_tensor(pair[1][:, c, :], b["h"][:, c, :], pair[0][:, c, :].bitcast(F32), ALU.subtract)


NB = 4


class U:

    def __init__(self, chunk, kind, dst, more=None, x=None, tokens=False, pair=None):
        self.chunk, self.kind, self.dst, self.more, self.x, self.tokens, self.pair = chunk, kind, dst, more, x, tokens, pair


def product_phase(nc, ring, layer, units, x, splits=(), loads=()):
    base, todo = ring.plan([u.chunk for u in units])
    conv = [n for n, u in enumerate(units) if u.kind == "conv"]
    paired = [n for n, u in enumerate(units) if u.pair is not None]
    with phase(nc, "loads affine finished gated x_high x_low timed pair_high " + " ".join(f"free{i}" for i in range(NB)) + " dve_step",
               [("cb", [P, 2, 2, 256])] if conv else [],
               [(f"mm{i}", HALF) for i in range(NB)]) as (block, s, b):
        bank = [b[f"mm{i}"] for i in range(NB)]
        free = [s[f"free{i}"] for i in range(NB)]

        def view(n):
            return bank[n % NB][:, :].rearrange("p (i t) -> p i t", i=2)

        sliced = bool(splits) and splits[0][1] is x
        slices = ([(splits[0][0][:, c:c + 2, :], [v[:, c:c + 2, :] for v in x]) for c in range(0, KD, 2)]
                  if sliced else [])
        others = splits[1:] if sliced else splits
        during = {2 * j: split for j, split in enumerate(others)}

        first = [c for c in todo if c <= base]
        after = [[c for c in todo if c == base + n + 1] for n in range(len(units))]

        @block.sync
        def _(sp):
            ring.send(sp, layer, loads, s["loads"])
            if loads:
                sp.wait_ge(s["loads"], 16 * len(loads))

        def low(pool, n):
            u = units[n]
            pool.wait_ge(s["pair_high"], paired.index(n) + 1)
            pool.tensor_tensor(u.pair[1], u.dst, u.pair[0].bitcast(F32), ALU.subtract)

        @block.gpsimd
        def _(pool):
            for c in first:
                ring.split_low(pool, c)
            for n, u in enumerate(units):
                for c in after[n]:
                    ring.split_low(pool, c)
                if n - 1 in paired:
                    low(pool, n - 1)
            if len(units) - 1 in paired:
                low(pool, len(units) - 1)

        @block.tensor
        def _(pe):
            def tile_ready(k):
                if k % 2 == 0:
                    pe.wait_ge(s["x_low"], k // 2 + 1)

            seen = 0
            for n, u in enumerate(units):
                if n >= NB:
                    pe.wait_ge(free[n % NB], n // NB)
                while seen < len(others) and u.x is others[seen][1]:
                    seen += 1
                    pe.wait_ge(s["x_low"], len(slices) + seen)
                w = ring.arrive(pe, base + n)
                unit_product(pe, bank[n % NB], w, x if u.x is None else u.x, u.tokens,
                             tile_ready if sliced and n == 0 else None).then_inc(ring.product, 1)

        @block.scalar
        def _(act):
            def early(n):
                u = units[n]
                fr = free[n % NB]
                if u.kind in ("act", "rows", "conv"):
                    act.wait_ge(ring.product, base + n + 1)
                v = view(n)
                if u.kind == "rows":
                    for p0, count, dst in u.more:
                        ins = act.activation(dst, v[p0:p0 + count, 0, :], ACT.Copy)
                    if u.dst is not None:
                        ins = act.activation(u.dst, v[:, 1, :], ACT.Copy)
                    ins.then_inc(fr, 1)
                elif u.kind == "act":
                    func, bias = u.more
                    if bias is None:
                        act.activation(u.dst, v, func).then_inc(fr, 1)
                    else:
                        act.activation(u.dst[:, 0, :], v[:, 0, :], func, bias=bias[:, 0:1])
                        act.activation(u.dst[:, 1, :], v[:, 1, :], func, bias=bias[:, 1:2]).then_inc(fr, 1)
                elif u.kind == "conv":
                    taps, wts, bs, c0, finish = u.more
                    i = conv.index(n)
                    if i >= 2:
                        act.wait_ge(s["finished"], i - 1)
                    for j in range(2):
                        c = c0 + j
                        cb = b["cb"][:, i % 2, j, :]
                        if bs is None:
                            ins = act.activation(cb, v[:, j, :], ACT.Copy, scale=wts[:, taps - 1, c:c + 1])
                        else:
                            ins = act.activation(cb, v[:, j, :], ACT.Identity, scale=wts[:, taps - 1, c:c + 1],
                                                 bias=bs[:, c:c + 1])
                    ins.then_inc(s["affine"], 1)

            def late(n):
                u = units[n]
                if u.kind == "conv" and u.more[4] == "silu":
                    act.wait_ge(free[n % NB], n // NB + 1)
                    act.activation(u.dst, b["cb"][:, conv.index(n) % 2, :, :], ACT.Silu).then_inc(s["finished"], 1)
                if u.pair is not None:
                    act.wait_ge(s["timed"], paired.index(n) + 1)
                    act.activation(u.pair[0], u.dst, ACT.Copy).then_inc(s["pair_high"], 1)

            for src, pair in slices:
                act.activation(pair[0], src, ACT.Copy).then_inc(s["x_high"], 1)
            for c in first:
                ring.split_high(act, c)
            for n in range(len(units)):
                if n:
                    early(n - 1)
                for c in after[n]:
                    ring.split_high(act, c)
                if n in during:
                    src, pair = during[n]
                    act.activation(pair[0], src, ACT.Copy).then_inc(s["x_high"], 1)
                if n:
                    late(n - 1)
            early(len(units) - 1)
            late(len(units) - 1)

        @block.vector
        def _(dve):
            chain = Chain(dve, s["dve_step"])

            def empty(n):
                u = units[n]
                fr = free[n % NB]
                v = view(n)
                if u.kind == "conv":
                    taps, wts, bs, c0, finish = u.more
                    i = conv.index(n)
                    dve.wait_ge(s["affine"], i + 1)
                    for tap in range(1, taps):
                        for j in range(2):
                            c = c0 + j
                            ins = dve.scalar_tensor_tensor(b["cb"][:, i % 2, j, tap:T], v[:, j, 0:T - tap],
                                                           wts[:, taps - 1 - tap, c:c + 1], b["cb"][:, i % 2, j, tap:T],
                                                           ALU.mult, ALU.add)
                        if tap < taps - 1:
                            chain.step(ins)
                        else:
                            ins.then_inc(fr, 1)
                    if finish == "times":
                        dve.wait_ge(fr, n // NB + 1)
                        dve.wait_ge(s["finished"], i)
                        dve.tensor_tensor(u.dst, u.dst, b["cb"][:, i % 2, :, :], ALU.mult).then_inc(s["finished"], 1)
                        if u.pair is not None:
                            dve.wait_ge(s["finished"], i + 1)
                            dve.sem_inc(s["timed"], 1)
                elif u.kind == "times":
                    dve.wait_ge(ring.product, base + n + 1)
                    gate = next(m for m in range(n) if units[m].dst is u.dst)
                    dve.wait_ge(free[gate % NB], gate // NB + 1)
                    dve.tensor_tensor(u.dst, u.dst, v, ALU.mult).then_inc(fr, 1)
                    if u.pair is not None:
                        dve.wait_ge(fr, n // NB + 1)
                        dve.sem_inc(s["timed"], 1)
                elif u.kind == "residual":
                    dve.wait_ge(ring.product, base + n + 1)
                    dve.scalar_tensor_tensor(u.dst, u.dst, u.more, v, ALU.mult, ALU.add).then_inc(fr, 1)
                elif u.kind in ("gate_first", "gate_add"):
                    dve.wait_ge(ring.product, base + n + 1)
                    gate = max(m for m in range(n) if units[m].dst is u.more)
                    dve.wait_ge(free[gate % NB], gate // NB + 1)
                    if u.kind == "gate_first":
                        chain.step(dve.tensor_tensor(u.dst, u.more, v, ALU.mult))
                        dve.sem_inc(fr, 1)
                    else:
                        chain.step(dve.tensor_tensor(u.more, u.more, v, ALU.mult))
                        dve.sem_inc(fr, 1)
                        chain.step(dve.tensor_tensor(u.dst, u.dst, u.more, ALU.add))

            for i, (src, pair) in enumerate(slices):
                dve.wait_ge(s["x_high"], i + 1)
                dve.tensor_tensor(pair[1], src, pair[0].bitcast(F32), ALU.subtract).then_inc(s["x_low"], 1)
            for c in first:
                ring.split_low(dve, c)
            for n in range(len(units)):
                if n:
                    empty(n - 1)
                for c in after[n]:
                    ring.split_low(dve, c)
                if n in during:
                    src, pair = during[n]
                    dve.wait_ge(s["x_high"], len(slices) + n // 2 + 1)
                    dve.tensor_tensor(pair[1], src, pair[0].bitcast(F32), ALU.subtract).then_inc(s["x_low"], 1)
            empty(len(units) - 1)


class Fill:

    names = " fill_free0 fill_free1"
    banks = [("fill0", HALF), ("fill1", HALF)]
    PARTS = 4

    def __init__(self, ring, units, x, s, b, banks=2):
        self.ring, self.units, self.x, self.nb = ring, units, x, banks
        self.base, self.todo = ring.plan([u.chunk for u in units])
        self.free = [s[f"fill_free{i}"] for i in range(banks)] if units else []
        self.bank = [b[f"fill{i}"] for i in range(banks)] if units else []
        self.parts = 0
        self.stepped = 0

    def pe(self, pe, parts=None):
        total = self.PARTS * len(self.units)
        end = total if parts is None else min(total, self.parts + parts)
        for at in range(self.parts, end):
            n, part = at // self.PARTS, at % self.PARTS
            i, u = part // 2, self.units[n]
            if part == 0:
                if n >= self.nb:
                    pe.wait_ge(self.free[n % self.nb], n // self.nb)
                self.w = self.ring.arrive(pe, self.base + n)
            x = self.x if u.x is None else u.x
            for k in range((part % 2) * KD // 2, (part % 2 + 1) * KD // 2):
                still, moving = (x, self.w) if u.tokens else (self.w, x)
                mm = passes(pe, self.bank[n % self.nb][:, i * 256:(i + 1) * 256],
                            [v[:, k, i * P:(i + 1) * P] for v in still], [v[:, k, :] for v in moving],
                            k == 0, k == KD - 1)
            if part == self.PARTS - 1:
                mm.then_inc(self.ring.product, 1)
        self.parts = end

    def empty(self, act, n):
        act.wait_ge(self.ring.product, self.base + n + 1)
        act.activation(self.units[n].dst, self.bank[n % self.nb][:, :].rearrange("p (i t) -> p i t", i=2), ACT.Copy
                       ).then_inc(self.free[n % self.nb], 1)

    def act(self, act, count=None, last=False):
        end = len(self.units) if count is None else min(len(self.units), self.stepped + count)
        for n in range(self.stepped, end):
            if n:
                self.empty(act, n - 1)
            if self.base + n + 1 in self.todo:
                self.ring.split_high(act, self.base + n + 1)
        self.stepped = end
        if last and self.units:
            self.empty(act, len(self.units) - 1)

    def first_chunk(self, act):
        if not self.units:
            for c in self.todo:
                self.ring.split_high(act, c)

    def pool(self, pool):
        for c in self.todo:
            self.ring.split_low_all(pool, c)


def down_phase(nc, ring, layer, names, h, x, scale):
    base, todo = ring.plan(names)
    with phase(nc, "", (), [(f"y{i}", HALF) for i in range(4)]) as (block, s, b):
        y = [b["y0"], b["y1"], b["y2"], b["y3"]]

        @block.sync
        def _(sp):
            ring.send(sp, layer)

        @block.scalar
        def _(act):
            for c in todo:
                ring.split_high(act, c)

        @block.gpsimd
        def _(pool):
            for c in todo:
                ring.split_low(pool, c)

        @block.tensor
        def _(pe):
            for n in range(len(names)):
                w = ring.arrive(pe, base + n)
                for kk in range(2):
                    k = 2 * n + kk
                    for j in range(KD):
                        mm = passes(pe, y[j // 2][:, (j % 2) * 256:(j % 2) * 256 + 256],
                                    [v[:, kk, j * P:(j + 1) * P] for v in w], [v[:, k, :] for v in h],
                                    k == 0 and j % 2 == 0, k == KF - 1, True)
                mm.then_inc(ring.product, 1)

        @block.vector
        def _(dve):
            for c in todo:
                ring.split_low(dve, c)
            dve.wait_ge(ring.product, base + len(names))
            for i in range(4):
                xs = x[:, 2 * i:2 * i + 2, :]
                dve.scalar_tensor_tensor(xs, xs, scale, y[i][:, :].rearrange("p (i t) -> p i t", i=2),
                                         ALU.mult, ALU.add)


def rope_phase(nc, K, jobs, ring, layer, units=(), x=None):
    with phase(nc, "rotated read0 read1 dve_step done" + Fill.names, [("c0", [P, 2, 256]), ("c1", [P, 2, 256]), ("r", [P, 2, 2, 256])],
               [("rot0", HALF), ("rot1", HALF)] + Fill.banks) as (block, s, b):
        fill = Fill(ring, units, x, s, b)
        rot, read, cb = [b["rot0"], b["rot1"]], [s["read0"], s["read1"]], [b["c0"], b["c1"]]

        @block.sync
        def _(sp):
            ring.send(sp, layer)

        @block.gpsimd
        def _(pool):
            fill.pool(pool)

        @block.scalar
        def _(act):
            fill.act(act, last=True)

        @block.tensor
        def _(pe):
            for n, (raw, perm, cos, sin) in enumerate(jobs):
                if n >= 2:
                    pe.wait_ge(read[n % 2], n // 2)
                w = raw.shape[1]
                pe.matmul(rot[n % 2][:, 0:w * 256], perm, raw.rearrange("p i t -> p (i t)"),
                          start=True, stop=True).then_inc(s["rotated"], 1)
                if n:
                    fill.pe(pe, 1)
            fill.pe(pe)

        @block.vector
        def _(dve):
            chain = Chain(dve, s["dve_step"])
            for n, (raw, perm, cos, sin) in enumerate(jobs):
                w = raw.shape[1]
                dve.wait_ge(s["rotated"], n + 1)
                r = b["r"][:, n % 2, 0:w, :]
                dve.tensor_tensor(r, rot[n % 2][:, 0:w * 256].rearrange("p (i t) -> p i t", i=w),
                                  sin.unsqueeze(1).to_broadcast([P, w, 256]), ALU.mult).then_inc(read[n % 2], 1)
                chain.step(dve.tensor_tensor(raw, raw, cos.unsqueeze(1).to_broadcast([P, w, 256]), ALU.mult))
                dve.wait_ge(read[n % 2], n // 2 + 1)
                dve.tensor_tensor(raw, raw, r, ALU.add)


def pair_slot(h):
    return (h % 2) * 2 + h // 2


class Group:

    def __init__(self, nk, scale, pairs, slot, mask, value, place, dst):
        self.nk, self.scale, self.pairs, self.slot = nk, scale, pairs, slot
        self.mask, self.value, self.place, self.dst = mask, value, place, dst


def attention_phase(nc, K, groups, ring, layer, units=(), x=None):
    with phase(nc, "scored masked shifted exped normed turned turned_out pv read_s0 read_s1 copied dve_step act_step "
                   "p_free out_free" + Fill.names,
               [("sm", [P, 2, 4, 256]), ("pt", [P, 2, 8, P]), ("mx", [P, 2, 4]), ("sum", [P, 2, 4]), ("rc", [P, 2, 4])],
               [("s0", 2 * HALF), ("s1", 2 * HALF), ("tp", 2 * HALF), ("o", HALF if units else 2 * HALF)]
               + (Fill.banks[:1] if units else [])) as (block, s, b):
        fill = Fill(ring, units, x, s, b, banks=1)
        sc = [b["s0"], b["s1"]]

        @block.sync
        def _(sp):
            ring.send(sp, layer)

        @block.gpsimd
        def _(pool):
            fill.pool(pool)

        @block.tensor
        def _(pe):
            def scores(n):
                g = groups[n]
                if n >= 2:
                    pe.wait_ge(s["masked"], n - 1)
                for h in range(4):
                    pairs = g.pairs(h)
                    at = g.slot(h) * 256
                    for i, (lhs, rhs) in enumerate(pairs):
                        mm = pe.matmul(sc[n % 2][:, at:at + g.nk], lhs, rhs,
                                       start=(i == 0), stop=(i == len(pairs) - 1))
                mm.then_inc(s["scored"], 1)

            scores(0)
            scores(1)
            for n, g in enumerate(groups):
                kts = g.nk // P
                fill.pe(pe, Fill.PARTS)
                pe.wait_ge(s["normed"], n + 1)
                if n:
                    pe.wait_ge(s["copied"], n)
                for h in range(4):
                    for kt in range(kts):
                        mm = pe.transpose(b["tp"][:, (h * 2 + kt) * P:(h * 2 + kt + 1) * P],
                                          b["sm"][:, n % 2, h, kt * P:(kt + 1) * P], K("ident"))
                mm.then_inc(s["turned"], 1)
                if n + 2 < len(groups):
                    scores(n + 2)
                pe.wait_ge(s["copied"], n + 1)
                if n:
                    pe.wait_ge(s["out_free"], n)
                for h in range(4):
                    for i, region in enumerate(g.place(b["o"], h)):
                        for kt in range(kts):
                            mm = pe.matmul(region, g.value(h, kt)[i], b["pt"][:, n % 2, g.slot(h) * 2 + kt, :],
                                           start=(kt == 0), stop=(kt == kts - 1))
                mm.then_inc(s["pv"], 1)

        @block.vector
        def _(dve):
            chain = Chain(dve, s["dve_step"])

            def weigh(n):
                g = groups[n]
                sm = b["sm"][:, n % 2, :, 0:g.nk]
                v = sc[n % 2][:, :].rearrange("p (h k) -> p h k", h=4)[:, :, 0:g.nk]
                dve.wait_ge(s["scored"], n + 1)
                if n >= 2:
                    dve.wait_ge(s["turned"], n - 1)
                if g.mask is None:
                    ins = dve.tensor_copy(sm, v)
                else:
                    ins = dve.tensor_tensor(sm, v, g.mask if g.mask.shape[1] == 4 else g.mask.to_broadcast([P, 4, g.nk]),
                                            ALU.add)
                ins.then_inc(s["masked"], 1)
                dve.wait_ge(s["masked"], n + 1)
                chain.step(dve.tensor_reduce(b["mx"][:, n % 2, :], sm, AX_X, ALU.max))
                dve.tensor_scalar(b["mx"][:, n % 2, :], b["mx"][:, n % 2, :], -g.scale, None, ALU.mult).then_inc(s["shifted"], 1)

            def normalise(n):
                g = groups[n]
                sm = b["sm"][:, n % 2, :, 0:g.nk]
                dve.wait_ge(s["exped"], 4 * (n + 1))
                chain.step(dve.reciprocal(b["rc"][:, n % 2, :], b["sum"][:, n % 2, :]))
                dve.tensor_tensor(sm, sm, b["rc"][:, n % 2, :].unsqueeze(2).to_broadcast([P, 4, g.nk]),
                                  ALU.mult).then_inc(s["normed"], 1)

            def store(n):
                dve.wait_ge(s["pv"], n + 1)
                for region, dst in groups[n].dst(b["o"]):
                    ins = dve.tensor_copy(dst, region)
                ins.then_inc(s["out_free"], 1)

            weigh(0)
            weigh(1)
            for n in range(len(groups)):
                normalise(n)
                if n:
                    store(n - 1)
                if n + 2 < len(groups):
                    weigh(n + 2)
            store(len(groups) - 1)

        @block.scalar
        def _(act):
            def exponentials(n):
                g = groups[n]
                act.wait_ge(s["shifted"], n + 1)
                for h in range(4):
                    act.activation(b["sm"][:, n % 2, h, 0:g.nk], b["sm"][:, n % 2, h, 0:g.nk], ACT.Exp,
                                   bias=b["mx"][:, n % 2, h:h + 1], scale=g.scale,
                                   accum_out=b["sum"][:, n % 2, h:h + 1]).then_inc(s["exped"], 1)

            fill.act(act, 1)
            exponentials(0)
            exponentials(1)
            for n, g in enumerate(groups):
                act.wait_ge(s["turned"], n + 1)
                if n >= 2:
                    act.wait_ge(s["pv"], n - 1)
                tp = b["tp"][:, :].rearrange("p (h k q) -> p h k q", h=4, k=2)[:, :, 0:g.nk // P, :]
                pt = b["pt"][:, n % 2, :, :].rearrange("p (h k) q -> p h k q", h=4)[:, :, 0:g.nk // P, :]
                act.activation(pt, tp, ACT.Copy).then_inc(s["copied"], 1)
                if n + 1 < len(groups):
                    fill.act(act, 1)
                if n + 2 < len(groups):
                    exponentials(n + 2)
            fill.act(act, last=True)


def side_phase(nc, K, prm, sgu_rows, buf, ring, layer):
    c8 = 2 * 4
    with phase(nc, "negc spread tril gates exped logged summed rooted vn mixed band pooled pmix dve_step act_step",
               [("wT", [P, 4, P]), ("lf", [4, 3, T]), ("on", [4, T]), ("m", [P, c8]), ("ms", [P, c8]), ("sd", [P, c8]),
                ("cen", [P, c8, 64]), ("sq", [P, c8, 64]), ("pooled", [P, 2, 256])],
               [("mix", HALF), ("pb", HALF), ("pm", HALF), ("c", 2 * HALF)]) as (block, s, b):

        @block.sync
        def _(sp):
            ring.send(sp, layer)

        @block.gpsimd
        def _(pool):
            pool.affine_select(out=b["wT"][:, :, :], in_=prm("sgu_wT").rearrange("p (g t) -> p g t", g=4),
                               compare_op=ALU.is_ge, fill=0.0, base=0, pattern=[[0, 4], [1, P]],
                               channel_multiplier=-1).then_inc(s["tril"], 1)

        @block.vector
        def _(dve):
            chain = Chain(dve, s["dve_step"])
            y, ab, lf = b["lf"][:, 0, :], b["lf"][:, 1, :], b["lf"][:, 2, :]
            dve.memset(b["on"][:, :], 1.0)
            chain.step(dve.tensor_scalar(y, buf["bf"][:, :], prm("b_forget")[0:4, :], None, ALU.add))
            chain.step(dve.tensor_scalar(ab, y, -1.0, None, ALU.mult))
            dve.tensor_tensor(ab, y, ab, ALU.max).then_inc(s["gates"], 1)
            cv = buf["cv"].rearrange("p t (g c) -> p (t g) c", g=4)
            chain.step(dve.tensor_reduce(b["m"][:, :], cv, AX_X, ALU.add))
            chain.step(dve.tensor_scalar(b["m"][:, :], b["m"][:, :], 1.0 / 64, None, ALU.mult))
            chain.step(dve.tensor_tensor(b["cen"][:, :, :], cv, b["m"][:, :].unsqueeze(2).to_broadcast([P, c8, 64]),
                                         ALU.subtract))
            chain.step(dve.tensor_tensor(b["sq"][:, :, :], b["cen"][:, :, :], b["cen"][:, :, :], ALU.mult))
            chain.step(dve.tensor_reduce(b["ms"][:, :], b["sq"][:, :, :], AX_X, ALU.add))
            dve.tensor_scalar(b["ms"][:, :], b["ms"][:, :], 1.0 / 64, LN_EPS, ALU.mult, ALU.add).then_inc(s["summed"], 1)
            dve.wait_ge(s["logged"], 1)
            chain.step(dve.scalar_tensor_tensor(lf, y, 0.0, lf, ALU.min, ALU.subtract))
            chain.step(dve.tensor_tensor_scan(y, b["on"][:, :], lf, 0.0, ALU.mult, ALU.add))
            dve.tensor_scalar(buf["negc"][:, :], y, -8.0, None, ALU.mult).then_inc(s["negc"], 1)
            dve.wait_ge(s["rooted"], 1)
            chain.step(dve.reciprocal(b["sd"][:, :], b["sd"][:, :]))
            chain.step(dve.tensor_tensor(b["cen"][:, :, :], b["cen"][:, :, :],
                                         b["sd"][:, :].unsqueeze(2).to_broadcast([P, c8, 64]), ALU.mult))
            cen = b["cen"][:, :, :].rearrange("p (t g) c -> p t (g c)", t=2)
            chain.step(dve.tensor_tensor(cen, cen, sgu_rows[:, 0:256].unsqueeze(1).to_broadcast([P, 2, 256]), ALU.mult))
            dve.tensor_tensor(cen, cen, sgu_rows[:, 256:512].unsqueeze(1).to_broadcast([P, 2, 256]),
                              ALU.add).then_inc(s["vn"], 1)
            dve.wait_ge(s["spread"], 1)
            for q in range(TT):
                dve.tensor_tensor(buf["forget"][:, q, :, :], b["c"][:, :].rearrange("p (h k) -> p h k", h=4),
                                  K("causal").rearrange("p (q k) -> p q k", q=2)[:, q:q + 1, :].to_broadcast([P, 4, T]),
                                  ALU.add)
            dve.wait_ge(s["mixed"], 1)
            dve.tensor_tensor(buf["yT"][:, 4:6, :], buf["cu"], b["mix"][:, :].rearrange("p (i t) -> p i t", i=2), ALU.mult)

        @block.scalar
        def _(act):
            act.preload_act_table_set("natural_log_exp_and_others")
            act.wait_ge(s["gates"], 1)
            act.activation(b["lf"][:, 2, :], b["lf"][:, 1, :], ACT.Exp, scale=-1.0).then_inc(s["exped"], 1)
            act.wait_ge(s["exped"], 1)
            act.activation(b["lf"][:, 2, :], b["lf"][:, 2, :], ACT.Ln, bias=1.0).then_inc(s["logged"], 1)
            act.wait_ge(s["summed"], 1)
            act.activation(b["sd"][:, :], b["ms"][:, :], ACT.Sqrt).then_inc(s["rooted"], 1)
            act.wait_ge(s["band"], 1)
            act.activation(b["pooled"][:, :, :], b["pb"][:, :].rearrange("p (i t) -> p i t", i=2), ACT.Copy).then_inc(s["pooled"], 1)
            act.wait_ge(s["pmix"], 1)
            for i in range(2):
                act.activation(buf["yT"][:, 6 + i, :], b["pm"][:, i * 256:(i + 1) * 256], ACT.Copy,
                               scale=prm("pool_scale")[:, i:i + 1])

        @block.tensor
        def _(pe):
            band = K("band").rearrange("p (s g t) -> p s g t", s=2, g=4)
            for g in range(4):
                r = slice((g % 2) * 64, (g % 2) * 64 + 64)
                for st in range(2):
                    mm = pe.matmul(b["pb"][r, (g // 2) * 256:(g // 2) * 256 + 256], buf["dp"][:, st, g * 64:(g + 1) * 64],
                                   band[:, st, g, :], start=(st == 0), stop=(st == 1))
            mm.then_inc(s["band"], 1)
            pe.wait_ge(s["pooled"], 1)
            pw = prm("pool_w").rearrange("p (i d) -> p i d", i=2)
            for g in range(4):
                r = slice((g % 2) * 64, (g % 2) * 64 + 64)
                mm = pe.matmul(b["pm"][r, (g // 2) * 256:(g // 2) * 256 + 256], pw[r, g // 2, :], b["pooled"][r, g // 2, :],
                               start=True, stop=True)
            mm.then_inc(s["pmix"], 1)
            pe.wait_ge(s["negc"], 1)
            for h in range(4):
                mm = pe.matmul(b["c"][:, pair_slot(h) * 256:(pair_slot(h) + 1) * 256],
                               K("select").rearrange("p (h m) -> p h m", h=8)[0:4, h, :], buf["negc"][:, :],
                               start=True, stop=True)
            mm.then_inc(s["spread"], 1)
            pe.wait_ge(s["tril"], 1)
            pe.wait_ge(s["vn"], 1)
            vn = b["cen"][:, :, :].rearrange("p (t g) c -> p t g c", t=2)
            for g in range(4):
                r = slice((g % 2) * 64, (g % 2) * 64 + 64)
                for tt in range(TT):
                    region = b["mix"][r, (g // 2) * 256 + tt * P:(g // 2) * 256 + (tt + 1) * P]
                    pe.matmul(region, vn[:, tt, g, :], b["wT"][:, g, :], start=True, stop=False)
                    mm = pe.matmul(region, K("ones")[0:1, 0:64], prm("sgu_b")[0:1, g * P:(g + 1) * P],
                                   start=False, stop=True)
            mm.then_inc(s["mixed"], 1)


def pair_of(nc, ctx, name, tiles):
    return [ctx.enter_context(nc.sbuf_tensor(f"{name}_{part}", [P, tiles, T], F32R))[:, :, :] for part in ("hi", "lo")]


def first_layer(nc, K, layer, x, xs, ring, par_dram, rows_dram):
    with ExitStack() as ctx:
        par = ctx.enter_context(nc.sbuf_tensor("par1_sb", [P, NPC1], F32))
        rows = ctx.enter_context(nc.sbuf_tensor("rows1_sb", [P, 512], F32))
        yT = ctx.enter_context(nc.sbuf_tensor("yT", [P, KD, T], F32))[:, :, :]
        prm = lambda name: par[:, PC1[name]]
        loads = [(par[:, :], par_dram[bass.ds(layer, 1), :, :].rearrange("o p n -> (o p) n")),
                 (rows[:, :], rows_dram[bass.ds(layer, 1), :].to_broadcast([P, 512]))]
        with ExitStack() as mix:
            def sb(name, shape):
                return mix.enter_context(nc.sbuf_tensor(name, shape, F32))

            buf = {"yT": yT}
            aqk, bqk = sb("aqk", [P, 4, T]), sb("bqk", [P, 4, T])
            av, bv = sb("av", [P, 2, 256]), sb("bv", [P, 2, 256])
            buf["bf"], buf["negc"], buf["forget"] = sb("bf", [4, T]), sb("negc", [4, T]), sb("forget", [P, 2, 4, T])
            buf["cu"], buf["cv"], buf["dp"] = (sb(n, [P, 2, 256])[:, :, :] for n in ("cu", "cv", "dp"))
            copy = (ACT.Copy, None)
            gelu = (ACT.Gelu, None)
            product_phase(nc, ring, layer, [
                U("in0", "act", aqk[:, 0:2, :], copy), U("in1", "act", aqk[:, 2:4, :], copy),
                U("in2", "act", av[:, :, :], copy, tokens=True), U("in3", "act", bqk[:, 0:2, :], copy),
                U("in4", "act", bqk[:, 2:4, :], copy), U("in5", "act", bv[:, :, :], copy, tokens=True),
                U("gate_row", "rows", None, [(0, 4, buf["bf"][:, :])]),
                U("in6", "act", buf["cu"], gelu), U("in7", "act", buf["cv"], gelu, tokens=True),
                U("in8", "act", buf["dp"], copy, tokens=True)], xs, loads=loads)
            rope_phase(nc, K, [(aqk[:, 2 * i:2 * i + 2, :], K("perm64"), K("cos"), K("sin")) for i in range(2)],
                       ring, layer)
            side_phase(nc, K, prm, rows, buf, ring, layer)

            def group(qk, v, y0, q0, forget):
                nk = q0 + P
                causal = K("causal").rearrange("p (q k) -> p q k", q=2)[:, q0 // P:q0 // P + 1, 0:nk]

                def pairs(h):
                    r = slice((h % 2) * 64, (h % 2) * 64 + 64)
                    return [(qk[r, h // 2, q0:q0 + P], qk[r, 2 + h // 2, 0:nk])]

                return Group(
                    nk=nk, scale=0.125, pairs=pairs, slot=pair_slot,
                    mask=buf["forget"][:, q0 // P, :, 0:nk] if forget else causal,
                    value=lambda h, kt: [v[:, kt, h * 64:(h + 1) * 64]],
                    place=lambda o, h: [o[(h % 2) * 64:(h % 2) * 64 + 64, (h // 2) * P:(h // 2 + 1) * P]],
                    dst=lambda o: [(o[:, 0:256].rearrange("p (i q) -> p i q", i=2), yT[:, y0:y0 + 2, q0:q0 + P])])

            attention_phase(nc, K, [group(aqk, av, 0, 0, False), group(aqk, av, 0, P, False),
                                    group(bqk, bv, 2, 0, True), group(bqk, bv, 2, P, True)], ring, layer)

        with ExitStack() as st:
            ys = pair_of(nc, st, "y_split", KD)
            product_phase(nc, ring, layer, [U(f"o{i}", "residual", x[:, 2 * i:2 * i + 2, :], ALPHA) for i in range(4)], ys,
                          splits=[(yT, ys)])
        norm_phase(nc, K, x, x, prm("ln1_g"), prm("ln1_b"), LN_EPS, False, pair=xs, ring=ring, layer=layer)
        with ExitStack() as st:
            hid = st.enter_context(nc.sbuf_tensor("hid1", [P, KF, T], F32))
            hs = pair_of(nc, st, "hid1_split", KF)
            taps = prm("conv_w").rearrange("p (j c) -> p j c", j=3)
            hv = [hid[:, 2 * i:2 * i + 2, :] for i in range(KF // 2)]
            hp = [[v[:, 2 * i:2 * i + 2, :] for v in hs] for i in range(KF // 2)]
            product_phase(nc, ring, layer, [
                U(f"up{i}", "conv", hv[i % 11], (3, taps, prm("conv_b"), 2 * i, "silu" if i < 11 else "times"),
                  pair=hp[i % 11] if i >= 11 else None) for i in range(KF)], xs)
            down_phase(nc, ring, layer, [f"down{i}" for i in range(11)], hs, x, ALPHA)
        ring.clear(nc)
        norm_phase(nc, K, x, x, prm("ln2_g"), prm("ln2_b"), LN_EPS, False, pair=xs, ring=ring, layer=layer + 1, head=True)
        ring.resume()


def begin_phase(nc, x, pair, x_dram, constants, ring=None):
    todo = ring.plan([])[1] if ring is not None else ()
    with phase(nc, "x constants high") as (block, s, b):
        @block.sync
        def _(sp):
            sp.dma_start(x, x_dram).then_inc(s["x"], 16)
            if ring is not None:
                ring.send_head(sp, 0, 1)
            for dst, src in constants:
                sp.dma_start(dst, src).then_inc(s["constants"], 16)
            if ring is not None:
                ring.send_head(sp, 0)
            sp.wait_ge(s["constants"], 16 * len(constants))

        @block.scalar
        def _(act):
            act.wait_ge(s["x"], 16)
            act.activation(pair[0], x, ACT.Copy).then_inc(s["high"], 1)
            for c in todo:
                ring.split_high(act, c)

        @block.gpsimd
        def _(pool):
            for c in todo:
                ring.split_low_all(pool, c)

        @block.vector
        def _(dve):
            dve.wait_ge(s["high"], 1)
            dve.tensor_tensor(pair[1], x, pair[0].bitcast(F32), ALU.subtract)


def chunked(parts, chunks):
    out = []
    for name, (w, row, col) in zip(chunks, parts):
        k, c = columns_of(name)
        a = w[:, row:row + k * P, col:col + c]
        out.append(a.reshape(a.shape[0], k, P, c).transpose(0, 2, 1, 3).reshape(a.shape[0], P, k * c))
    return np.ascontiguousarray(np.concatenate(out, axis=2))


def head_and_rest(w, chunks):
    at = sum(k * c for k, c in (columns_of(n) for n in chunks[:SLOTS]))
    head = np.zeros((DEPTH + 1, P, at), np.float32)
    head[:DEPTH] = w[:, :, :at]
    return head, np.ascontiguousarray(w[:, :, at:])


def lay_first(i):
    w_in, w_o, w_up, w_down = i["w_in"], i["w_o"], i["w_up"], i["w_down"]
    gate = np.zeros((DEPTH, D, P), np.float32)
    gate[:, :, 0:4] = w_in[:, :, 1536:1540]
    parts = ([(w_in, 0, 256 * n) for n in range(6)] + [(gate, 0, 0)] + [(w_in, 0, 1540 + 256 * n) for n in range(3)]
             + [(w_o, 0, 256 * n) for n in range(4)] + [(w_up, 0, 256 * n) for n in range(22)]
             + [(w_down, 256 * n, 0) for n in range(11)])
    par = np.zeros((DEPTH, P, NPC1), np.float32)

    def cols(name, a):
        par[:, :, PC1[name]] = a.reshape(DEPTH, -1, P).transpose(0, 2, 1)

    for name in ("ln1_g", "ln1_b", "ln2_g", "ln2_b", "conv_b", "pool_scale"):
        cols(name, i[name])
    cols("conv_w", i["conv_w"].reshape(DEPTH, -1))
    par[:, 0:4, PC1["b_forget"]] = i["b_forget"][:, :, None]
    par[:, :, PC1["sgu_wT"]] = i["sgu_w"].transpose(0, 3, 1, 2).reshape(DEPTH, P, -1)
    par[:, 0, PC1["sgu_b"]] = i["sgu_b"].reshape(DEPTH, -1)
    par[:, :, PC1["pool_w"]] = i["pool_w"].reshape(DEPTH, 2, P, 64).transpose(0, 2, 1, 3).reshape(DEPTH, P, -1)
    rows = np.concatenate([i["sgu_ln_g"], i["sgu_ln_b"]], axis=1)
    return chunked(parts, CHUNKS_1), par, rows


def tiles_of(a):
    return np.ascontiguousarray(a.reshape(T, KD, P).transpose(2, 1, 0))


def angle_phase(nc, K, pos_dram, tables):
    magic = 1.5 * 2.0 ** 23
    c1 = 6.28125
    c2 = float(np.float32(2 * np.pi - c1).view(np.int32) // 4096 * 4096 and
               (np.float32(2 * np.pi - c1).view(np.int32) // 4096 * 4096).astype(np.int32).view(np.float32))
    c3 = 2 * np.pi - c1 - c2
    with phase(nc, "pos reduced sined dve_step",
               [("pos", [P, T]), ("k", [P, 2, T]), ("a", [P, 2, T]), ("h", [P, 2, T])]) as (block, s, b):
        posi = b["k"][:, 0, :].bitcast(I32)

        @block.sync
        def _(sp):
            sp.dma_start(posi, pos_dram.to_broadcast([P, T])).then_inc(s["pos"], 16)

        @block.vector
        def _(dve):
            chain = Chain(dve, s["dve_step"])
            dve.wait_ge(s["pos"], 16)
            chain.step(dve.tensor_copy(b["pos"][:, :], posi))
            for j in range(2):
                chain.step(dve.tensor_scalar(b["a"][:, j, :], b["pos"][:, :], K("freq")[:, j:j + 1], None, ALU.mult))
            a, k = b["a"][:, :, :], b["k"][:, :, :]
            chain.step(dve.tensor_scalar(k, a, 1.0 / (2 * np.pi), magic, ALU.mult, ALU.add))
            chain.step(dve.tensor_scalar(k, k, magic, None, ALU.subtract))
            for c in (c1, c2, c3):
                chain.step(dve.scalar_tensor_tensor(a, k, -c, a, ALU.mult, ALU.add))
            dve.tensor_scalar(a, a, 3.1415925, -3.1415925, ALU.min, ALU.max).then_inc(s["reduced"], 1)
            dve.wait_ge(s["sined"], 2)
            chain.step(dve.tensor_tensor(b["h"][:, :, :], b["h"][:, :, :], b["h"][:, :, :], ALU.mult))
            dve.tensor_scalar(tables[:, 0:2, :], b["h"][:, :, :], -2.0, 1.0, ALU.mult, ALU.add)

        @block.scalar
        def _(act):
            act.wait_ge(s["reduced"], 1)
            act.activation(tables[:, 2:4, :], b["a"][:, :, :], ACT.Sin).then_inc(s["sined"], 1)
            act.activation(b["h"][:, :, :], b["a"][:, :, :], ACT.Sin, scale=0.5).then_inc(s["sined"], 1)


QTY = 5


def decay_phase(nc, K, prm, small, ge, rowq, tokq, units, x, ring, layer):
    with phase(nc, "beta absed exped logged alog g gced ged rows turned dve_step act_step" + Fill.names,
               [("y", [8, T]), ("ab", [8, T]), ("lf", [8, T]), ("on", [8, T]), ("ea", [8, 1])],
               [("tq", HALF)] + Fill.banks) as (block, s, b):
        fill = Fill(ring, units, x, s, b)

        @block.sync
        def _(sp):
            ring.send(sp, layer)

        @block.vector
        def _(dve):
            chain = Chain(dve, s["dve_step"])
            y, ab, lf = b["y"][:, :], b["ab"][:, :], b["lf"][:, :]
            gc = rowq[:, 1, :]
            dve.memset(b["on"][:, :], 1.0)
            chain.step(dve.tensor_scalar(y, small[:, 1, :], prm("dt_bias")[0:8, :], None, ALU.add))
            chain.step(dve.tensor_scalar(ab, y, -1.0, None, ALU.mult))
            dve.tensor_tensor(ab, y, ab, ALU.max).then_inc(s["absed"], 1)
            dve.tensor_scalar(rowq[:, 4, :], small[:, 2, :], IDX_SCALE, None, ALU.mult)
            dve.wait_ge(s["logged"], 1)
            dve.wait_ge(s["alog"], 1)
            chain.step(dve.scalar_tensor_tensor(lf, y, 0.0, lf, ALU.max, ALU.add))
            chain.step(dve.tensor_scalar(lf, lf, b["ea"][:, 0:1], -1.0, ALU.mult, ALU.mult))
            for c in range(NCH):
                r = slice(c * CH, (c + 1) * CH)
                ins = dve.tensor_tensor_scan(rowq[:, 1, r], b["on"][:, r], lf[:, r], 0.0, ALU.mult, ALU.add)
            chain.step(ins)
            v = gc.rearrange("p (c i) -> p c i", c=NCH)
            dve.tensor_tensor(ab.rearrange("p (c i) -> p c i", c=NCH), v, v[:, :, CH - 1:CH].to_broadcast([8, NCH, CH]),
                              ALU.subtract).then_inc(s["gced"], 1)
            dve.wait_ge(s["ged"], 2)
            dve.wait_ge(s["beta"], 1)
            dve.tensor_tensor(rowq[:, 2, :], rowq[:, 0, :], ge, ALU.mult).then_inc(s["rows"], 1)
            dve.wait_ge(s["turned"], 1)
            dve.tensor_copy(tokq, b["tq"][:, 0:TT * QTY * 8].rearrange("p (t q h) -> p t q h", t=TT, q=QTY))

        @block.scalar
        def _(act):
            act.activation(rowq[:, 0, :], small[:, 0, :], ACT.Sigmoid).then_inc(s["beta"], 1)
            act.preload_act_table_set("natural_log_exp_and_others")
            act.activation(b["ea"][:, :], prm("a_log")[0:8, :], ACT.Exp).then_inc(s["alog"], 1)
            act.wait_ge(s["absed"], 1)
            act.activation(b["lf"][:, :], b["ab"][:, :], ACT.Exp, scale=-1.0).then_inc(s["exped"], 1)
            act.wait_ge(s["exped"], 1)
            act.activation(b["lf"][:, :], b["lf"][:, :], ACT.Ln, bias=1.0).then_inc(s["logged"], 1)
            fill.act(act, 1)
            act.wait_ge(s["gced"], 1)
            act.activation(ge, rowq[:, 1, :], ACT.Exp).then_inc(s["ged"], 1)
            act.activation(rowq[:, 3, :], b["ab"][:, :], ACT.Exp, scale=-1.0).then_inc(s["ged"], 1)
            fill.act(act, last=True)

        @block.gpsimd
        def _(pool):
            fill.pool(pool)

        @block.tensor
        def _(pe):
            fill.pe(pe)
            pe.wait_ge(s["rows"], 1)
            for tt in range(TT):
                for q in range(QTY):
                    at = (tt * QTY + q) * 8
                    mm = pe.transpose(b["tq"][:, at:at + 8], rowq[:, q, tt * P:(tt + 1) * P], K("ident")[0:8, 0:8])
            mm.then_inc(s["turned"], 1)


def unit_keys_phase(nc, K, q, k, units, x, ring, layer):
    jobs = [(v, i, sc) for v, sc in ((q, P ** -0.5), (k, 1.0)) for i in range(0, KD, 2)]
    with phase(nc, "squared summed logged inverted scaled" + Fill.names,
               [("sq", [P, 2, 2, T]), ("r", [P, 2, 2, T])], [("ss0", HALF), ("ss1", HALF)] + Fill.banks) as (block, s, b):
        fill = Fill(ring, units, x, s, b)
        ss = [b["ss0"], b["ss1"]]

        @block.sync
        def _(sp):
            ring.send(sp, layer)

        @block.tensor
        def _(pe):
            for n in range(len(jobs)):
                pe.wait_ge(s["squared"], n + 1)
                if n >= 2:
                    pe.wait_ge(s["logged"], n - 1)
                pe.matmul(ss[n % 2][:, :], K("ones"), b["sq"][:, n % 2, :, :].rearrange("p i t -> p (i t)"),
                          start=True, stop=True).then_inc(s["summed"], 1)
                if n in (2, 3, 4, 5):
                    fill.pe(pe, 1)
            fill.pe(pe)

        @block.gpsimd
        def _(pool):
            fill.pool(pool)

        @block.scalar
        def _(act):
            act.preload_act_table_set("natural_log_exp_and_others")
            for n in range(len(jobs)):
                r = b["r"][:, n % 2, :, :]
                act.wait_ge(s["summed"], n + 1)
                if n >= 2:
                    act.wait_ge(s["scaled"], n - 1)
                act.activation(r, ss[n % 2][:, :].rearrange("p (i t) -> p i t", i=2), ACT.Ln, bias=K("eps")
                               ).then_inc(s["logged"], 1)
                act.wait_ge(s["logged"], n + 1)
                act.activation(r, r, ACT.Exp, scale=-0.5).then_inc(s["inverted"], 1)
                if n == 1:
                    fill.act(act, 1)
            fill.act(act, last=True)

        @block.vector
        def _(dve):
            def square(n):
                v, i, sc = jobs[n]
                if n >= 2:
                    dve.wait_ge(s["summed"], n - 1)
                dve.tensor_tensor(b["sq"][:, n % 2, :, :], v[:, i:i + 2, :], v[:, i:i + 2, :], ALU.mult
                                  ).then_inc(s["squared"], 1)

            square(0)
            square(1)
            for n, (v, i, sc) in enumerate(jobs):
                if n + 2 < len(jobs):
                    square(n + 2)
                dve.wait_ge(s["inverted"], n + 1)
                dve.scalar_tensor_tensor(v[:, i:i + 2, :], b["r"][:, n % 2, :, :], sc, v[:, i:i + 2, :],
                                         ALU.mult, ALU.mult).then_inc(s["scaled"], 1)


NP = 8


def delta_prepare_phase(nc, K, hf, q, k, v, z, ge, rowq, tokq, h, ring, layer):
    sel = K("select").rearrange("p (h m) -> p h m", h=8)
    upper, strict = K("upper"), K("strict")
    with phase(nc, "turned read spread_g spread_e spread_b bread grams diffed exped masked dve_step eb_read gread",
               [("e", [P, NP, P]), ("es", [P, NP, P])],
               [("g0", HALF), ("g1", HALF), ("e0", HALF), ("e1", HALF), ("t0", HALF), ("t1", HALF), ("m0", HALF),
                ("m1", HALF)]) as (block, s, b):
        g, e, t, m = [b["g0"], b["g1"]], [b["e0"], b["e1"]], [b["t0"], b["t1"]], [b["m0"], b["m1"]]

        @block.sync
        def _(sp):
            ring.send(sp, layer)

        @block.tensor
        def _(pe):
            for hh in range(4):
                pe.matmul(g[hh // 2][:, (hh % 2) * T:(hh % 2 + 1) * T], sel[0:8, 4 * hf + hh, :], rowq[:, 1, :],
                          start=True, stop=True).then_inc(s["spread_g"], 1)
            for hh in range(4):
                mm = pe.matmul(e[hh // 2][:, (hh % 2) * T:(hh % 2 + 1) * T], sel[0:8, 4 * hf + hh, :], ge,
                               start=True, stop=True)
            mm.then_inc(s["spread_e"], 1)
            for n, src in enumerate((k, v)):
                for tt in range(TT):
                    if n:
                        pe.wait_ge(s["read"], 1 + tt)
                    for hh in range(4):
                        mm = pe.transpose(t[tt][:, hh * P:(hh + 1) * P], src[:, 4 * hf + hh, tt * P:(tt + 1) * P],
                                          K("ident"))
                    mm.then_inc(s["turned"], 1)
            pe.wait_ge(s["diffed"], 1)
            for hh in range(4):
                mm = pe.matmul(g[hh // 2][:, (hh % 2) * T:(hh % 2 + 1) * T], sel[0:8, 4 * hf + hh, :], rowq[:, 0, :],
                               start=True, stop=True)
            mm.then_inc(s["spread_b"], 1)
            for n, other in enumerate((q, k)):
                for tt in range(TT):
                    if n:
                        pe.wait_ge(s["gread"], 1 + tt)
                    for hh in range(4):
                        hd, c = 4 * hf + hh, slice(tt * P, (tt + 1) * P)
                        mm = pe.matmul(m[tt][:, hh * P:(hh + 1) * P], k[:, hd, c], other[:, hd, c], start=True, stop=True)
                    mm.then_inc(s["grams"], 1)

        @block.vector
        def _(dve):
            chain = Chain(dve, s["dve_step"])
            for hh in range(4):
                dve.wait_ge(s["spread_g"], 4)
                for tt in range(TT):
                    ins = dve.tensor_scalar(b["e"][:, tt * 4 + hh, :],
                                            g[hh // 2][:, (hh % 2) * T + tt * P:(hh % 2) * T + (tt + 1) * P],
                                            tokq[:, tt, 1, 4 * hf + hh:4 * hf + hh + 1], 0.0, ALU.subtract, ALU.min)
            ins.then_inc(s["diffed"], 1)
            dve.wait_ge(s["spread_e"], 1)
            for i in range(2):
                ev = e[i][:, :].rearrange("p (h t) -> p h t", h=2)
                dve.tensor_copy(h["ge"][:, 2 * i:2 * i + 2, :], ev)
                dve.tensor_tensor(h["qd"][:, 2 * i:2 * i + 2, :], q[:, 4 * hf + 2 * i:4 * hf + 2 * i + 2, :], ev, ALU.mult)

            def token(qty, tt):
                return tokq[:, tt, qty, 4 * hf:4 * hf + 4].unsqueeze(2).to_broadcast([P, 4, P])

            for tt in range(TT):
                dve.wait_ge(s["turned"], tt + 1)
                tv = t[tt][:, :].rearrange("p (h d) -> p h d", h=4)
                pr = slice(tt * 4, tt * 4 + 4)
                dve.tensor_tensor(h["kb"][:, pr, :], tv, token(2, tt), ALU.mult)
                dve.tensor_tensor(h["kd"][:, pr, :], tv, token(3, tt), ALU.mult).then_inc(s["read"], 1)
            for tt in range(TT):
                dve.wait_ge(s["turned"], TT + tt + 1)
                dve.tensor_tensor(h["vb"][:, tt * 4:tt * 4 + 4, :], t[tt][:, :].rearrange("p (h d) -> p h d", h=4),
                                  token(0, tt), ALU.mult)
            dve.wait_ge(s["exped"], 1)
            chain.step(dve.tensor_tensor(b["e"][:, :, :], b["e"][:, :, :], upper.unsqueeze(1).to_broadcast([P, NP, P]), ALU.mult))
            chain.step(dve.tensor_tensor(b["es"][:, :, :], b["e"][:, :, :], strict.unsqueeze(1).to_broadcast([P, NP, P]),
                                         ALU.mult))
            dve.wait_ge(s["spread_b"], 1)
            es = b["es"][:, :, :].rearrange("p (tt hh) i -> p hh tt i", tt=TT)
            for i in range(2):
                ins = dve.tensor_tensor(es[:, 2 * i:2 * i + 2, :, :], es[:, 2 * i:2 * i + 2, :, :],
                                        g[i][:, :].rearrange("p (hh tt i) -> p hh tt i", hh=2, tt=TT), ALU.mult)
            chain.step(ins)
            for tt in range(TT):
                dve.wait_ge(s["grams"], tt + 1)
                pr = slice(tt * 4, tt * 4 + 4)
                dve.tensor_tensor(h["at"][:, pr, :], m[tt][:, :].rearrange("p (h i) -> p h i", h=4), b["e"][:, pr, :],
                                  ALU.mult).then_inc(s["gread"], 1)
            for tt in range(TT):
                dve.wait_ge(s["grams"], TT + tt + 1)
                pr = slice(tt * 4, tt * 4 + 4)
                dve.tensor_tensor(h["mt"][:, pr, :], m[tt][:, :].rearrange("p (h i) -> p h i", h=4), b["es"][:, pr, :], ALU.mult)

        @block.scalar
        def _(act):
            act.wait_ge(s["diffed"], 1)
            act.activation(b["e"][:, :, :], b["e"][:, :, :], ACT.Exp).then_inc(s["exped"], 1)
            act.activation(z[:, 4 * hf:4 * hf + 4, :], z[:, 4 * hf:4 * hf + 4, :], ACT.Silu)


def delta_solve_phase(nc, K, h, ring, layer):
    ident = K("ident").unsqueeze(1).to_broadcast([P, 4, P])
    lev = K("levels").rearrange("p (l i) -> p l i", l=6)
    with phase(nc, "begun lower0 lower1 masked0 masked1 cross0 cross1 kept0 kept1 solved dve_step",
               [("t", [P, NP, P]), ("y", [P, NP, P])],
               [(f"{n}{i}", HALF) for n in ("y_ps", "d_ps", "c_ps") for i in range(2)]) as (block, s, b):
        yp, dp, cp = [b["y_ps0"], b["y_ps1"]], [b["d_ps0"], b["d_ps1"]], [b["c_ps0"], b["c_ps1"]]
        lower, masked = [s["lower0"], s["lower1"]], [s["masked0"], s["masked1"]]
        cross, kept = [s["cross0"], s["cross1"]], [s["kept0"], s["kept1"]]

        @block.sync
        def _(sp):
            ring.send(sp, layer)

        @block.tensor
        def _(pe):
            for g in range(2):
                for n in range(4 * g, 4 * g + 4):
                    mm = pe.transpose(yp[g][:, (n % 4) * P:(n % 4 + 1) * P], h["mt"][:, n, :], K("ident"))
                mm.then_inc(lower[g], 1)
            for lv in range(1, 6):
                for g in range(2):
                    pe.wait_ge(kept[g], 2 * lv)
                    for n in range(4 * g, 4 * g + 4):
                        mm = pe.matmul(yp[g][:, (n % 4) * P:(n % 4 + 1) * P], h["mt"][:, n, :], b["t"][:, n, :],
                                       start=True, stop=True)
                    mm.then_inc(lower[g], 1)
                for g in range(2):
                    pe.wait_ge(masked[g], lv + 1)
                    for n in range(4 * g, 4 * g + 4):
                        c = slice((n % 4) * P, (n % 4 + 1) * P)
                        if lv < 5:
                            pe.matmul(dp[g][:, c], h["ti"][:, n, :], b["y"][:, n, :], start=True, stop=True)
                        mm = pe.matmul(cp[g][:, c], b["y"][:, n, :], h["ti"][:, n, :], start=True, stop=True)
                    mm.then_inc(cross[g], 1)
            for g in range(2):
                pe.wait_ge(kept[g], 11)
                for n in range(4 * g, 4 * g + 4):
                    c = slice((n % 4) * P, (n % 4 + 1) * P)
                    pe.matmul(yp[g][:, c], h["ti"][:, n, :], h["vb"][:, n, :], start=True, stop=True)
                    mm = pe.matmul(dp[g][:, c], h["kb"][:, n, :], h["ti"][:, n, :], start=True, stop=True)
                mm.then_inc(s["solved"], 1)

        @block.vector
        def _(dve):
            for g in range(2):
                pr = slice(4 * g, 4 * g + 4)
                dve.tensor_tensor(h["ti"][:, pr, :], h["mt"][:, pr, :],
                                  K("level0T").unsqueeze(1).to_broadcast([P, 4, P]), ALU.mult).then_inc(s["begun"], 1)
            for g in range(2):
                pr = slice(4 * g, 4 * g + 4)
                dve.wait_ge(lower[g], 1)
                dve.tensor_tensor(b["t"][:, pr, :], yp[g][:, :].rearrange("p (n i) -> p n i", n=4),
                                  lev[:, 0:1, :].to_broadcast([P, 4, P]), ALU.mult).then_inc(masked[g], 1)
                dve.wait_ge(s["begun"], g + 1)
                dve.tensor_tensor(h["ti"][:, pr, :], ident, h["ti"][:, pr, :], ALU.subtract).then_inc(kept[g], 1)
                dve.wait_ge(masked[g], 1)
                dve.tensor_tensor(b["t"][:, pr, :], ident, b["t"][:, pr, :], ALU.subtract).then_inc(kept[g], 1)
            for lv in range(1, 6):
                for g in range(2):
                    pr = slice(4 * g, 4 * g + 4)
                    dve.wait_ge(lower[g], lv + 1)
                    dve.tensor_tensor(b["y"][:, pr, :], yp[g][:, :].rearrange("p (n i) -> p n i", n=4),
                                      lev[:, lv:lv + 1, :].to_broadcast([P, 4, P]), ALU.mult).then_inc(masked[g], 1)
                for g in range(2):
                    pr = slice(4 * g, 4 * g + 4)
                    dve.wait_ge(cross[g], lv)
                    dve.wait_ge(kept[g], 2 * lv)
                    dve.tensor_tensor(h["ti"][:, pr, :], h["ti"][:, pr, :], cp[g][:, :].rearrange("p (n i) -> p n i", n=4),
                                      ALU.subtract).then_inc(kept[g], 1)
                    if lv < 5:
                        dve.tensor_tensor(b["t"][:, pr, :], b["t"][:, pr, :], dp[g][:, :].rearrange("p (n i) -> p n i", n=4),
                                          ALU.subtract).then_inc(kept[g], 1)
            for g in range(2):
                dve.wait_ge(s["solved"], g + 1)
                dve.tensor_copy(h["u"][:, 4 * g:4 * g + 4, :], yp[g][:, :].rearrange("p (n i) -> p n i", n=4))

        @block.scalar
        def _(act):
            for g in range(2):
                act.wait_ge(s["solved"], g + 1)
                act.activation(h["w"][:, 4 * g:4 * g + 4, :], dp[g][:, :].rearrange("p (n i) -> p n i", n=4), ACT.Copy)


def delta_scan_phase(nc, K, prm, hf, h, z, o_dn, units, x, ring, layer):
    with phase(nc, "zeroed ws vnew out state kept squared plus_eps rooted normed turned dve_step" + Fill.names,
               [("st", [P, 4, P]), ("vn", [P, 4, P]), ("sq", [P, NP, P]), ("ms", [P, NP])],
               [("w_ps", HALF), ("o_ps", HALF), ("k_ps", HALF), ("t0", HALF), ("t1", HALF)] + Fill.banks) as (block, s, b):
        fill = Fill(ring, units, x, s, b)
        tp = [b["t0"], b["t1"]]
        o = h["u"]

        @block.sync
        def _(sp):
            ring.send(sp, layer)

        @block.tensor
        def _(pe):
            for c in range(NCH):
                tt, r = c // 2, slice((c % 2) * CH, (c % 2 + 1) * CH)
                pe.wait_ge(s["state"], 4 * c + 1)
                for hh in range(4):
                    mm = pe.matmul(b["w_ps"][r, hh * P:(hh + 1) * P], h["w"][:, tt * 4 + hh, r], b["st"][:, hh, :],
                                   start=True, stop=True)
                mm.then_inc(s["ws"], 1)
                fill.pe(pe, 1)
                pe.wait_ge(s["vnew"], c + 1)
                if c:
                    pe.wait_ge(s["kept"], c)
                for hh in range(4):
                    n = tt * 4 + hh
                    mm = pe.matmul(b["k_ps"][:, hh * P:(hh + 1) * P], h["kd"][r, n, :], b["vn"][r, hh, :], start=True, stop=True)
                mm.then_inc(s["out"], 1)
                for hh in range(4):
                    n = tt * 4 + hh
                    cols = slice(hh * P, (hh + 1) * P)
                    pe.matmul(b["o_ps"][r, cols], h["qd"][:, hh, c * CH:(c + 1) * CH], b["st"][:, hh, :], start=True, stop=False)
                    mm = pe.matmul(b["o_ps"][r, cols], h["at"][r, n, r], b["vn"][r, hh, :], start=False, stop=True)
                mm.then_inc(s["out"], 1)
                fill.pe(pe, 1)
            fill.pe(pe)
            for tt in range(TT):
                pe.wait_ge(s["normed"], 1)
                for hh in range(4):
                    mm = pe.transpose(tp[tt][:, hh * P:(hh + 1) * P], b["sq"][:, tt * 4 + hh, :], K("ident"))
                mm.then_inc(s["turned"], 1)

        @block.vector
        def _(dve):
            chain = Chain(dve, s["dve_step"])
            dve.memset(b["st"][:, :, :], 0.0).then_inc(s["state"], 1)
            for c in range(NCH):
                tt, r = c // 2, slice((c % 2) * CH, (c % 2 + 1) * CH)
                dve.wait_ge(s["ws"], c + 1)
                dve.tensor_tensor(b["vn"][r, :, :], h["u"][r, tt * 4:tt * 4 + 4, :],
                                  b["w_ps"][r, :].rearrange("p (h d) -> p h d", h=4), ALU.subtract).then_inc(s["vnew"], 1)
                if c + 1 < NCH:
                    dve.wait_ge(s["out"], 2 * c + 2)
                    dve.wait_ge(s["state"], 4 * c + 1)
                    for hh in range(4):
                        at = (c + 1) * CH - 1
                        dve.scalar_tensor_tensor(b["st"][:, hh, :], b["st"][:, hh, :], h["ge"][:, hh, at:at + 1],
                                                 b["k_ps"][:, hh * P:(hh + 1) * P], ALU.mult, ALU.add).then_inc(s["state"], 1)
            dve.wait_ge(s["squared"], 1)
            chain.step(dve.tensor_reduce(b["ms"][:, :], b["sq"][:, :, :], AX_X, ALU.add))
            dve.tensor_scalar(b["ms"][:, :], b["ms"][:, :], 1.0 / P, NORM_EPS, ALU.mult, ALU.add).then_inc(s["plus_eps"], 1)
            dve.wait_ge(s["rooted"], 1)
            chain.step(dve.reciprocal(b["ms"][:, :], b["ms"][:, :]))
            dve.tensor_tensor(b["sq"][:, :, :], o[:, :, :], b["ms"][:, :].unsqueeze(2).to_broadcast([P, NP, P]),
                              ALU.mult).then_inc(s["normed"], 1)
            for tt in range(TT):
                dve.wait_ge(s["turned"], tt + 1)
                c = slice(tt * P, (tt + 1) * P)
                dve.scalar_tensor_tensor(o_dn[:, 4 * hf:4 * hf + 4, c], tp[tt][:, :].rearrange("p (h t) -> p h t", h=4),
                                         prm("dn_norm"), z[:, 4 * hf:4 * hf + 4, c], ALU.mult, ALU.mult)

        @block.gpsimd
        def _(pool):
            fill.pool(pool)

        @block.scalar
        def _(act):
            fill.act(act, 1)
            for c in range(NCH):
                tt, r = c // 2, slice((c % 2) * CH, (c % 2 + 1) * CH)
                act.wait_ge(s["out"], 2 * c + 2)
                act.activation(o[r, tt * 4:tt * 4 + 4, :], b["o_ps"][r, :].rearrange("p (h d) -> p h d", h=4),
                               ACT.Copy).then_inc(s["kept"], 1)
                if c == 1:
                    fill.act(act, 1)
            act.wait_ge(s["kept"], NCH)
            act.activation(b["sq"][:, :, :], o[:, :, :], ACT.Square).then_inc(s["squared"], 1)
            fill.act(act)
            act.wait_ge(s["plus_eps"], 1)
            act.activation(b["ms"][:, :], b["ms"][:, :], ACT.Sqrt).then_inc(s["rooted"], 1)
            fill.act(act, last=True)


def index_phase(nc, K, iq, ik, tokq, masks, units, x, ring, layer):
    with phase(nc, "scored0 scored1 relued summed masked max8 dve_step" + Fill.names,
               [("r", [P, 2, 8, T]), ("sc", [P, T]), ("wk", [P, T]), ("m8", [P, 8])],
               [("a0", HALF), ("b0", HALF), ("a1", 2 * HALF), ("b1", 2 * HALF)] + Fill.banks) as (block, s, b):
        fill = Fill(ring, units, x, s, b)
        ps = [[b["a0"], b["b0"]], [b["a1"], b["b1"]]]
        scored = [s["scored0"], s["scored1"]]

        @block.sync
        def _(sp):
            ring.send(sp, layer)

        @block.tensor
        def _(pe):
            for qt in range(TT):
                nk = (qt + 1) * P
                for h in range(8):
                    r = slice((h % 2) * 64, (h % 2 + 1) * 64)
                    mm = pe.matmul(ps[qt][h % 2][:, (h // 2) * nk:(h // 2 + 1) * nk], iq[r, h // 2, qt * P:(qt + 1) * P],
                                   ik[r, 0:nk], start=True, stop=True)
                mm.then_inc(scored[qt], 1)
                fill.pe(pe, Fill.PARTS)
            fill.pe(pe)

        @block.gpsimd
        def _(pool):
            fill.pool(pool)

        @block.scalar
        def _(act):
            for qt in range(TT):
                nk = (qt + 1) * P
                fill.act(act, 1)
                act.wait_ge(scored[qt], 1)
                for half in range(2):
                    act.activation(b["r"][:, qt, 4 * half:4 * half + 4, 0:nk],
                                   ps[qt][half][:, :].rearrange("p (h k) -> p h k", h=4),
                                   ACT.Relu).then_inc(s["relued"], 1)
            fill.act(act, last=True)

        @block.vector
        def _(dve):
            chain = Chain(dve, s["dve_step"])
            for qt in range(TT):
                nk = (qt + 1) * P
                sc, wk = b["sc"][:, 0:nk], b["wk"][:, 0:nk]
                dve.wait_ge(s["relued"], 2 * qt + 2)
                mask = K("chunk_causal").rearrange("p (q k) -> p q k", q=2)[:, qt, 0:nk]
                for h in range(8):
                    at = (h % 2) * 4 + h // 2
                    chain.step(dve.scalar_tensor_tensor(sc, b["r"][:, qt, at, 0:nk], tokq[:, qt, 4, h:h + 1],
                                                        mask if h == 0 else sc, ALU.mult, ALU.add))
                for i in range(TOPK // 8):
                    src = sc if i == 0 else wk
                    chain.step(dve.max(b["m8"][:, :], src))
                    chain.step(dve.match_replace(wk, b["m8"][:, :], src, TAKEN))
                chain.step(dve.tensor_scalar(wk, wk, TAKEN / 2, 1.0, ALU.is_le, ALU.subtract))
                dve.tensor_scalar(masks[:, qt, 0:nk], wk, -NEG, None, ALU.mult)


def second_layer(nc, K, layer, x, hs, mem_dram, ring, par_dram, tables):
    with ExitStack() as ctx:
        def sb(stack, name, shape):
            return stack.enter_context(nc.sbuf_tensor(name, shape, F32))

        par = sb(ctx, "par2_sb", [P, NPC2])
        prm = lambda name: par[:, PC2[name]]
        o_dn, sq, xq = (sb(ctx, n, [P, KD, T])[:, :, :] for n in ("o_dn", "sq_", "xq"))
        mem = xq
        o_sa, o_xa = sq, xq
        tokq = sb(ctx, "tokq", [P, TT, QTY, 8])[:, :, :, :]
        ik = sb(ctx, "ik", [P, T])[:, :]
        copy = (ACT.Copy, None)
        rms_phase(nc, K, x, prm("norm_mix"), hs, ring, layer, params=(
            par[:, :], par_dram[bass.ds(layer, 1), :, :].rearrange("o p n -> (o p) n")))

        with ExitStack() as st:
            q, k, v, z = (sb(st, n, [P, KD, T])[:, :, :] for n in ("dq", "dk", "dv", "dz"))
            small, rowq, ge = sb(st, "small", [8, 3, T]), sb(st, "rowq", [8, QTY, T])[:, :, :], sb(st, "ge_row", [8, T])[:, :]
            taps = prm("conv_w").rearrange("p (j c) -> p j c", j=4)
            units = [U("small", "rows", ik, [(32 * n, 8, small[:, n, :]) for n in range(3)])]
            for n in range(12):
                dst = (q, k, v)[n // 4][:, 2 * (n % 4):2 * (n % 4) + 2, :]
                units.append(U(f"dn{n}", "conv", dst, (4, taps, None, 2 * n, "silu")))
            product_phase(nc, ring, layer, units, hs, loads=[(mem, mem_dram)])
            others = [U(f"dn{12 + n}", "act", z[:, 2 * n:2 * n + 2, :], copy) for n in range(4)]
            others += [U(f"sa{n}", "act", sq[:, 2 * n:2 * n + 2, :], copy) for n in range(4)]
            decay_phase(nc, K, prm, small, ge, rowq, tokq, others[:1], hs, ring, layer)
            unit_keys_phase(nc, K, q, k, others[1:2], hs, ring, layer)
            for hf in range(2):
                with ExitStack() as half:
                    h = {}
                    for n in ("kb", "kd", "vb", "at", "mt", "ti"):
                        h[n] = sb(half, f"{n}_{hf}", [P, NP, P])[:, :, :]
                    h["u"], h["w"] = h["vb"], h["kb"]
                    h["qd"], h["ge"] = (sb(half, f"{n}_{hf}", [P, 4, T])[:, :, :] for n in ("qd", "ge"))
                    delta_prepare_phase(nc, K, hf, q, k, v, z, ge, rowq, tokq, h, ring, layer)
                    delta_solve_phase(nc, K, h, ring, layer)
                    delta_scan_phase(nc, K, prm, hf, h, z, o_dn, others[5:] if hf else others[2:5], hs, ring, layer)


        memory = ctx.enter_context(ExitStack())
        mk, mv = sb(memory, "mk", [P, KD, T])[:, :, :], sb(memory, "mv_", [P, TT, D])[:, :, :]
        mn = pair_of(nc, memory, "mem_split", KD)
        sk = sb(memory, "sk_", [P, KD, T])[:, :, :]
        rms_phase(nc, K, mem, prm("norm_mem"), mn, ring, layer)

        with ExitStack() as st:
            sv, iq = sb(st, "sv_", [P, TT, D])[:, :, :], sb(st, "iq_", [P, 4, T])[:, :, :]
            masks = sb(st, "masks", [P, TT, T])[:, :, :]
            units = [U(f"sa{4 + n}", "act", sk[:, 2 * n:2 * n + 2, :], copy) for n in range(4)]
            units += [U(f"sa{8 + n}", "act", sv[:, :, n * 256:(n + 1) * 256], copy, tokens=True) for n in range(4)]
            units += [U(f"iq{n}", "act", iq[:, 2 * n:2 * n + 2, :], copy) for n in range(2)]
            others = [U(f"xq{n}", "act", xq[:, 2 * n:2 * n + 2, :], copy) for n in range(4)]
            others += [U(f"kv{n}", "act", mk[:, 2 * n:2 * n + 2, :], copy, x=mn) for n in range(4)]
            others += [U(f"kv{4 + n}", "act", mv[:, :, n * 256:(n + 1) * 256], copy, x=mn, tokens=True) for n in range(4)]
            product_phase(nc, ring, layer, units + others[:1], hs)
            cs128, sn128 = tables[:, 0, :], tables[:, 2, :]
            cs64, sn64 = tables[:, 1, :], tables[:, 3, :]
            rope_phase(nc, K, [(t[:, 2 * i:2 * i + 2, :], K("perm128"), cs128, sn128) for t in (sq, sk) for i in range(4)]
                       + [(iq[:, 2 * i:2 * i + 2, :], K("perm64"), cs64, sn64) for i in range(2)]
                       + [(ik.unsqueeze(1), K("perm64"), cs64, sn64)], ring, layer, others[1:4], hs)
            index_phase(nc, K, iq, ik, tokq, masks, others[4:8], hs, ring, layer)

            def group(h0, qt):
                nk, c = (qt + 1) * P, slice(qt * P, (qt + 1) * P)
                return Group(
                    nk=nk, scale=128 ** -0.5, slot=lambda h: h, mask=masks[:, qt:qt + 1, 0:nk],
                    pairs=lambda h: [(sq[:, h0 + h, c], sk[:, h0 + h, 0:nk])],
                    value=lambda h, kt: [sv[:, kt, (h0 + h) * P:(h0 + h + 1) * P]],
                    place=lambda o, h: [o[:, h * P:(h + 1) * P]],
                    dst=lambda o: [(o[:, 0:HALF].rearrange("p (i q) -> p i q", i=4), o_sa[:, h0:h0 + 4, c])])

            attention_phase(nc, K, [group(h0, qt) for h0 in (0, 4) for qt in range(TT)], ring, layer,
                            others[8:], hs)

        with ExitStack() as st:
            def group(qt):
                c = slice(qt * P, (qt + 1) * P)
                return Group(
                    nk=T, scale=256 ** -0.5, slot=lambda h: h, mask=None,
                    pairs=lambda h: [(xq[:, 2 * h + i, c], mk[:, 2 * h + i, :]) for i in range(2)],
                    value=lambda h, kt: [mv[:, kt, (2 * h + i) * P:(2 * h + i + 1) * P] for i in range(2)],
                    place=lambda o, h: [o[:, (2 * h + i) * P:(2 * h + i + 1) * P] for i in range(2)],
                    dst=lambda o: [(o[:, :].rearrange("p (i q) -> p i q", i=8), o_xa[:, :, c])])

            attention_phase(nc, K, [group(qt) for qt in range(TT)], ring, layer)

        memory.close()

        merged = sb(ctx, "merged", [P, KD, T])[:, :, :]
        with ExitStack() as st:
            gates = sb(st, "gates", [P, 2, 3, 4, T])
            split = [pair_of(nc, st, f"o{i}_split", KD) for i in range(3)]
            units = []
            bg = prm("b_gate")
            for c in range(2):
                pair = [merged[:, 4 * c + 2 * u:4 * c + 2 * u + 2, :] for u in range(2)]
                for i in range(3):
                    g = [gates[:, c, i, 2 * u:2 * u + 2, :] for u in range(2)]
                    at = 8 * i + 4 * c
                    units += [U(f"gl{i}_{2 * c + u}", "act", g[u],
                                (ACT.Sigmoid, bg[:, at + 2 * u:at + 2 * u + 2])) for u in range(2)]
                    units += [U(f"wb{i}_{2 * c + u}", "gate_add" if i else "gate_first", pair[u], g[u], x=split[i])
                              for u in range(2)]
            product_phase(nc, ring, layer, units, hs, splits=list(zip((o_dn, o_sa, o_xa), split)))
        with ExitStack() as st:
            ms = pair_of(nc, st, "merged_split", KD)
            product_phase(nc, ring, layer, [U(f"out{i}", "residual", x[:, 2 * i:2 * i + 2, :], 1.0) for i in range(4)], ms,
                          splits=[(merged, ms)])

        rms_phase(nc, K, x, prm("norm_ffn"), hs, ring, layer)
        with ExitStack() as st:
            hid = st.enter_context(nc.sbuf_tensor("hid2", [P, KF, T], F32))
            fs = pair_of(nc, st, "hid2_split", KF)
            hv = [hid[:, 2 * i:2 * i + 2, :] for i in range(KF // 2)]
            hp = [[v[:, 2 * i:2 * i + 2, :] for v in fs] for i in range(KF // 2)]
            product_phase(nc, ring, layer,
                          [U(f"fin{i}", "act" if i < 11 else "times", hv[i % 11], (ACT.Silu, None),
                             pair=hp[i % 11] if i >= 11 else None) for i in range(KF)], hs)
            down_phase(nc, ring, layer, [f"fout{i}" for i in range(11)], fs, x, 1.0)
        ring.clear(nc)


def build(nc, a, out_dram):
    with ExitStack() as ctx:
        const = ctx.enter_context(nc.sbuf_tensor("const_sb", [P, NCC2], F32))
        x = ctx.enter_context(nc.sbuf_tensor("x_sb", [P, KD, T], F32))[:, :, :]
        xs = pair_of(nc, ctx, "x_split", KD)
        loads = [(const[:, :], a["const"][:, 0:NCC2])]
        if "w1" not in a:
            begin_phase(nc, x, xs, a["xT"], loads)
        if "w1" in a:
            with ExitStack() as first:
                more = first.enter_context(nc.sbuf_tensor("const1_sb", [P, NCC - NCC2], F32))
                ring = Ring(nc, first, "w1", CHUNKS_1, a["w1"], a["head1"])

                def K(name):
                    c = CC[name]
                    return const[:, c] if c.stop <= NCC2 else more[:, c.start - NCC2:c.stop - NCC2]

                begin_phase(nc, x, xs, a["xT"], loads + [(more[:, :], a["const"][:, NCC2:NCC])], ring)
                ring.resume()
                with nc.Fori(0, DEPTH) as layer:
                    first_layer(nc, K, layer, x, xs, ring, a["par1"], a["rows1"])
                ring.settle(nc)
        K = lambda name: const[:, CC[name]]
        if "w2" not in a:
            with phase(nc, "stored") as (block, s, b):
                @block.sync
                def _(sp):
                    sp.dma_start(out_dram, x).then_inc(s["stored"], 16)
                    sp.wait_ge(s["stored"], 16)
            return
        with ExitStack() as second:
            ring = Ring(nc, second, "w2", CHUNKS_2, a["w2"])
            tables = second.enter_context(nc.sbuf_tensor("tables", [P, 4, T], F32))[:, :, :]
            angle_phase(nc, K, a["positions"], tables)
            with nc.Fori(0, DEPTH) as layer:
                second_layer(nc, K, layer, x, xs, a["memT"], ring, a["par2"], tables)
        gain = ctx.enter_context(nc.sbuf_tensor("final_gain", [P, D], F32))
        with phase(nc, "gain") as (block, s, b):
            @block.sync
            def _(sp):
                sp.dma_start(gain[:, :], a["norm_final"].to_broadcast([P, D])).then_inc(s["gain"], 16)
                sp.wait_ge(s["gain"], 16)
        norm_phase(nc, K, x, None, gain[:, :], None, NORM_EPS, True, out=out_dram)


def lay_second(i):
    w = i["w_in_2"]
    at = dict(zip("dq dk dv dz db da sq sk sv iq ik iw xq gl".split(),
                  np.cumsum([0, D, D, D, D, 8, 8, D, D, D, 512, 64, 8, D]).tolist()))
    wb = i["w_branch_2"].reshape(DEPTH, 3 * D, D)
    small = np.zeros((DEPTH, D, 256), np.float32)
    for n, name in enumerate(("db", "da", "iw")):
        small[:, :, 32 * n:32 * n + 8] = w[:, :, at[name]:at[name] + 8]
    for n in range(2):
        small[:, :, P + 64 * n:P + 64 * (n + 1)] = w[:, :, at["ik"]:at["ik"] + 64]
    parts = ([(small, 0, 0)] + [(w, 0, 256 * n) for n in range(16)] + [(w, 0, at["sq"] + 256 * n) for n in range(12)]
             + [(w, 0, at["iq"] + 256 * n) for n in range(2)] + [(w, 0, at["xq"] + 256 * n) for n in range(4)]
             + [(i["w_mem_kv_2"], 0, 256 * n) for n in range(8)]
             + [p for c in range(2) for b in range(3) for p in
                [(w, 0, at["gl"] + D * b + 512 * c + 256 * u) for u in range(2)]
                + [(wb, D * b, 512 * c + 256 * u) for u in range(2)]]
             + [(i["w_out_2"], 0, 256 * n) for n in range(4)] + [(i["w_ffn_in_2"], 0, 256 * n) for n in range(22)]
             + [(i["w_ffn_out_2"], 256 * n, 0) for n in range(11)])
    par = np.zeros((DEPTH, P, NPC2), np.float32)
    for name in ("norm_mix", "norm_mem", "norm_ffn", "b_gate", "conv_w", "dn_norm"):
        par[:, :, PC2[name]] = i[name + "_2"].reshape(DEPTH, -1, P).transpose(0, 2, 1)
    for name in ("a_log", "dt_bias"):
        par[:, 0:8, PC2[name]] = i[name + "_2"][:, :, None]
    return chunked(parts, CHUNKS_2), par


def kernel(**inputs):
    import concourse.bacc as bacc
    from concourse.bass_utils import run_bass_kernel_spmd as run

    i = {name: np.asarray(v) for name, v in inputs.items()}
    w1, par1, rows1 = lay_first(i)
    head1, w1 = head_and_rest(w1, CHUNKS_1)
    w2, par2 = lay_second(i)
    arrays = {"xT": tiles_of(i["x"][0]), "head1": head1, "w1": w1, "par1": par1, "rows1": rows1, "w2": w2, "par2": par2,
              "memT": tiles_of(i["mem_2"][0]), "positions": i["positions_2"],
              "norm_final": i["norm_final_2"].reshape(1, D), "const": constants()}
    nc = bacc.Bacc("TRN2", target_bir_lowering=False, num_devices=1)
    dram = {n: nc.dram_tensor(n, v.shape, mybir.dt.from_np(v.dtype), kind="ExternalInput").ap() for n, v in arrays.items()}
    out = nc.dram_tensor("out", (T, D), F32, kind="ExternalOutput").ap()
    build(nc, dram, out)
    r = run(nc, [arrays], core_ids=[0])
    return r.results[0]["out"].reshape(1, T, D)
```
